# Optimizing a Trainium2 kernel written in Bass

```python
import jax
import jax.numpy as jnp
from jax import lax
import numpy as np

D_MODEL = 1024
BATCH = 1
SEQ = 512
DEPTH = 2
DEC_BATCH = 8
DEC_SEQ = 8
PAST_LEN = 2048
PAGE_SIZE = 128

HEAD_DIM = 64
MIX_WIDTH = 3 * D_MODEL // 4
MEM_WIDTH = D_MODEL - MIX_WIDTH
MEM_HEADS = MEM_WIDTH // HEAD_DIM
N_MEM = 256
N_HEADS = MIX_WIDTH // HEAD_DIM
KV_HEADS = 4
GROUP = N_HEADS // KV_HEADS
KV_WIDTH = KV_HEADS * HEAD_DIM
CONV_WIDTH = 3
CMP_BLOCK = 32
CMP_STRIDE = 16
SEL_BLOCK = 64
N_SEL = 16
WINDOW = 512
ROT_DIM = HEAD_DIM // 4
ROPE_THETA = 500000.0
NORM_EPS = 1e-6
FORCE_BONUS = 1e4
Q_BLOCK = 64
N_CONV_LAYERS = (DEPTH + 1) // 2
N_NSA_LAYERS = DEPTH // 2
CONV_SPLITS = (MEM_WIDTH, MEM_WIDTH, MIX_WIDTH, MIX_WIDTH, MIX_WIDTH, MIX_WIDTH)
NSA_SPLITS = (MEM_WIDTH, MEM_WIDTH, MIX_WIDTH) + (KV_WIDTH,) * 6 + (3 * N_HEADS, MIX_WIDTH)
CONV_IN = sum(CONV_SPLITS)
NSA_IN = sum(NSA_SPLITS)

kernel_name = 'hybrid_shortconv_nsa_memory_decoder_step'

def rmsnorm(x, g):
    x32 = x.astype(jnp.float32)
    y = x32 * lax.rsqrt(jnp.mean(x32 * x32, axis=-1, keepdims=True) + NORM_EPS)
    return (y * g.astype(jnp.float32)).astype(x.dtype)

def split_cols(p, sizes):
    return jnp.split(p, [int(v) for v in np.cumsum(sizes)[:-1]], axis=-1)

def rope_partial(x, pos):
    half = ROT_DIM // 2
    inv = ROPE_THETA ** (-jnp.arange(half, dtype=jnp.float32) * 2.0 / ROT_DIM)
    ang = pos.astype(jnp.float32)[:, None] * inv[None, :]
    shape = (ang.shape[0],) + (1,) * (x.ndim - 3) + (half,)
    cos = jnp.cos(ang).reshape(shape).astype(x.dtype)
    sin = jnp.sin(ang).reshape(shape).astype(x.dtype)
    x1 = x[..., :half]
    x2 = x[..., half:ROT_DIM]
    return jnp.concatenate([x1 * cos - x2 * sin, x2 * cos + x1 * sin, x[..., ROT_DIM:]], axis=-1)

def masked_softmax(s, mask):
    s = jnp.where(mask, s.astype(jnp.float32), -1e30)
    m = jnp.max(s, axis=-1, keepdims=True)
    p = jnp.exp(s - m) * mask
    return p / jnp.maximum(jnp.sum(p, axis=-1, keepdims=True), 1e-30)

def memory_kv(mem, g, w):
    B = mem.shape[0]
    return (rmsnorm(mem, g) @ w).reshape(B, N_MEM, 2, MEM_HEADS, HEAD_DIM)

def mem_attend(q, kv):
    B, T = q.shape[:2]
    qh = q.reshape(B, T, MEM_HEADS, HEAD_DIM)
    s = jnp.einsum('bthd,bmhd->bhtm', qh, kv[:, :, 0]) * (HEAD_DIM ** -0.5)
    p = jax.nn.softmax(s.astype(jnp.float32), axis=-1).astype(q.dtype)
    return jnp.einsum('bhtm,bmhd->bthd', p, kv[:, :, 1]).reshape(B, T, MEM_WIDTH)

def short_conv(b_g, c_g, h_in, conv_w, u_prev):
    u = c_g * h_in
    T = u.shape[1]
    u_ext = jnp.concatenate([u_prev.astype(u.dtype), u], axis=1)
    y = conv_w[0] * u_ext[:, 0:T]
    for j in range(1, CONV_WIDTH):
        y = y + conv_w[j] * u_ext[:, j:j + T]
    return b_g * y, u_ext[:, -(CONV_WIDTH - 1):]

def nsa_project(q, kc, vc, ks, vs, kw, vw, glog, pos):
    B, T = q.shape[:2]
    q = rope_partial(q.reshape(B, T, KV_HEADS, GROUP, HEAD_DIM), pos)
    heads = lambda a: a.reshape(B, T, KV_HEADS, HEAD_DIM)
    kvc = jnp.stack([rope_partial(heads(kc), pos), heads(vc)], axis=2)
    kvs = jnp.stack([rope_partial(heads(ks), pos), heads(vs)], axis=2)
    kvw = jnp.stack([rope_partial(heads(kw), pos), heads(vw)], axis=2)
    gates = jax.nn.sigmoid(glog.astype(jnp.float32)).astype(q.dtype).reshape(B, T, 3, KV_HEADS, GROUP)
    return q, kvc, kvs, kvw, gates

def chunk_partials(kv, pos_w):
    B, L = kv.shape[:2]
    nck = L // CMP_STRIDE
    ratio = CMP_BLOCK // CMP_STRIDE
    chunks = kv[:, :nck * CMP_STRIDE].reshape(B, nck, CMP_STRIDE, 2, KV_HEADS, HEAD_DIM)
    pw = pos_w.reshape(2, ratio, CMP_STRIDE, HEAD_DIM)
    return jnp.einsum('bcjsgd,smjd->mbcsgd', chunks, pw)

def blocks_from_partials(parts, phi):
    ratio, nck = parts.shape[0], parts.shape[2]
    nc = nck - ratio + 1
    blk = parts[0, :, 0:nc]
    for m in range(1, ratio):
        blk = blk + parts[m, :, m:m + nc]
    blk = jnp.einsum('bnsgd,sde->bnsge', blk, phi)
    return blk[:, :, 0], blk[:, :, 1]

def nsa_core(q, q_pos, kc_blk, vc_blk, gather_sel, n_sel_blocks, kvw, kw_pos):
    scale = HEAD_DIM ** -0.5
    dt = q.dtype
    nc = kc_blk.shape[1]
    s_c = jnp.einsum('bqgrd,bngd->bgrqn', q, kc_blk) * scale
    blk_end = jnp.arange(nc, dtype=jnp.int32) * CMP_STRIDE + (CMP_BLOCK - 1)
    p_c = masked_softmax(s_c, blk_end[None, :] <= q_pos[:, None])
    o_c = jnp.einsum('bgrqn,bngd->bqgrd', p_c.astype(dt), vc_blk)
    imp = p_c.sum(axis=2)
    ratio = CMP_BLOCK // CMP_STRIDE
    chunk = jnp.pad(imp, ((0, 0), (0, 0), (0, 0), (0, ratio - 1)))
    for m in range(1, ratio):
        chunk = chunk + jnp.pad(imp, ((0, 0), (0, 0), (0, 0), (m, ratio - 1 - m)))
    cps = SEL_BLOCK // CMP_STRIDE
    chunk = jnp.pad(chunk, ((0, 0), (0, 0), (0, 0), (0, n_sel_blocks * cps - chunk.shape[-1])))
    imp_s = chunk.reshape(chunk.shape[:3] + (n_sel_blocks, cps)).sum(-1)
    cur = q_pos // SEL_BLOCK
    j = jnp.arange(n_sel_blocks, dtype=jnp.int32)
    forced = (j[None, :] == 0) | (j[None, :] == cur[:, None]) | (j[None, :] == cur[:, None] - 1)
    score = jnp.where(j[None, :] <= cur[:, None], imp_s + jnp.where(forced, FORCE_BONUS, 0.0), -jnp.inf)
    _, idx = lax.top_k(score, min(N_SEL, n_sel_blocks))
    valid = idx <= cur[:, None]
    kv_g = gather_sel(idx)
    key_pos = idx[..., None] * SEL_BLOCK + jnp.arange(SEL_BLOCK, dtype=jnp.int32)
    mask_s = valid[..., None] & (key_pos <= q_pos[:, None, None])
    s_s = jnp.einsum('bqgrd,bgqnkd->bgrqnk', q, kv_g[..., 0, :]) * scale
    sh = s_s.shape
    p_s = masked_softmax(s_s.reshape(sh[:4] + (sh[4] * sh[5],)),
                         mask_s.reshape(sh[:2] + (1, sh[3], sh[4] * sh[5]))).reshape(sh)
    o_s = jnp.einsum('bgrqnk,bgqnkd->bqgrd', p_s.astype(dt), kv_g[..., 1, :])
    s_w = jnp.einsum('bqgrd,bkgd->bgrqk', q, kvw[:, :, 0]) * scale
    mask_w = (kw_pos[None, :] <= q_pos[:, None]) & (kw_pos[None, :] > q_pos[:, None] - WINDOW) & (kw_pos[None, :] >= 0)
    p_w = masked_softmax(s_w, mask_w)
    o_w = jnp.einsum('bgrqk,bkgd->bqgrd', p_w.astype(dt), kvw[:, :, 1])
    return o_c, o_s, o_w

def combine_nsa(gates, o_c, o_s, o_w):
    B, T = o_c.shape[:2]
    o = gates[:, :, 0, :, :, None] * o_c + gates[:, :, 1, :, :, None] * o_s + gates[:, :, 2, :, :, None] * o_w
    return o.reshape(B, T, MIX_WIDTH)

def nsa_prompt(parts, pos, cmp_pos_w, cmp_phi):
    q, kvc, kvs, kvw, gates = nsa_project(*parts, pos)
    B, T = q.shape[:2]
    kc_blk, vc_blk = blocks_from_partials(chunk_partials(kvc, cmp_pos_w), cmp_phi)
    n_sel_blocks = -(-T // SEL_BLOCK)
    sel_blocks = jnp.pad(kvs, ((0, 0), (0, n_sel_blocks * SEL_BLOCK - T), (0, 0), (0, 0), (0, 0))).reshape(
        B, n_sel_blocks, SEL_BLOCK, 2, KV_HEADS, HEAD_DIM)
    bi = jnp.arange(B)[:, None, None, None]
    gi = jnp.arange(KV_HEADS)[None, :, None, None]

    def gather_sel(idx):
        return sel_blocks[bi, idx, :, :, gi, :]

    kvw_pad = jnp.pad(kvw, ((0, 0), (WINDOW, 0), (0, 0), (0, 0), (0, 0)))
    n_qb = T // Q_BLOCK
    q_blocks = q.reshape(B, n_qb, Q_BLOCK, KV_HEADS, GROUP, HEAD_DIM).transpose(1, 0, 2, 3, 4, 5)
    starts = jnp.arange(n_qb, dtype=jnp.int32) * Q_BLOCK

    def step(args):
        qb, s = args
        q_pos = s + jnp.arange(Q_BLOCK, dtype=jnp.int32)
        kw = lax.dynamic_slice_in_dim(kvw_pad, s, WINDOW + Q_BLOCK, axis=1)
        kw_pos = s - WINDOW + jnp.arange(WINDOW + Q_BLOCK, dtype=jnp.int32)
        return nsa_core(qb, q_pos, kc_blk, vc_blk, gather_sel, n_sel_blocks, kw, kw_pos)

    o_c, o_s, o_w = lax.map(step, (q_blocks, starts))
    unblock = lambda o: o.transpose(1, 0, 2, 3, 4, 5).reshape(B, T, KV_HEADS, GROUP, HEAD_DIM)
    out = combine_nsa(gates, unblock(o_c), unblock(o_s), unblock(o_w))
    return out, kvc, kvs, kvw[:, -min(WINDOW, T):]

def nsa_sample(parts, pos, cmp_pos_w, cmp_phi, cache_cmp, cache_sel, page_table, win_state):
    q, kvc, kvs, kvw, gates = nsa_project(*parts, pos)
    Bd, T = q.shape[:2]
    past_c = cache_cmp[page_table].reshape(Bd, PAST_LEN, 2, KV_HEADS, HEAD_DIM)
    partials = jnp.concatenate([chunk_partials(past_c, cmp_pos_w), chunk_partials(kvc, cmp_pos_w)], axis=2)
    kc_blk, vc_blk = blocks_from_partials(partials, cmp_phi)
    total = PAST_LEN + T
    n_sel_blocks = -(-total // SEL_BLOCK)
    npb = PAST_LEN // SEL_BLOCK
    nnb = n_sel_blocks - npb
    bpp = PAGE_SIZE // SEL_BLOCK
    pool = cache_sel.reshape((-1, SEL_BLOCK, 2, KV_HEADS, HEAD_DIM))
    new_blocks = jnp.pad(kvs, ((0, 0), (0, nnb * SEL_BLOCK - T), (0, 0), (0, 0), (0, 0))).reshape(
        Bd, nnb, SEL_BLOCK, 2, KV_HEADS, HEAD_DIM)
    bi = jnp.arange(Bd)[:, None, None, None]
    gi = jnp.arange(KV_HEADS)[None, :, None, None]

    def gather_sel(idx):
        jp = jnp.minimum(idx, npb - 1)
        phys = page_table[bi, jp // bpp] * bpp + jp % bpp
        past = pool[phys, :, :, gi, :]
        jn = jnp.clip(idx - npb, 0, nnb - 1)
        new = new_blocks[bi, jn, :, :, gi, :]
        return jnp.where((idx < npb)[..., None, None, None], past, new)

    w_keep = win_state.shape[1]
    kw = jnp.concatenate([win_state.astype(kvw.dtype), kvw], axis=1)
    kw_pos = PAST_LEN - w_keep + jnp.arange(w_keep + T, dtype=jnp.int32)
    o_c, o_s, o_w = nsa_core(q, pos, kc_blk, vc_blk, gather_sel, n_sel_blocks, kw, kw_pos)
    return combine_nsa(gates, o_c, o_s, o_w), kvc, kvs, kw[:, -w_keep:]

def layer_update(x, mq, mg, mem_kv, mix, zg, w_out_i):
    y = jnp.concatenate([jax.nn.silu(mg) * mem_attend(mq, mem_kv), jax.nn.silu(zg) * mix], axis=-1)
    return x + y @ w_out_i

def forward_prompt(x, mem, norm_g, final_norm_g, mem_norm_g, w_mem_kv, w_in_conv, conv_w,
                   w_in_nsa, cmp_pos_w, cmp_phi, w_out):
    B, T, _ = x.shape
    pos = jnp.arange(T, dtype=jnp.int32)
    conv_st, cmp_rows, sel_rows, win_rows, mem_kvs = [], [], [], [], []
    for i in range(DEPTH):
        l = i // 2
        h = rmsnorm(x, norm_g[i])
        mem_kv = memory_kv(mem, mem_norm_g[i], w_mem_kv[i])
        mem_kvs.append(mem_kv)
        if i % 2 == 0:
            mq, mg, b_g, c_g, h_in, zg = split_cols(h @ w_in_conv[l], CONV_SPLITS)
            u_prev = jnp.zeros((B, CONV_WIDTH - 1, MIX_WIDTH), x.dtype)
            mix, st = short_conv(b_g, c_g, h_in, conv_w[l], u_prev)
            conv_st.append(st)
        else:
            parts = split_cols(h @ w_in_nsa[l], NSA_SPLITS)
            mq, mg, zg = parts[0], parts[1], parts[-1]
            mix, kvc, kvs, kvw = nsa_prompt(parts[2:-1], pos, cmp_pos_w[l], cmp_phi[l])
            cmp_rows.append(kvc)
            sel_rows.append(kvs)
            win_rows.append(kvw)
        x = layer_update(x, mq, mg, mem_kv, mix, zg, w_out[i])
    return (rmsnorm(x, final_norm_g), jnp.stack(conv_st), jnp.stack(cmp_rows), jnp.stack(sel_rows),
            jnp.stack(win_rows), jnp.stack(mem_kvs))

def forward_sample(x, cache_mem_kv, cache_cmp_kv, cache_sel_kv, page_table, state_conv, state_win_kv,
                   norm_g, final_norm_g, w_in_conv, conv_w, w_in_nsa, cmp_pos_w, cmp_phi, w_out):
    T = x.shape[1]
    pos = PAST_LEN + jnp.arange(T, dtype=jnp.int32)
    conv_st, cmp_rows, sel_rows, win_rows = [], [], [], []
    for i in range(DEPTH):
        l = i // 2
        h = rmsnorm(x, norm_g[i])
        mem_kv = cache_mem_kv[i]
        if i % 2 == 0:
            mq, mg, b_g, c_g, h_in, zg = split_cols(h @ w_in_conv[l], CONV_SPLITS)
            mix, st = short_conv(b_g, c_g, h_in, conv_w[l], state_conv[l])
            conv_st.append(st)
        else:
            parts = split_cols(h @ w_in_nsa[l], NSA_SPLITS)
            mq, mg, zg = parts[0], parts[1], parts[-1]
            mix, kvc, kvs, kvw = nsa_sample(parts[2:-1], pos, cmp_pos_w[l], cmp_phi[l], cache_cmp_kv[l],
                                            cache_sel_kv[l], page_table, state_win_kv[l])
            cmp_rows.append(kvc)
            sel_rows.append(kvs)
            win_rows.append(kvw)
        x = layer_update(x, mq, mg, mem_kv, mix, zg, w_out[i])
    return (rmsnorm(x, final_norm_g), jnp.stack(conv_st), jnp.stack(cmp_rows), jnp.stack(sel_rows),
            jnp.stack(win_rows))

def setup_inputs(seed: int = 0) -> dict:
    key = jax.random.key(seed)
    ks = jax.random.split(key, 24)
    f32 = jnp.float32
    n_pages = PAST_LEN // PAGE_SIZE
    n_used = DEC_BATCH * n_pages
    n_pool = n_used + max(1, n_used // 4)
    w_keep = min(WINDOW, PAST_LEN)

    def nrm(k, shape, s=1.0):
        return s * jax.random.normal(k, shape, f32)

    page_table = jax.random.permutation(ks[6], n_pool)[:n_used].reshape(DEC_BATCH, n_pages).astype(jnp.int32)
    return {
        'x_prompt': nrm(ks[0], (BATCH, SEQ, D_MODEL)),
        'x_sample': nrm(ks[1], (DEC_BATCH, DEC_SEQ, D_MODEL)),
        'mem_prompt': nrm(ks[2], (BATCH, N_MEM, D_MODEL)),
        'cache_mem_kv': nrm(ks[3], (DEPTH, DEC_BATCH, N_MEM, 2, MEM_HEADS, HEAD_DIM)),
        'cache_cmp_kv': nrm(ks[4], (N_NSA_LAYERS, n_pool, PAGE_SIZE, 2, KV_HEADS, HEAD_DIM)),
        'cache_sel_kv': nrm(ks[5], (N_NSA_LAYERS, n_pool, PAGE_SIZE, 2, KV_HEADS, HEAD_DIM)),
        'page_table': page_table,
        'state_conv': nrm(ks[7], (N_CONV_LAYERS, DEC_BATCH, CONV_WIDTH - 1, MIX_WIDTH)),
        'state_win_kv': nrm(ks[8], (N_NSA_LAYERS, DEC_BATCH, w_keep, 2, KV_HEADS, HEAD_DIM)),
        'norm_g': 1.0 + nrm(ks[9], (DEPTH, D_MODEL), 0.1),
        'final_norm_g': 1.0 + nrm(ks[10], (D_MODEL,), 0.1),
        'mem_norm_g': 1.0 + nrm(ks[11], (DEPTH, D_MODEL), 0.1),
        'w_mem_kv': nrm(ks[12], (DEPTH, D_MODEL, 2 * MEM_WIDTH), D_MODEL ** -0.5),
        'w_in_conv': nrm(ks[13], (N_CONV_LAYERS, D_MODEL, CONV_IN), D_MODEL ** -0.5),
        'conv_w': nrm(ks[14], (N_CONV_LAYERS, CONV_WIDTH, MIX_WIDTH), CONV_WIDTH ** -0.5),
        'w_in_nsa': nrm(ks[15], (N_NSA_LAYERS, D_MODEL, NSA_IN), D_MODEL ** -0.5),
        'cmp_pos_w': (CMP_BLOCK ** -0.5) * (1.0 + nrm(ks[16], (N_NSA_LAYERS, 2, CMP_BLOCK, HEAD_DIM), 0.2)),
        'cmp_phi': nrm(ks[17], (N_NSA_LAYERS, 2, HEAD_DIM, HEAD_DIM), HEAD_DIM ** -0.5),
        'w_out': nrm(ks[18], (DEPTH, D_MODEL, D_MODEL), D_MODEL ** -0.5),
    }

def reference(x_prompt, x_sample, mem_prompt, cache_mem_kv, cache_cmp_kv, cache_sel_kv, page_table,
              state_conv, state_win_kv, norm_g, final_norm_g, mem_norm_g, w_mem_kv, w_in_conv, conv_w,
              w_in_nsa, cmp_pos_w, cmp_phi, w_out):
    y_prompt, conv_p, cmp_p, sel_p, win_p, mem_p = forward_prompt(
        x_prompt, mem_prompt, norm_g, final_norm_g, mem_norm_g, w_mem_kv, w_in_conv, conv_w,
        w_in_nsa, cmp_pos_w, cmp_phi, w_out)
    y_sample, conv_s, cmp_s, sel_s, win_s = forward_sample(
        x_sample, cache_mem_kv, cache_cmp_kv, cache_sel_kv, page_table, state_conv, state_win_kv,
        norm_g, final_norm_g, w_in_conv, conv_w, w_in_nsa, cmp_pos_w, cmp_phi, w_out)
    return (y_prompt, y_sample, conv_p, cmp_p, sel_p, win_p, mem_p, conv_s, cmp_s, sel_s, win_s)


_drawn_inputs = setup_inputs


def setup_inputs(seed=0):
    import zlib

    import numpy as np

    out = dict(_drawn_inputs(seed))
    spreads = {}
    factors = {'cache_sel_kv': 4.319}
    for name, (base, spread) in spreads.items():
        noise = np.random.default_rng([zlib.crc32(name.encode()), seed]).standard_normal(out[name].shape)
        drawn = base * np.exp(spread * noise) if base else spread * noise
        out[name] = jnp.asarray(drawn.astype(out[name].dtype))
    for name, factor in factors.items():
        out[name] = (out[name] * factor).astype(out[name].dtype)
    return out
```

```python
from contextlib import ExitStack

import numpy as np
import concourse.bass as bass
from concourse import mybir

F32 = mybir.dt.float32
I32 = mybir.dt.int32
ALU = mybir.AluOpType
ACT = mybir.ActivationFunctionType
AX = mybir.AxisListType.X

D = 1024
KD = D // 128
SEQ = 512
NB, NT = 8, 8
NS = NB * NT
PT = SEQ // 128
TT = PT + 1
TOK = TT * 128
PAST = 2048
PAGE = 128
NPG = PAST // PAGE
POOL = 160
HD = 64
MIX = 768
CT = MIX // 128
NMEM = 256
KVH = 4
GRP = 3
SB = 64
NSB = PAST // SB + 1
NC = PAST // 16 - 1
NCP = SEQ // 16 - 1
WIN = 512
NEG = -1e30
SCALE = HD ** -0.5
ARENA = 53080


class START:
    cp_a = 8
    cp_b = 8
    cp_sum = 4
    conv_y = 2
    ms_s = 2
    u_made = 1
    pa_t = 4
    pa_o = 1
    sa_bt = 7
    c_copied = 1
    s_copied = 1
    b_used = 1
    z_used = 1
    ms_kc = 1
    ms_c = 1
    ms_done = 1
    cp_rows = 1
    cp_cols = 1
    cp_took = 1
    pa_p = 4
    pa_mix = 1
    pa_ta = 1
    pa_ts = 1
    sa_ba = 4
    sa_bd = 4
    sa_m = 1
    sa_p = 1
    sa_done = 1
    state_kept = 3
    ms_y = 2
    sa_y = 1
    pa_s = 1
    sa_used = 7
    sa_ft = 7
    sa_s = 2
    ms_o = 2


LINKS_OF_TURN = 28
EPS = 1e-6

CONST = {}
CONST_W = 0
for _n, _w in [("ident", 128), ("causal", 128), ("cmp_add", 128), ("cmp_mul", 128), ("same_gt", 128),
               ("new_add", 120), ("win_add", 8), ("chunk", 250), ("cos", 40), ("sin", 40),
               ("forced", NSB + 1)]:
    CONST[_n] = (CONST_W, _w)
    CONST_W += _w
SMALL = {}
SMALL_W = 0
for _n, _w in [("g_mem", 16), ("g_x", 16), ("conv_w", CT * 3), ("state", CT * 16), ("pos0", 512), ("pos1", 512),
               ("phi_k", 128), ("phi_v", 128)]:
    SMALL[_n] = (SMALL_W, _w)
    SMALL_W += _w

B_KV, B_C0, B_CONV, B_OUT0, B_N, B_OUT1 = 0, 2, 3, 9, 11, 18
NBLK = 20
TILES_OF = [2, 2, 5] + [4] * CT + [5, 5] + [5] * 7 + [5, 5]
PBASE = [sum(TILES_OF[:n]) + (5 if n >= B_OUT1 else 0) for n in range(NBLK + 1)]
P_GATES = sum(TILES_OF[:B_OUT1])


class Turn:

    def __init__(self, i, n, per):
        self.i, self.n, self.per = i, n, per

    def value(self, each, plus, base=0):
        rest = base + each * self.n + plus
        if isinstance(self.i, int):
            return self.i * self.per * each + rest
        assert rest > 0
        return self.i * (self.per * each) + rest

    def at(self, stride, plus=0):
        return self.i * (self.per * stride) + (self.n * stride + plus)


class Links:

    def __init__(self, eng, sem):
        self.eng, self.sem, self.n, self.i, self.per = eng, sem, 0, None, 0

    def did(self, ins):
        ins.then_inc(self.sem, 1)
        self.n += 1

    def settle(self):
        self.eng.wait_ge(self.sem, self.n if self.i is None else self.i * self.per + self.n)

    def link(self, ins):
        self.did(ins)
        self.settle()

    def enter(self, i, per):
        self.i, self.per, self.start = i, per, self.n

    def leave(self, trips):
        assert self.n - self.start == self.per, (self.n - self.start, self.per)
        self.i, self.n = None, self.start + trips * self.per


def build(nc, I, O):
    ctx = ExitStack()
    with ctx:
        def sem(name):
            return ctx.enter_context(nc.semaphore(name))

        arena = ctx.enter_context(nc.sbuf_tensor("arena", [128, ARENA], F32))
        ptab = ctx.enter_context(nc.sbuf_tensor("ptab", [1, NB * NPG], I32))
        PS = ctx.enter_context(nc.psum_tensor("PS", [128, 8, 512], F32))
        gates_dram = nc.dram_tensor("gates_scratch", [NS, 36], F32, kind="Internal").ap()

        top = [0]

        def keep(n):
            a = arena[:, top[0]:top[0] + n]
            top[0] += n
            return a

        X = keep(TT * D).rearrange("p (t c) -> p t c", t=TT)
        HT = keep(KD * TOK).rearrange("p (k c) -> p k c", k=KD)
        KC = keep(2 * NB * 128).rearrange("p (g b n) -> p g b n", g=2, b=NB)
        VC = keep(NB * 256).rearrange("p (b c) -> p b c", b=NB)
        KCp = keep(64).rearrange("p (g n) -> p g n", g=2)
        VCp = keep(256)
        cst = keep(CONST_W)
        small = keep(SMALL_W)
        stats = keep(400)
        Kn = keep(256).rearrange("p (s g n) -> p s g n", s=2, g=2)
        Vn = keep(512).rearrange("p (s c) -> p s c", s=2)
        Gate = keep(TT * 36).rearrange("p (t c) -> p t c", t=TT)
        Grow = keep(NB * 3).rearrange("p (b c) -> p b c", b=NB)
        CS = keep(CT * 18)
        QZ = keep(2 * NB * 128).rearrange("p (g b m) -> p g b m", g=2, b=NB)
        base = top[0]

        def at(off, n):
            assert base + off + n <= ARENA, (base, off, n)
            return arena[:, base + off:base + off + n]

        def C(name):
            a, w = CONST[name]
            return cst[:, a:a + w]

        def S(name):
            a, w = SMALL[name]
            return small[:, a:a + w]

        ident = C("ident")
        W = [at(4096 * n, 4096).rearrange("p (k c) -> p k c", k=KD) for n in range(2)]
        P1 = [at(8192 + 2560 * n, 2560).rearrange("p (t c) -> p t c", t=TT) for n in range(7)]
        P1all = at(8192, 7 * 2560)
        MKV = [at(26112 + 1024 * l, 1024).rearrange("p (m c) -> p m c", m=2) for l in range(2)]
        KTm = [at(28160 + 512 * l, 512).rearrange("p (g m) -> p g m", g=2) for l in range(2)]
        YT0 = at(8192, 5120).rearrange("p (k c) -> p k c", k=KD)
        YT0f = at(8192, 5120)
        MQG0 = at(13312, 2560).rearrange("p (t c) -> p t c", t=TT)
        memT = [at(15872 + 2048 * l, 2048).rearrange("p (k c) -> p k c", k=KD) for l in range(2)]
        M = at(19968, 2048).rearrange("p (t c) -> p t c", t=2)
        H = [at(22016 + 1024 * n, 1024) for n in range(2)]
        SQ = at(24064, 1024)
        Cb = at(15872, 576)
        U = [at(16448 + 600 * n, 600) for n in range(2)]
        Y = at(17648, 576)
        E = at(18224, 576)
        Sb = at(18800, 256)
        Wg = at(29184, 288).rearrange("p (k c) -> p k c", k=KD)
        MA = [15872, 0]
        QT = at(26112, 3072).rearrange("p (r g c) -> p r g c", r=3, g=2)
        QTf = at(26112, 3072)
        KTs = at(29184, 1024).rearrange("p (g c) -> p g c", g=2)
        KTw = at(30208, 1024).rearrange("p (g c) -> p g c", g=2)
        rope_t = [at(31008 + 320 * n, 320) for n in range(4)]
        sig = at(0, 3840)
        CPA = [at(19056 + 512 * n, 512) for n in range(4)]
        CPB = [at(21104 + 512 * n, 512) for n in range(4)]
        CR = at(23152, 512)
        CBL = at(23664, 512).rearrange("p (s c) -> p s c", s=4)
        PG = [at(29472 + 512 * n, 512) for n in range(5)] + [at(24176 + 512 * n, 512) for n in range(3)]
        PA = [at(31232 + 512 * n, 512) for n in range(2)]
        PB = [at(8192 + 512 * n, 512) for n in range(2)]
        CRp = at(9216, 512)
        BLp = at(9728, 512).rearrange("p (s c) -> p s c", s=4)
        Qs = [at(1024 * n, 1024).rearrange("p (g c) -> p g c", g=2) for n in range(1)]
        PP = [at(1024 + 1056 * n, 1056) for n in range(2)]
        PTt = at(3200, 1152)
        Om = at(4400, 256)
        MIXB = at(4700, 3072).rearrange("p (t c) -> p t c", t=PT)
        SV = [at(4096 * n, 4096).rearrange("p (s c) -> p s c", s=NPG) for n in range(2)]
        SK = [at(8192 + 2048 * n, 2048).rearrange("p (s c) -> p s c", s=8) for n in range(2)]
        SKT = at(12288, 4096).rearrange("p (g c) -> p g c", g=2)
        SM = at(16384, 2112)
        SWKT = at(18496, 1024).rearrange("p (g c) -> p g c", g=2)
        SIMP = at(19520, 130)
        SCH = at(19650, 128)
        SSC = at(19780, 40)
        SMB = at(19820, 40)
        SS2 = at(20460, 40)
        SM8 = at(19860, 8)
        SNM = at(19868, 64)
        SQB = [at(19940 + 256 * n, 256).rearrange("p (g m) -> p g m", g=2) for n in range(2)]
        SWI = [at(26112 + 2048 * n, 2048).rearrange("p (s c) -> p s c", s=4) for n in range(2)]
        SPT = [at(30208 + 512 * n, 512).rearrange("p (s c) -> p s c", s=4) for n in range(2)]
        SW = at(31232, 576)
        SPC = [at(31808 + 128 * n, 128) for n in range(2)]
        SO = at(32064, 256)
        gfin = at(0, 1024)
        fin = [at(1024 + 1024 * n, 1024) for n in range(2)]
        HTf = arena[:, TT * D:TT * D + KD * TOK]

        MIXf = at(4700, 3072)
        rs = lambda a, b: stats[:, a:b]

        const_in = sem("const_in")
        mem_in = sem("mem_in")
        x_in = sem("x_in")
        pad_zero = sem("pad_zero")
        x_zero = sem("x_zero")
        w_in = [sem(f"w_in{n}") for n in range(2)]
        wg_in = sem("wg_in")
        product = sem("product")
        squared = sem("squared")
        mean_sq = sem("mean_sq")
        root = sem("root")
        rstd = sem("rstd")
        scaled = sem("scaled")
        h_turned = sem("h_turned")
        h_taken = sem("h_taken")
        kv_taken = sem("kv_taken")
        kt_turned = sem("kt_turned")
        kt_taken = sem("kt_taken")
        kv_out = sem("kv_out")
        chunk_taken = sem("chunk_taken")
        gates_taken = sem("gates_taken")
        c_copied = sem("c_copied")
        z_exp = sem("z_exp")
        s_copied = sem("s_copied")
        u_made = sem("u_made")
        b_used = sem("b_used")
        z_used = sem("z_used")
        state_set = sem("state_set")
        state_kept = sem("state_kept")
        state_out = sem("state_out")
        conv_y = sem("conv_y")
        sig_exp = sem("sig_exp")
        sig_done = sem("sig_done")
        ma_q, ma_qt, ma_qc, ma_s, ma_m, ma_p, ma_t, ma_td, ma_ta, ma_o, ma_y, ma_yt, ma_done = [
            sem("ma_" + n) for n in ("q_scaled", "q_turned", "q_copied", "scored", "max", "probs", "p_turned",
                                     "p_took_dve", "p_took_act", "out", "y", "y_turned", "y_took")]
        ms_in = [sem(f"ms_in{n}") for n in range(2)]
        ms_q, ms_qt, ms_qz, ms_qb, ms_kt, ms_kc, ms_s, ms_m, ms_p, ms_t, ms_c, ms_o, ms_n, ms_y, ms_done, ms_g, ms_gm = [
            sem("ms_" + n) for n in ("q_scaled", "q_turned", "q_spread", "q_set", "k_turned", "k_copied", "scored",
                                     "max", "probs", "p_turned", "p_copied", "out", "normed", "y_turned", "y_took",
                                     "gate_turned", "gated")]
        out_added = sem("out_added")
        roped = sem("roped")
        r_turned = sem("r_turned")
        r_took = sem("r_took")
        kv_stored = sem("kv_stored")
        gates_back = sem("gates_back")
        gates_written = sem("gates_written")
        vn_copied = sem("vn_copied")
        qz_zero = sem("qz_zero")
        win_copied = sem("win_copied")
        cp_in = [sem(f"cp_in{n}") for n in range(8)]
        cp_a, cp_b, cp_sum, cp_rows, cp_turned, cp_cols, cp_phi, cp_took = [
            sem("cp_" + n) for n in ("prod0", "prod1", "summed", "rows", "turned", "cols", "phi", "took")]
        pa_q, pa_s, pa_m, pa_p, pa_cm, pa_t, pa_ts, pa_ta, pa_o, pa_mix = [
            sem("pa_" + n) for n in ("q_set", "scored", "max", "probs", "cmp_masked", "p_turned", "took_sel",
                                     "took_act", "out", "mixed")]
        sa_v = [sem(f"sa_v{n}") for n in range(2)]
        sa_k = [sem(f"sa_k{n}") for n in range(2)]
        (sa_qb, sa_cs, sa_cm, sa_ce, sa_cn, sa_imp, sa_mask, sa_ft, sa_fa, sa_fd, sa_s, sa_m, sa_p,
         sa_bt, sa_ba, sa_bd, sa_used, sa_mix, sa_y, sa_done) = [
            sem("sa_" + n) for n in ("q_set", "cmp_scored", "cmp_max", "cmp_exp", "cmp_normed", "imp",
                                     "mask", "k_turned", "k_took_act", "k_took_dve", "scored", "max", "probs",
                                     "p_turned", "p_took_act", "p_took_dve", "values_used", "mixed", "y_turned", "y_took")]
        sa_w = [sem(f"sa_w{n}") for n in range(2)]
        sa_new = sem("sa_new_read")
        sz_t = sem("sample_gate_turned")
        sz_done = sem("sample_gated")
        r_spread = sem("r_spread")
        ht_zero = sem("ht_zero")
        yg = sem("y_gated")
        yg_t = sem("y_gated_turned")
        yg_c = sem("y_gated_took")
        gfin_in = sem("gfin_in")
        fin_scaled = sem("fin_scaled")
        y_ready = sem("y_ready")
        y_out = [sem(f"y_out{n}") for n in range(2)]
        dve_links = sem("dve_links")
        act_links = sem("act_links")
        pool_links = sem("pool_links")

        block = ctx.enter_context(nc.Block())

        def step_dve():
            nc.vector.memset(rs(398, 399), 0.0)

        def mem_bufs(l):
            o = MA[l]
            return {
                "QZ": at(o, 2048).rearrange("p (g b m) -> p g b m", g=2, b=NB),
                "QB": [at(o + 2048 + 256 * n, 256).rearrange("p (g m) -> p g m", g=2) for n in range(2)],
                "KTb": [at(o + 2560 + 512 * n, 512) for n in range(2)],
                "SP": [at(o + 3584 + 256 * n, 256) for n in range(2)],
                "SPT": [at(o + 4096 + 256 * n, 256) for n in range(2)],
                "SO": [at(o + 4608 + 256 * n, 256) for n in range(2)],
                "MC": [at(o + 5632 + 1024 * n, 1024).rearrange("p (m c) -> p m c", m=2) for n in range(2)],
                "QS": at(o + 5120, 256),
                "QT": [at(30496 + 256 * n, 256) for n in range(2)],
                "P": [HTf[:, 2560 + 1024 * n:3584 + 1024 * n].rearrange("p (h m) -> p h m", h=4) for n in range(2)],
                "PT": at(29472, 1024),
                "OY": at(o + 5376, 256),
                "MG": HTf[:, 1280:2560].rearrange("p (t c) -> p t c", t=TT),
            }

        def sample_phase(eng, front, middle, back, lk=None):
            front(Turn(0, 0, 2), None)
            with eng.Fori(0, NB // 2 - 1) as i:
                if lk is not None:
                    lk.enter(i, 2 * LINKS_OF_TURN)
                for n in range(2):
                    t, nxt = Turn(i, n, 2), Turn(i, n + 1, 2)
                    middle(t)
                    front(nxt, t)
                    back(t, 2)
                if lk is not None:
                    lk.leave(NB // 2 - 1)
            t, nxt = Turn(NB // 2 - 1, 0, 2), Turn(NB // 2 - 1, 1, 2)
            middle(t)
            front(nxt, t)
            back(t, 2)
            middle(nxt)
            back(nxt, 1)

        @block.sync
        def _(sp):
            def load_w(n, i=None, blk=None):
                src = I["wall"][n] if blk is None else I["wall"][bass.ds(blk, 1)].rearrange("a p c -> (a p) c")
                sp.dma_start(W[n % 2].rearrange("p k c -> p (k c)"), src).then_inc(w_in[n % 2], 16)

            sp.dma_start(M, I["mem"].rearrange("(t p) c -> p t c", p=128)).then_inc(mem_in, 16)
            sp.dma_start(cst, I["const"]).then_inc(const_in, 16)
            sp.dma_start(small, I["small"]).then_inc(const_in, 16)
            sp.dma_start(ptab[:, :], I["pages"]).then_inc(const_in, 16)
            load_w(0)
            sp.dma_start(X[:, 0:PT, :], I["xp"].rearrange("(t p) c -> p t c", p=128)).then_inc(x_in, 16)
            sp.dma_start(X[0:NS, PT, :], I["xs"]).then_inc(x_in, 16)
            load_w(1)
            sp.wait_ge(product, PBASE[1])
            load_w(2)
            sp.wait_ge(product, PBASE[2])
            load_w(B_CONV)
            for l in range(2):
                sp.wait_ge(kv_taken, 2 * (l + 1))
                sp.dma_start(O["mem"][l].rearrange("(m p) c -> p m c", p=128), MKV[l]).then_inc(kv_out, 16)

            def load_pages(t, first, last):
                for p in range(first, last):
                    sp.wait_ge(cp_a, t.value(NPG, p - 7, base=START.cp_a))
                    sp.wait_ge(cp_b, t.value(NPG, p - 7, base=START.cp_b))
                    page = sp.value_load(ptab[0:1, bass.ds(t.at(NPG, p), 1)], min_val=0, max_val=POOL - 1)
                    sp.dma_start(PG[p % 8], I["ccmp"][bass.ds(page, 1)].rearrange("a p c -> (a p) c")
                                 ).then_inc(cp_in[p % 8], 16)

            sp.wait_ge(const_in, 48)
            sp.wait_ge(h_turned, 14)
            with sp.Fori(0, CT // 2) as i:
                for n in range(2):
                    t = Turn(i, n, 2)
                    load_pages(t, 0, 8)
                    sp.wait_ge(product, t.value(4, 0, base=PBASE[B_CONV]))
                    sp.dma_start(W[(B_CONV + 1 + n) % 2].rearrange("p k c -> p (k c)"),
                                 I["wall"][bass.ds(t.at(1, B_CONV + 1), 1)].rearrange("a p c -> (a p) c")
                                 ).then_inc(w_in[(B_CONV + 1 + n) % 2], 16)
                    load_pages(t, 8, NPG)
            sp.wait_ge(product, PBASE[B_OUT0])
            load_w(B_OUT0 + 1)
            sp.wait_ge(state_kept, START.state_kept + 2 * CT)
            sp.dma_start(O["conv"], CS).then_inc(state_out, 16)

            def mem_loads(l):
                with sp.Fori(0, NB // 2) as i:
                    for n in range(2):
                        t = Turn(i, n, 2)
                        if l == 0:
                            sp.wait_ge(conv_y, START.conv_y + CT)
                        else:
                            sp.wait_ge(gates_taken, 1)
                        sp.wait_ge(ms_o, t.value(1, -1, base=NB * l + START.ms_o))
                        MC = at(MA[l] + 5632 + 1024 * n, 1024).rearrange("p (m c) -> p m c", m=2)
                        sp.dma_start(MC, I["cmem"][l, bass.ds(t.at(1), 1)].rearrange("a (m p) c -> (a p) m c", p=128)
                                     ).then_inc(ms_in[n], 16)

            sp.wait_ge(cp_phi, CT)
            mem_loads(0)
            sp.wait_ge(ma_done, PT)
            sp.wait_ge(ms_gm, 1)
            load_pages(Turn(0, CT, 1), 0, NPG)
            sp.wait_ge(product, PBASE[B_N - 1])
            load_w(B_N)
            load_pages(Turn(0, CT + 1, 1), 0, NPG)
            sp.dma_start(O["win_s"][:, 0:WIN - NT, :], I["win"][:, NT:WIN, :]).then_inc(win_copied, 16)
            sp.dma_start(Wg.rearrange("p k c -> p (k c)"), I["wg"]).then_inc(wg_in, 16)
            for n in range(B_N + 1, B_OUT1):
                sp.wait_ge(product, PBASE[n - 1])
                load_w(n)
            sp.wait_ge(sig_done, 3)
            sp.dma_start(gates_dram, Gate[0:NS, PT, :]).then_inc(gates_written, 16)
            mem_loads(1)
            sp.wait_ge(gates_written, 16)
            sp.wait_ge(qz_zero, 2)
            g_src = gates_dram.rearrange("(b t) (s r g) -> t b s r g", b=NB, s=3, r=GRP)
            with nc.allow_non_contiguous_dma(reason="2304 numbers in all"):
                for g in range(KVH):
                    for r in range(GRP):
                        for s in range(3):
                            sp.dma_start(Grow[32 * g + 8 * r:32 * g + 8 * r + 8, :, s:s + 1], g_src[:, :, s:s + 1, r, g]
                                         ).then_inc(gates_back, 16)
            sp.wait_ge(roped, 4)
            for s, (name, kc, ko, vc, vo) in enumerate((("cmp", 2, 256, 3, 0), ("sel", 3, 256, 4, 0), ("win", 4, 256, 5, 0))):
                for half, (c, o) in enumerate(((kc, ko), (vc, vo))):
                    sp.dma_start(O[name + "_p"][:, half * 256:half * 256 + 256].rearrange("(t p) c -> p t c", p=128),
                                 P1[c][:, 0:PT, o:o + 256]).then_inc(kv_stored, 16)
                    rows = P1[c][0:NS, PT, o:o + 256]
                    if name == "win":
                        for b in range(NB):
                            sp.dma_start(O["win_s"][b, WIN - NT:WIN, half * 256:half * 256 + 256],
                                         P1[c][NT * b:NT * b + NT, PT, o:o + 256]).then_inc(kv_stored, 16)
                    else:
                        sp.dma_start(O[name + "_s"][:, half * 256:half * 256 + 256], rows).then_inc(kv_stored, 16)



            sp.wait_ge(yg_c, PT)
            sp.wait_ge(kv_stored, 16 * (2 * 3 + 2 * 2 + 2 * NB))
            with sp.Fori(0, NB // 2) as i:
                for n in range(2):
                    t = Turn(i, n, 2)
                    b = t.at(1)
                    first = b * NPG
                    for half in range(2):
                        sp.wait_ge(sa_ft, t.value(10, -6 + 4 * half, base=START.sa_ft))
                        for p in range(8):
                            page = sp.value_load(ptab[0:1, bass.ds(first + (8 * half + p), 1)], min_val=0, max_val=POOL - 1)
                            row = I["csel"][bass.ds(page, 1)].rearrange("a p c -> (a p) c")
                            sp.dma_start(SK[half][:, p, :], row[:, 0:256]).then_inc(sa_k[half], 16)
                            if half == 0 and p == 0:
                                sp.wait_ge(sa_used, t.value(6, -6, base=START.sa_used))
                            sp.dma_start(SV[n][:, 8 * half + p, :], row[:, 256:512]).then_inc(sa_v[n], 16)
                    sp.dma_start(SWI[n], I["win"][bass.ds(b, 1)].rearrange("a (s p) c -> (a p) s c", p=128)
                                 ).then_inc(sa_w[n], 16)
            sp.wait_ge(sz_done, 1)
            for n in range(B_OUT1, NBLK):
                load_w(n)
            sp.wait_ge(product, PBASE[NBLK])
            sp.dma_start(gfin, I["gfin"]).then_inc(gfin_in, 16)
            for t in range(TT):
                sp.wait_ge(y_ready, t + 1)
                if t < PT:
                    sp.dma_start(O["yp"][128 * t:128 * t + 128, :], fin[t % 2]).then_inc(y_out[t % 2], 16)
                else:
                    sp.dma_start(O["ys"], fin[t % 2][0:NS, :]).then_inc(y_out[t % 2], 16)
            for n in range(2):
                sp.wait_ge(y_out[n], 16 * ((TT + 1 - n) // 2))
            sp.wait_ge(state_out, 16)
            sp.wait_ge(kv_out, 32)
            sp.wait_ge(win_copied, 16)

        @block.gpsimd
        def _(pool):
            for signal, start in (
                    (cp_a, START.cp_a), (cp_b, START.cp_b), (cp_sum, START.cp_sum), (conv_y, START.conv_y), (ms_s, START.ms_s),
                    (u_made, START.u_made), (pa_t, START.pa_t), (pa_o, START.pa_o), (sa_bt, START.sa_bt),
                    (c_copied, START.c_copied), (s_copied, START.s_copied), (b_used, START.b_used), (z_used, START.z_used),
                    (ms_kc, START.ms_kc), (ms_c, START.ms_c), (ms_done, START.ms_done), (cp_rows, START.cp_rows), (cp_cols, START.cp_cols),
                    (cp_took, START.cp_took), (pa_p, START.pa_p), (pa_mix, START.pa_mix), (pa_ta, START.pa_ta),
                    (pa_ts, START.pa_ts), (sa_ba, START.sa_ba), (sa_bd, START.sa_bd), (sa_m, START.sa_m),
                    (sa_p, START.sa_p), (sa_done, START.sa_done), (state_kept, START.state_kept), (ms_y, START.ms_y),
                    (sa_y, START.sa_y), (pa_s, START.pa_s), (sa_used, START.sa_used), (sa_ft, START.sa_ft),
                    (sa_s, START.sa_s), (ms_o, START.ms_o),):
                pool.sem_inc(signal, start)
            nc.gpsimd.memset(QZ, 0.0).then_inc(qz_zero, 1)
            nc.gpsimd.memset(Grow, 0.0).then_inc(qz_zero, 1)
            pool.wait_ge(const_in, 48)
            pool.wait_ge(product, PBASE[B_C0])
            for n in range(2):
                nc.gpsimd.memset(U[n][:, 0:2], 0.0).then_inc(pad_zero, 1)
            for k in range(KD):
                ins = nc.gpsimd.memset(YT0[:, k, SEQ + NS:TOK], 0.0)
            ins.then_inc(pad_zero, 1)

            def page_prod1(t):
                for p in range(NPG):
                    pool.wait_ge(cp_in[p % 8], t.value(32, 16 * (p // 8 + 1)))
                    pool.wait_ge(cp_sum, t.value(NPG, p - 3, base=START.cp_sum))
                    nc.gpsimd.tensor_tensor(CPB[p % 4], PG[p % 8], S("pos1"), ALU.mult).then_inc(cp_b, 1)

            with pool.Fori(0, CT // 2) as i:
                for n in range(2):
                    t = Turn(i, n, 2)
                    Us = U[n][:, 514:594].rearrange("p (b c) -> p b c", b=NB)
                    pool.wait_ge(conv_y, t.value(1, -1, base=START.conv_y))
                    src = small[:, bass.ds(t.at(16, SMALL["state"][0]), 16)].rearrange("p (b c) -> p b c", b=NB)
                    nc.gpsimd.tensor_copy(Us[:, :, 0:2], src).then_inc(state_set, 1)
                    page_prod1(t)
                    pool.wait_ge(u_made, t.value(2, 2, base=START.u_made))
                    nc.gpsimd.tensor_copy(CS[:, bass.ds(t.at(18), 2)], U[n][:, 512:514]).then_inc(state_kept, 1)
                    nc.gpsimd.tensor_copy(CS[:, bass.ds(t.at(18, 2), 16)].rearrange("p (b c) -> p b c", b=NB),
                                          Us[:, :, 8:10]).then_inc(state_kept, 1)

            def mem_q(l):
                QZm = at(MA[l], 2048).rearrange("p (g b m) -> p g b m", g=2, b=NB)
                if l == 0:
                    pool.wait_ge(conv_y, START.conv_y + CT)
                    pool.wait_ge(state_kept, START.state_kept + 2 * CT)
                else:
                    pool.wait_ge(sig_done, 3)
                nc.gpsimd.memset(QZm, 0.0).then_inc(ms_qz, 1)
                pool.wait_ge(ms_qz, 5 * (l + 1))
                with pool.Fori(0, NB // 2) as i:
                    for n in range(2):
                        t = Turn(i, n, 2)
                        QB = at(MA[l] + 2048 + 256 * n, 256).rearrange("p (g m) -> p g m", g=2)
                        pool.wait_ge(ms_s, t.value(1, -1, base=NB * l + START.ms_s))
                        nc.gpsimd.tensor_copy(QB, QZm[:, :, bass.ds(t.at(1), 1), :].rearrange("p g a m -> p g (a m)")
                                              ).then_inc(ms_qb, 1)
            mem_q(0)
            pool.wait_ge(ma_done, PT)
            pool.wait_ge(ms_gm, 1)
            for b in range(CT, NB):
                page_prod1(Turn(0, b, 1))
            mem_q(1)

            for p in range(PT):
                pool.wait_ge(ma_done, 2 * PT)
                pool.wait_ge(ms_gm, 2)
                pool.wait_ge(roped, 4)
                if p >= 2:
                    pool.wait_ge(cp_sum, NB * NPG + START.cp_sum + p - 1)
                nc.gpsimd.tensor_tensor(PB[p % 2][:, 0:256], P1[2][:, p, 256:512], S("pos1")[:, 0:256], ALU.mult)
                nc.gpsimd.tensor_tensor(PB[p % 2][:, 256:512], P1[3][:, p, 0:256], S("pos1")[:, 256:512],
                                        ALU.mult).then_inc(cp_b, 1)

            pool.wait_ge(r_spread, 6)
            pool.wait_ge(yg_c, PT)
            pool.wait_ge(kv_stored, 16 * (2 * 3 + 2 * 2 + 2 * NB))
            nc.gpsimd.memset(HT[:, 2:8, SEQ + NS:TOK], 0.0).then_inc(ht_zero, 1)
            with pool.Fori(0, NB // 2) as i:
                for n in range(2):
                    t = Turn(i, n, 2)
                    pool.wait_ge(sa_s, t.value(1, -1, base=START.sa_s))
                    nc.gpsimd.tensor_copy(SQB[n], QZ[:, :, bass.ds(t.at(1), 1), :].rearrange("p g a m -> p g (a m)")
                                          ).then_inc(sa_qb, 1)

        @block.scalar
        def _(act):
            lk = Links(act, act_links)

            def norm_act(tiles, first, number):
                for j, src in enumerate(tiles):
                    if number == 0:
                        act.wait_ge(mem_in if j < 2 else x_in, 16 if j < 2 else 32)
                        if j == 6:
                            act.wait_ge(x_zero, 1)
                    elif number == 1:
                        act.wait_ge(out_added, 2 * TT)
                    else:
                        act.wait_ge(out_added, 4 * TT)
                    nc.scalar.activation(SQ, src, ACT.Square, accum_out=rs(first + j, first + j + 1)).then_inc(squared, 1)
                    act.wait_ge(squared, first + j + 1)
                act.wait_ge(mean_sq, number + 1)
                nc.scalar.activation(rs(20 + first, 20 + first + len(tiles)), rs(20 + first, 20 + first + len(tiles)),
                                     ACT.Sqrt).then_inc(root, 1)
                act.wait_ge(rstd, number + 1)

            tiles0 = [M[:, 0, :], M[:, 1, :]] + [X[:, t, :] for t in range(TT)]
            norm_act(tiles0, 0, 0)
            for j, src in enumerate(tiles0):
                if j >= 2:
                    act.wait_ge(h_turned, 2 * (j - 1))
                nc.scalar.activation(H[j % 2], src, ACT.Copy, scale=rs(20 + j, 21 + j)).then_inc(scaled, 1)
            for l in range(2):
                for m in range(2):
                    act.wait_ge(product, 2 * l + m + 1)
                    nc.scalar.copy(MKV[l][:, m, :], PS[:, 2 * l + m, :]).then_inc(kv_taken, 1)
            for l in range(2):
                act.wait_ge(kt_turned, l + 1)
                nc.scalar.copy(KTm[l].rearrange("p g m -> p (g m)"), PS[:, 4 + l, :]).then_inc(kt_taken, 1)

            def take_chunk(c, P, first):
                for t in range(TT):
                    act.wait_ge(product, first + t + 1)
                    nc.scalar.copy(P[:, t, :], PS[:, t, :]).then_inc(chunk_taken, 1)

            take_chunk(0, MQG0, PBASE[B_C0])

            def copy_rows(t):
                act.wait_ge(cp_sum, t.value(NPG, NPG, base=START.cp_sum))
                nc.scalar.copy(CR[0:NC, :], PS[0:NC, 5, :]).then_inc(cp_rows, 1)

            def keep_blocks(t):
                act.wait_ge(cp_turned, t.value(1, 1))
                nc.scalar.copy(CBL[:, :, 0:NC], PS[:, 6, :].rearrange("p (s c) -> p s c", s=4)[:, :, 0:NC]
                               ).then_inc(cp_cols, 1)
                act.wait_ge(cp_phi, t.value(1, 1))
                nc.scalar.copy(KC[:, :, bass.ds(t.at(1), 1), 0:NC].rearrange("p g a n -> p g (a n)"),
                               PS[:, 7, 0:256].rearrange("p (g n) -> p g n", g=2)[:, :, 0:NC])
                nc.scalar.copy(VC[0:NC, bass.ds(t.at(1), 1), :].rearrange("p a n -> p (a n)"),
                               PS[0:NC, 7, 256:512]).then_inc(cp_took, 1)

            with act.Fori(0, CT // 2) as i:
                for n in range(2):
                    t = Turn(i, n, 2)
                    act.wait_ge(product, t.value(4, 1, base=PBASE[B_CONV]))
                    act.wait_ge(u_made, t.value(2, 0, base=START.u_made))
                    nc.scalar.copy(Cb[:, 0:512], PS[:, 0, :]).then_inc(c_copied, 1)
                    copy_rows(t)
                    act.wait_ge(product, t.value(4, 4, base=PBASE[B_CONV]))
                    act.wait_ge(conv_y, t.value(1, 0, base=START.conv_y))
                    nc.scalar.copy(Sb, PS[:, 4, 0:256]).then_inc(s_copied, 1)
                    nc.scalar.activation(E[:, 0:512], PS[:, 3, :], ACT.Exp, scale=-1.0)
                    act.wait_ge(s_copied, t.value(1, 1, base=START.s_copied))
                    nc.scalar.activation(E[:, 512:576], Sb[:, 192:256], ACT.Exp, scale=-1.0).then_inc(z_exp, 1)
                    keep_blocks(t)

            def mem_prompt_act(l, YT):
                QTt, P, PTb, MG = (mem_bufs(l)[k] for k in ("QT", "P", "PT", "MG"))
                act.wait_ge(chunk_taken, TT if l == 0 else 8 * TT)
                if l == 0:
                    act.wait_ge(conv_y, START.conv_y + CT)
                else:
                    act.wait_ge(gates_taken, 1)
                P0 = MQG0 if l == 0 else P1[0]
                nc.scalar.activation(MG, P0[:, :, 256:512], ACT.Exp, scale=-1.0).then_inc(sig_exp, 1)
                for n in range(PT):
                    T = l * PT + n
                    act.wait_ge(ma_qt, T + 1)
                    nc.scalar.copy(QTt[n % 2], PS[:, 5, 256 * (n % 2):256 * (n % 2) + 256]).then_inc(ma_qc, 1)
                    act.wait_ge(ma_m, 2 * (T + 1))
                    if T >= 2:
                        act.wait_ge(ma_t, 2 * (T - 1))
                    for h in range(4):
                        nc.scalar.activation(P[n % 2][:, h, :], PS[:, 2 * (n % 2) + h % 2, 256 * (h // 2):256 * (h // 2) + 256],
                                             ACT.Exp, bias=rs(60 + 8 * (n % 2) + h, 61 + 8 * (n % 2) + h),
                                             accum_out=rs(76 + 8 * (n % 2) + h, 77 + 8 * (n % 2) + h)).then_inc(ma_p, 1)
                    act.wait_ge(ma_t, 2 * (T + 1))
                    act.wait_ge(ma_o, T)
                    nc.scalar.copy(PTb[:, 512:1024], PS[:, 7, :]).then_inc(ma_ta, 1)
                    act.wait_ge(ma_yt, T + 1)
                    nc.scalar.copy(YT[:, 0:2, 128 * n:128 * n + 128],
                                   PS[:, 5, 256 * (n % 2):256 * (n % 2) + 256].rearrange("p (g c) -> p g c", g=2)
                                   ).then_inc(ma_done, 1)

            def mem_sample_act(l):
                b_ = mem_bufs(l)
                with act.Fori(0, NB // 2) as i:
                    for n in range(2):
                        t = Turn(i, n, 2)
                        v = lambda plus: t.value(1, plus, base=NB * l)
                        act.wait_ge(ms_kt, v(1))
                        nc.scalar.copy(b_["KTb"][n], PS[:, 6, :]).then_inc(ms_kc, 1)
                        act.wait_ge(ms_m, v(1))
                        nc.scalar.activation(b_["SP"][n], PS[:, n, 0:256], ACT.Exp, bias=rs(100 + n, 101 + n),
                                             accum_out=rs(104 + n, 105 + n)).then_inc(ms_p, 1)

            mem_prompt_act(0, YT0)
            mem_sample_act(0)
            for b in range(CT, NB):
                copy_rows(Turn(0, b, 1))
                keep_blocks(Turn(0, b, 1))
            norm_act([X[:, t, :] for t in range(TT)], 7, 1)
            for j in range(TT):
                act.wait_ge(h_turned, 2 * (7 + j - 1))
                nc.scalar.activation(H[(7 + j) % 2], X[:, j, :], ACT.Copy, scale=rs(27 + j, 28 + j)).then_inc(scaled, 1)
            with act.Fori(0, 3) as i:
                for n in range(2):
                    t = Turn(i, n, 2)
                    for j in range(TT):
                        act.wait_ge(product, t.value(TT, j + 1, base=PBASE[B_N]))
                        nc.scalar.copy(P1all[:, bass.ds(t.at(2560, 512 * j), 512)], PS[:, j, :]).then_inc(chunk_taken, 1)
            take_chunk(6, P1[6], PBASE[B_N + 6])
            act.wait_ge(product, P_GATES + TT)
            nc.scalar.activation(Gate[:, :, :], PS[:, 5, 0:180].rearrange("p (t c) -> p t c", t=TT), ACT.Exp,
                                 scale=-1.0).then_inc(gates_taken, 1)
            Z5 = sig[:, 0:1280].rearrange("p (t c) -> p t c", t=TT)
            Z6 = sig[:, 1280:3840].rearrange("p (t c) -> p t c", t=TT)
            act.wait_ge(gates_taken, 1)
            act.wait_ge(chunk_taken, 8 * TT)
            nc.scalar.activation(Z5, P1[5][:, :, 256:512], ACT.Exp, scale=-1.0).then_inc(z_exp, 1)
            nc.scalar.activation(Z6, P1[6], ACT.Exp, scale=-1.0).then_inc(z_exp, 1)
            mem_prompt_act(1, HT)
            mem_sample_act(1)
            for j in range(10):
                act.wait_ge(r_turned, j + 1)
                if j < 6:
                    nc.scalar.activation(QT[:, j // 2, j % 2, :], PS[:, j % 4, :], ACT.Copy, scale=SCALE).then_inc(r_took, 1)
                else:
                    K = (KTs, KTw)[(j - 6) // 2]
                    nc.scalar.copy(K[:, j % 2, :], PS[:, j % 4, :]).then_inc(r_took, 1)
            act.wait_ge(cp_sum, NB * NPG + PT + START.cp_sum)
            nc.scalar.copy(CRp[0:NCP, :], PS[0:NCP, 2, :]).then_inc(cp_rows, 1)
            act.wait_ge(cp_turned, NB + 1)
            nc.scalar.copy(BLp[:, :, 0:NCP], PS[:, 3, :].rearrange("p (s c) -> p s c", s=4)[:, :, 0:NCP]
                           ).then_inc(cp_cols, 1)
            act.wait_ge(cp_phi, NB + 1)
            nc.scalar.copy(KCp[:, :, 0:NCP], PS[:, 5, 0:256].rearrange("p (g n) -> p g n", g=2)[:, :, 0:NCP])
            nc.scalar.copy(VCp[0:NCP, :], PS[0:NCP, 5, 256:512]).then_inc(cp_took, 1)
            with act.Fori(0, GRP) as r:
                def exps(n):
                    t = Turn(r, n, 16)
                    ti = n % PT
                    pr = n % 2
                    act.wait_ge(pa_m, t.value(3, 3))
                    act.wait_ge(pa_t, t.value(3, -3, base=START.pa_t))
                    nk = 128 * (ti + 1)
                    nc.scalar.activation(PP[pr][:, 1024:1024 + NCP], PS[:, 4, 0:NCP], ACT.Exp,
                                         bias=rs(120 + 4 * pr, 121 + 4 * pr)).then_inc(pa_p, 1)
                    for s in range(2):
                        nc.scalar.activation(PP[pr][:, 512 * s:512 * s + nk], PS[:, 2 * pr + s, 0:nk], ACT.Exp,
                                             bias=rs(121 + s + 4 * pr, 122 + s + 4 * pr),
                                             accum_out=rs(129 + s + 4 * pr, 130 + s + 4 * pr)).then_inc(pa_p, 1)

                def took(n):
                    t = Turn(r, n, 16)
                    nk = 128 * (n % PT + 1)
                    act.wait_ge(pa_t, t.value(3, 1, base=START.pa_t))
                    act.wait_ge(pa_o, t.value(1, 0, base=START.pa_o))
                    nc.scalar.copy(PTt[0:NCP, 1024:1152], PS[0:NCP, 5, 0:128]).then_inc(pa_ta, 1)
                    act.wait_ge(pa_t, t.value(3, 3, base=START.pa_t))
                    nc.scalar.copy(PTt[:, 512:512 + nk], PS[:, 7, 0:nk]).then_inc(pa_ta, 1)

                for n in range(16):
                    exps(n)
                    if n:
                        took(n - 1)
                took(15)
            for t in range(PT):
                act.wait_ge(yg_t, 2 * t + 1)
                nc.scalar.copy(HT[:, 2:6, 128 * t:128 * t + 128], PS[:, 6, :].rearrange("p (k c) -> p k c", k=4))
                act.wait_ge(yg_t, 2 * t + 2)
                nc.scalar.copy(HT[:, 6:8, 128 * t:128 * t + 128], PS[:, 7, 0:256].rearrange("p (k c) -> p k c", k=2)
                               ).then_inc(yg_c, 1)

            def front(t, prev):
                act.wait_ge(sa_cm, t.value(1, 1))
                act.wait_ge(sa_bt, t.value(6, -6, base=START.sa_bt))
                nc.scalar.activation(SPC[t.n % 2][:, 0:NC], PS[:, 5, 0:NC], ACT.Exp, bias=rs(140, 141),
                                     accum_out=rs(141, 142)).then_inc(sa_ce, 1)
                for j in range(0, 10, 2):
                    act.wait_ge(sa_ft, t.value(10, j + 1, base=START.sa_ft))
                    if j < 8:
                        nc.scalar.copy(SKT[:, :, 256 * j:256 * j + 256], PS[:, 6, :].rearrange("p (g c) -> p g c", g=2)
                                       ).then_inc(sa_fa, 1)
                    else:
                        nc.scalar.copy(SWKT[:, 0, :], PS[:, 6, :]).then_inc(sa_fa, 1)

            def middle(t):
                act.wait_ge(sa_m, t.value(2, 1, base=START.sa_m))
                nc.scalar.activation(SM, SM, ACT.Exp, bias=rs(150, 151), accum_out=rs(152, 153)).then_inc(sa_p, 1)
                act.wait_ge(sa_m, t.value(2, 2, base=START.sa_m))
                nc.scalar.activation(SW[:, 0:512], PS[:, 4, :], ACT.Exp, bias=rs(151, 152), accum_out=rs(153, 154)
                                     ).then_inc(sa_p, 1)
                nc.scalar.activation(SW[:, 512:576], SW[:, 512:576], ACT.Exp, bias=rs(151, 152),
                                     accum_out=rs(154, 155)).then_inc(sa_p, 1)

            def back(t, fronts):
                for j in range(0, 6, 2):
                    act.wait_ge(sa_bt, t.value(6, j + 1, base=START.sa_bt))
                    act.wait_ge(sa_used, t.value(6, j - 1, base=START.sa_used))
                    nc.scalar.copy(SPT[0], PS[:, 6, :].rearrange("p (s c) -> p s c", s=4)).then_inc(sa_ba, 1)

            sample_phase(act, front, middle, back)
            norm_act([X[:, t, :] for t in range(TT)], 12, 2)
            for j in range(TT):
                if j >= 2:
                    act.wait_ge(y_ready, j - 1)
                nc.scalar.activation(H[j % 2], X[:, j, :], ACT.Copy, scale=rs(32 + j, 33 + j)).then_inc(fin_scaled, 1)

        @block.tensor
        def _(pe):
            def mm(out, lhsT, rhs, start=True, stop=True):
                return nc.tensor.matmul(out, lhsT, rhs, start=start, stop=stop, skip_group_check=True)

            def turn(out, in_):
                return nc.tensor.transpose(out, in_, ident[0:in_.shape[0], 0:in_.shape[0]])

            pe.wait_ge(const_in, 48)

            def norm_turns(first, count):
                for j in range(first, first + count):
                    pe.wait_ge(scaled, j + 1)
                    for half in range(2):
                        n = 2 * j + half
                        if n >= 4:
                            pe.wait_ge(h_taken, n - 3)
                        for k in range(4):
                            ins = turn(PS[:, n % 4, 128 * k:128 * k + 128],
                                       H[j % 2][:, 512 * half + 128 * k:512 * half + 128 * k + 128])
                        ins.then_inc(h_turned, 1)

            norm_turns(0, 7)
            pe.wait_ge(h_taken, 14)
            for l in range(2):
                pe.wait_ge(w_in[l], 16)
                for m in range(2):
                    for k in range(KD):
                        ins = mm(PS[:, 2 * l + m, :], memT[l][:, k, 128 * m:128 * m + 128], W[l][:, k, :],
                                 k == 0, k == KD - 1)
                    ins.then_inc(product, 1)
            for l in range(2):
                pe.wait_ge(kv_taken, 2 * (l + 1))
                for g in range(2):
                    for m in range(2):
                        ins = turn(PS[:, 4 + l, 256 * g + 128 * m:256 * g + 128 * m + 128],
                                   MKV[l][:, m, 128 * g:128 * g + 128])
                ins.then_inc(kt_turned, 1)

            def chunk(src, Wb, taken, beside=None):
                for t in range(TT):
                    if taken is not None:
                        pe.wait_ge(*taken(t))
                    for k in range(KD):
                        ins = mm(PS[:, t, :], src[:, k, 128 * t:128 * t + 128], Wb[:, k, :], k == 0, k == KD - 1)
                    ins.then_inc(product, 1)
                    if beside is not None:
                        beside(t)

            pe.wait_ge(w_in[0], 32)
            pe.wait_ge(kv_taken, 4)
            pe.wait_ge(kt_taken, 2)
            chunk(HT, W[0], None)
            pe.wait_ge(kt_taken, 2)
            pe.wait_ge(chunk_taken, TT)

            def sums(A, Bp, p, pages, out):
                n = 8 * pages
                mm(out, C("chunk")[:, 120 - 8 * p:120 - 8 * p + n], A, p == 0, False)
                mm(out, C("chunk")[:, 121 - 8 * p:121 - 8 * p + n], Bp, False, p == pages - 1).then_inc(cp_sum, 1)

            def turn_blocks(rows, bank, nch):
                for s in range(4):
                    ins = turn(PS[:, bank, 128 * s:128 * s + nch], rows[0:nch, 128 * s:128 * s + 128])
                ins.then_inc(cp_turned, 1)

            def phi(BL, bank, nch):
                for g in range(2):
                    mm(PS[:, bank, 128 * g:128 * g + nch], S("phi_k"), BL[:, g, 0:nch])
                for g in range(2):
                    ins = mm(PS[0:nch, bank, 256 + 128 * g:384 + 128 * g], BL[:, 2 + g, 0:nch], S("phi_v"))
                ins.then_inc(cp_phi, 1)

            def page_sums(t, first, last):
                if first == 0:
                    pe.wait_ge(cp_rows, t.value(1, 0, base=START.cp_rows))
                for p in range(first, last):
                    pe.wait_ge(cp_a, t.value(NPG, p + 1, base=START.cp_a))
                    pe.wait_ge(cp_b, t.value(NPG, p + 1, base=START.cp_b))
                    sums(CPA[p % 4], CPB[p % 4], p, NPG, PS[:, 5, :])

            def page_turn(t):
                pe.wait_ge(cp_rows, t.value(1, 1, base=START.cp_rows))
                pe.wait_ge(cp_cols, t.value(1, 0, base=START.cp_cols))
                turn_blocks(CR, 6, NC)

            def page_phi(t):
                pe.wait_ge(cp_cols, t.value(1, 1, base=START.cp_cols))
                pe.wait_ge(cp_took, t.value(1, 0, base=START.cp_took))
                phi(CBL, 7, NC)

            between = {(1, 3): (0, 4), (1, 7): (4, 8), (2, 3): (8, 12), (2, 7): (12, NPG)}
            with pe.Fori(0, CT // 2) as i:
                for n in range(2):
                    t = Turn(i, n, 2)
                    w = (n + 1) % 2
                    pe.wait_ge(w_in[w], i * 16 + (32 if w == 1 else 48))
                    for q in range(4):
                        if q == 0:
                            pe.wait_ge(c_copied, t.value(1, 0, base=START.c_copied))
                            pe.wait_ge(s_copied, t.value(1, 0, base=START.s_copied))
                        elif q == 1:
                            pe.wait_ge(u_made, t.value(2, 0, base=START.u_made))
                        elif q == 2:
                            pe.wait_ge(b_used, t.value(1, 0, base=START.b_used))
                        else:
                            pe.wait_ge(z_used, t.value(1, 0, base=START.z_used))
                        for k in range(KD):
                            mm(PS[:, q, :], W[w][:, k, 128 * q:128 * q + 128], HT[:, k, 0:512], k == 0, k == KD - 1)
                            if (q, k) in between:
                                page_sums(t, *between[q, k])
                            if (q, k) == (3, 6):
                                page_turn(t)
                        for k in range(KD):
                            ins = mm(PS[:, 4, 64 * q:64 * q + 64], W[w][:, k, 128 * q:128 * q + 128],
                                     HT[:, k, 512:576], k == 0, k == KD - 1)
                        ins.then_inc(product, 1)
                    page_phi(t)

            def mem_prompt(l):
                b_ = mem_bufs(l)
                QTt, P, PTb = b_["QT"], b_["P"], b_["PT"]
                for n in range(PT):
                    T = l * PT + n
                    pr = n % 2
                    pe.wait_ge(ma_q, T + 1)
                    pe.wait_ge(ma_done, T)
                    for g in range(2):
                        ins = turn(PS[:, 5, 256 * pr + 128 * g:256 * pr + 128 * g + 128], b_["QS"][:, 128 * g:128 * g + 128])
                    ins.then_inc(ma_qt, 1)
                    pe.wait_ge(ma_qc, T + 1)
                    if T >= 2:
                        pe.wait_ge(ma_p, 4 * (T - 1))
                    for h in range(4):
                        o = 64 * (h % 2)
                        ins = mm(PS[:, 2 * pr + h % 2, 256 * (h // 2):256 * (h // 2) + 256],
                                 QTt[pr][o:o + 64, 128 * (h // 2):128 * (h // 2) + 128], KTm[l][o:o + 64, h // 2, :])
                    ins.then_inc(ma_s, 1)
                    pe.wait_ge(ma_p, 4 * (T + 1))
                    pe.wait_ge(ma_td, T)
                    pe.wait_ge(ma_ta, T)
                    for h in range(4):
                        for m in range(2):
                            ins = turn(PS[:, 6 + h // 2, 256 * (h % 2) + 128 * m:256 * (h % 2) + 128 * m + 128],
                                       P[pr][:, h, 128 * m:128 * m + 128])
                        if h % 2:
                            ins.then_inc(ma_t, 1)
                    if T >= 2:
                        pe.wait_ge(ma_y, T - 1)
                    pe.wait_ge(ma_td, T + 1)
                    pe.wait_ge(ma_ta, T + 1)
                    for h in range(4):
                        for m in range(2):
                            ins = mm(PS[:, 4, 256 * pr + 64 * h:256 * pr + 64 * h + 64],
                                     PTb[:, 256 * h + 128 * m:256 * h + 128 * m + 128],
                                     MKV[l][:, m, 256 + 64 * h:256 + 64 * h + 64], m == 0, m == 1)
                    ins.then_inc(ma_o, 1)
                    pe.wait_ge(ma_y, T + 1)
                    for g in range(2):
                        ins = turn(PS[:, 5, 256 * pr + 128 * g:256 * pr + 128 * g + 128], b_["OY"][:, 128 * g:128 * g + 128])
                    ins.then_inc(ma_yt, 1)

            def mem_sample(l):
                b_ = mem_bufs(l)
                pe.wait_ge(ms_q, l + 1)
                pe.wait_ge(ma_done, PT * (l + 1))
                for g in range(2):
                    ins = turn(PS[:, 5, 128 * g:128 * g + 128], b_["QS"][:, 128 * g:128 * g + 128])
                ins.then_inc(ms_qt, 1)
                pe.wait_ge(ma_y, PT * (l + 1))
                with pe.Fori(0, NB // 2) as i:
                    for n in range(2):
                        t = Turn(i, n, 2)
                        v = lambda plus: t.value(1, plus, base=NB * l)
                        pe.wait_ge(ms_in[n], i * 16 + 16 * (1 + l * NB // 2))
                        pe.wait_ge(ms_kc, v(START.ms_kc))
                        for g in range(2):
                            for m in range(2):
                                ins = turn(PS[:, 6, 256 * g + 128 * m:256 * g + 128 * m + 128],
                                           b_["MC"][n][:, m, 128 * g:128 * g + 128])
                        ins.then_inc(ms_kt, 1)
                        pe.wait_ge(ms_kc, v(START.ms_kc + 1))
                        pe.wait_ge(ms_qb, v(1))
                        for g in range(2):
                            ins = mm(PS[:, n, 0:256], b_["QB"][n][:, g, :], b_["KTb"][n][:, 256 * g:256 * g + 256],
                                     g == 0, g == 1)
                        ins.then_inc(ms_s, 1)
                        pe.wait_ge(ms_p, v(1))
                        pe.wait_ge(ms_c, v(START.ms_c))
                        for m in range(2):
                            ins = turn(PS[:, 7, 128 * m:128 * m + 128], b_["SP"][n][:, 128 * m:128 * m + 128])
                        ins.then_inc(ms_t, 1)
                        pe.wait_ge(ms_c, v(START.ms_c + 1))
                        for m in range(2):
                            ins = mm(PS[:, 2 + n, 0:256], b_["SPT"][n][:, 128 * m:128 * m + 128],
                                     b_["MC"][n][:, m, 256:512], m == 0, m == 1)
                        ins.then_inc(ms_o, 1)
                        pe.wait_ge(ms_n, v(1))
                        pe.wait_ge(ms_done, v(START.ms_done))
                        for g in range(2):
                            ins = turn(PS[:, 4, 128 * g:128 * g + 128], b_["SO"][n][:, 128 * g:128 * g + 128])
                        ins.then_inc(ms_y, 1)
                pe.wait_ge(ms_qz, 5 * (l + 1))
                P0 = MQG0 if l == 0 else P1[0]
                for g in range(2):
                    ins = turn(PS[:, 5, 128 * g:128 * g + 128], P0[:, PT, 256 + 128 * g:256 + 128 * g + 128])
                ins.then_inc(ms_g, 1)

            def out_proj(YT, first, l):
                for n in range(2):
                    def beside(j):
                        t = Turn(0, CT + n, 1)
                        if j < PT:
                            page_sums(t, 4 * j, 4 * j + 4)
                        else:
                            page_turn(t)
                            page_phi(t)

                    pe.wait_ge(w_in[(first + n) % 2], w_count(first + n))
                    chunk(YT, W[(first + n) % 2],
                          lambda t, n=n: (out_added, 2 * TT * l + t + 1 if n else 2 * TT * l),
                          beside if l == 0 else None)

            pe.wait_ge(conv_y, START.conv_y + CT)
            pe.wait_ge(cp_took, START.cp_took + CT)
            mem_prompt(0)
            mem_sample(0)
            pe.wait_ge(ms_gm, 1)
            pe.wait_ge(pad_zero, 3)
            pe.wait_ge(ma_done, PT)
            out_proj(YT0, B_OUT0, 0)
            pe.wait_ge(out_added, 2 * TT)
            norm_turns(7, TT)
            pe.wait_ge(h_taken, 2 * 12)
            with pe.Fori(0, 3) as i:
                for n in range(2):
                    t = Turn(i, n, 2)
                    w = (B_N + n) % 2
                    pe.wait_ge(w_in[w], i * 16 + w_count(B_N + n))
                    chunk(HT, W[w], lambda j: (chunk_taken, t.value(TT, j - 4, base=TT)))
            pe.wait_ge(w_in[(B_N + 6) % 2], w_count(B_N + 6))
            chunk(HT, W[(B_N + 6) % 2], lambda j: (chunk_taken, 7 * TT + j - 4))
            pe.wait_ge(wg_in, 16)
            for j in range(TT):
                for k in range(KD):
                    ins = mm(PS[:, 5, 36 * j:36 * j + 36], HT[:, k, 128 * j:128 * j + 128], Wg[:, k, :], k == 0, k == KD - 1)
                ins.then_inc(product, 1)
            pe.wait_ge(chunk_taken, 8 * TT)
            pe.wait_ge(gates_taken, 1)
            mem_prompt(1)
            mem_sample(1)
            pe.wait_ge(roped, 4)
            pe.wait_ge(ms_gm, 2)
            pe.wait_ge(ms_p, 2 * NB)
            pe.wait_ge(ms_n, 2 * NB)
            for j in range(10):
                if j >= 4:
                    pe.wait_ge(r_took, j - 3)
                for t in range(PT):
                    if j < 6:
                        r, g = j // 2, j % 2
                        src = P1[1 + r // 2][:, t, 256 * (r % 2) + 128 * g:256 * (r % 2) + 128 * g + 128]
                    else:
                        src = P1[3 + (j - 6) // 2][:, t, 256 + 128 * (j % 2):384 + 128 * (j % 2)]
                    ins = turn(PS[:, j % 4, 128 * t:128 * t + 128], src)
                ins.then_inc(r_turned, 1)
            for j in range(6):
                r, g = j // 2, j % 2
                src = P1[1 + r // 2][0:NS, PT, 256 * (r % 2) + 128 * g:256 * (r % 2) + 128 * g + 128]
                ins = turn(PS[:, 6, 64 * j:64 * j + 64], src)
            ins.then_inc(r_turned, 1)
            for j in range(4):
                src = P1[3 + j // 2][0:NS, PT, 256 + 128 * (j % 2):384 + 128 * (j % 2)]
                ins = turn(PS[:, 7, 64 * j:64 * j + 64], src)
            ins.then_inc(r_turned, 1)
            pe.wait_ge(r_took, 10)
            for p in range(PT):
                pe.wait_ge(cp_a, START.cp_a + NB * NPG + p + 1)
                pe.wait_ge(cp_b, START.cp_b + NB * NPG + p + 1)
                sums(PA[p % 2], PB[p % 2], p, PT, PS[0:8 * PT, 2, :])
            pe.wait_ge(cp_rows, START.cp_rows + NB + 1)
            turn_blocks(CRp, 3, NCP)
            pe.wait_ge(cp_cols, START.cp_cols + NB + 1)
            phi(BLp, 5, NCP)
            pe.wait_ge(cp_took, START.cp_took + NB + 1)
            with pe.Fori(0, GRP) as r:
                def scores(n):
                    t = Turn(r, n, 16)
                    g, ti, pr = n // PT, n % PT, n % 2
                    gp, o = g // 2, 64 * (g % 2)
                    nk = 128 * (ti + 1)
                    pe.wait_ge(pa_p, t.value(3, -3, base=START.pa_p))
                    q = Qs[0][o:o + 64, gp, 128 * ti:128 * ti + 128]
                    mm(PS[:, 2 * pr, 0:nk], q, KTs[o:o + 64, gp, 0:nk])
                    mm(PS[:, 2 * pr + 1, 0:nk], q, KTw[o:o + 64, gp, 0:nk])
                    pe.wait_ge(pa_p, t.value(3, -2, base=START.pa_p))
                    mm(PS[:, 4, 0:NCP], q, KCp[o:o + 64, gp, 0:NCP]).then_inc(pa_s, 1)

                def turns(n):
                    t = Turn(r, n, 16)
                    g, ti, pr = n // PT, n % PT, n % 2
                    pe.wait_ge(pa_mix, t.value(1, 0, base=START.pa_mix))
                    pe.wait_ge(pa_ta, t.value(2, 0, base=START.pa_ta))
                    pe.wait_ge(pa_cm, t.value(1, 1))
                    turn(PS[0:NCP, 5, 0:128], PP[pr][:, 1024:1024 + NCP]).then_inc(pa_t, 1)
                    pe.wait_ge(pa_p, t.value(3, 3, base=START.pa_p))
                    pe.wait_ge(pa_ts, t.value(1, 0, base=START.pa_ts))
                    for j in range(ti + 1):
                        ins = turn(PS[:, 6, 128 * j:128 * j + 128], PP[pr][:, 128 * j:128 * j + 128])
                    ins.then_inc(pa_t, 1)
                    for j in range(ti + 1):
                        ins = turn(PS[:, 7, 128 * j:128 * j + 128], PP[pr][:, 512 + 128 * j:640 + 128 * j])
                    ins.then_inc(pa_t, 1)

                def outs(n):
                    t = Turn(r, n, 16)
                    g, ti, pr = n // PT, n % PT, n % 2
                    o = 128
                    pe.wait_ge(pa_ta, t.value(2, 1, base=START.pa_ta))
                    pe.wait_ge(pa_ts, t.value(1, 1, base=START.pa_ts))
                    for j in range(ti + 1):
                        mm(PS[:, 5, o + 64:o + 128], PTt[:, 128 * j:128 * j + 128], P1[4][:, j, 64 * g:64 * g + 64],
                           j == 0, j == ti)
                    pe.wait_ge(pa_ta, t.value(2, 2, base=START.pa_ta))
                    for j in range(ti + 1):
                        mm(PS[:, 5, o + 128:o + 192], PTt[:, 512 + 128 * j:640 + 128 * j], P1[5][:, j, 64 * g:64 * g + 64],
                           j == 0, j == ti)
                    mm(PS[:, 5, o:o + 64], PTt[0:NCP, 1024:1152], VCp[0:NCP, 64 * g:64 * g + 64]).then_inc(pa_o, 1)

                pe.wait_ge(pa_q, r + 1)
                for n in range(16):
                    scores(n)
                    if n:
                        turns(n - 1)
                        outs(n - 1)
                turns(15)
                outs(15)
            for t in range(PT):
                pe.wait_ge(yg, t + 1)
                pe.wait_ge(yg_c, t)
                for k in range(4):
                    ins = turn(PS[:, 6, 128 * k:128 * k + 128], MIXB[:, t, 128 * k:128 * k + 128])
                ins.then_inc(yg_t, 1)
                for k in range(4, 6):
                    ins = turn(PS[:, 7, 128 * (k - 4):128 * (k - 3)], MIXB[:, t, 128 * k:128 * k + 128])
                ins.then_inc(yg_t, 1)
            pe.wait_ge(yg_c, PT)

            def front(t, prev):
                n = t.n % 2
                pe.wait_ge(sa_qb, t.value(1, 1))
                pe.wait_ge(sa_ba, t.value(3, -3, base=START.sa_ba))
                pe.wait_ge(sa_bd, t.value(3, -3, base=START.sa_bd))
                for j in range(10):
                    pe.wait_ge(sa_fa if j % 2 == 0 else sa_fd, t.value(5, j // 2))
                    if j < 8:
                        if j % 4 == 0:
                            pe.wait_ge(sa_k[j // 4], t.value(128, 128))
                        for g in range(2):
                            for q in range(2):
                                p = 2 * j + q
                                ins = turn(PS[:, 6 + j % 2, 256 * g + 128 * q:256 * g + 128 * q + 128],
                                           SK[p // 8][:, p % 8, 128 * g:128 * g + 128])
                    else:
                        if j == 8:
                            pe.wait_ge(sa_w[n], pair_value(t, 16))
                        for p in range(4):
                            ins = turn(PS[:, 6 + j % 2, 128 * p:128 * p + 128], SWI[n][:, p, 128 * (j - 8):128 * (j - 7)])
                    ins.then_inc(sa_ft, 1)
                    if j == 1:
                        pe.wait_ge(sa_new, t.value(1, 0))
                        for g in range(2):
                            ins = mm(PS[:, 5, 0:NC], SQB[n][:, g, :],
                                     KC[:, g, bass.ds(t.at(1), 1), 0:NC].rearrange("p a n -> p (a n)"), g == 0, g == 1)
                        ins.then_inc(sa_cs, 1)
                    if j == 5:
                        pe.wait_ge(sa_cn, t.value(1, 1))
                        mm(PS[:, 5, 384:384 + NC], C("same_gt"), SPC[n][:, 0:NC]).then_inc(sa_imp, 1)

            def middle(t):
                n = t.n % 2
                pe.wait_ge(sa_fa, t.value(5, 5))
                pe.wait_ge(sa_fd, t.value(5, 5))
                pe.wait_ge(sa_mask, t.value(1, 1))
                pe.wait_ge(sa_m, t.value(2, 0, base=START.sa_m))
                pe.wait_ge(sa_p, t.value(3, 0, base=START.sa_p))
                pe.wait_ge(sa_done, t.value(1, 0, base=START.sa_done))
                for c in range(4):
                    for g in range(2):
                        mm(PS[:, c, :], SQB[n][:, g, :], SKT[:, g, 512 * c:512 * c + 512], g == 0, g == 1)
                for g in range(2):
                    mm(PS[:, 4, :], SQB[n][:, g, :], SWKT[:, g, :], g == 0, g == 1)
                for s in range(2):
                    for g in range(2):
                        ins = mm(PS[:, 5, 128 + 64 * s:192 + 64 * s], SQB[n][:, g, :], Kn[:, s, g, :], g == 0, g == 1)
                ins.then_inc(sa_s, 1)

            def back(t, fronts):
                n = t.n % 2
                sel, win, cmp = PS[:, 0, 0:256], PS[:, 0, 256:512], PS[:, 1, 0:256]
                tiles = [(SM[:, 128 * j:128 * j + 128], SV[n][:, j, :], sel, j == 0, j == NPG - 1) for j in range(NPG)]
                tiles.insert(1, (SM[:, 2048:2112], Vn[0:NS, 0, :], sel, False, False))
                tiles += [(SW[:, 128 * j:128 * j + 128], SWI[n][:, j, 256:512], win, j == 0, j == 3) for j in range(4)]
                tiles.insert(18, (SW[:, 512:576], Vn[0:NS, 1, :], win, False, False))
                tiles += [(SPC[n][:, 0:NC], VC[0:NC, bass.ds(t.at(1), 1), :].rearrange("p a c -> p (a c)"), cmp, True, True)]

                def turns(j):
                    if j < 2:
                        pe.wait_ge(sa_fa if j % 2 == 0 else sa_fd, t.value(5, 5 * fronts))
                    pe.wait_ge(sa_ba if j % 2 == 0 else sa_bd, t.value(3, j // 2, base=START.sa_ba))
                    for q, (p, _, _, _, _) in enumerate(tiles[4 * j:4 * j + 4]):
                        ins = turn(PS[0:p.shape[1], 6 + j % 2, 128 * q:128 * q + 128], p)
                    ins.then_inc(sa_bt, 1)

                pe.wait_ge(sa_p, t.value(3, 3, base=START.sa_p))
                pe.wait_ge(sa_v[n], pair_value(t, 256))
                turns(0)
                for j in range(6):
                    if j < 5:
                        turns(j + 1)
                    pe.wait_ge(sa_ba if j % 2 == 0 else sa_bd, t.value(3, j // 2 + 1, base=START.sa_ba))
                    for q, (p, v, out, first, last) in enumerate(tiles[4 * j:4 * j + 4]):
                        ins = mm(out, SPT[j % 2][0:p.shape[1], q, :], v, first, last)
                    ins.then_inc(sa_used, 1)
                pe.wait_ge(sa_mix, t.value(1, 1))
                for gp in range(2):
                    ins = turn(PS[:, 1, 128 * gp:128 * gp + 128], SO[:, 128 * gp:128 * gp + 128])
                ins.then_inc(sa_y, 1)

            pe.wait_ge(r_spread, 6)
            pe.wait_ge(pa_mix, START.pa_mix + 48)
            sample_phase(pe, front, middle, back)
            for k in range(6):
                src = P1[5][0:NS, PT, 256 + 128 * k:384 + 128 * k] if k < 2 else P1[6][0:NS, PT, 128 * (k - 2):128 * (k - 1)]
                ins = turn(PS[:, 2, 64 * k:64 * k + 64], src)
            ins.then_inc(sz_t, 1)
            pe.wait_ge(sz_done, 1)
            pe.wait_ge(ht_zero, 1)
            out_proj(HT, B_OUT1, 1)

        @block.vector
        def _(dve):
            lk = Links(dve, dve_links)
            tt, tcopy, ts = nc.vector.tensor_tensor, nc.vector.tensor_copy, nc.vector.tensor_scalar
            bc = lambda ap, n: ap.unsqueeze(len(ap.shape)).to_broadcast(list(ap.shape) + [n])

            def norm_dve(first, count, number):
                a, b = 20 + first, 20 + first + count
                dve.wait_ge(squared, first + count)
                ts(rs(a, b), rs(first, first + count), 1.0 / D, EPS, ALU.mult, ALU.add).then_inc(mean_sq, 1)
                dve.wait_ge(root, number + 1)
                nc.vector.reciprocal(rs(a, b), rs(a, b)).then_inc(rstd, 1)

            def take_h(j, outs):
                for half in range(2):
                    n = 2 * j + half
                    dve.wait_ge(h_turned, n + 1)
                    for dst, g in outs:
                        ins = tt(dst[:, 4 * half:4 * half + 4, :],
                                 PS[:, n % 4, :].rearrange("p (k c) -> p k c", k=4), bc(g[:, 4 * half:4 * half + 4], 128),
                                 ALU.mult)
                    ins.then_inc(h_taken, 1)

            nc.vector.memset(X[NS:128, PT, :], 0.0).then_inc(x_zero, 1)
            dve.wait_ge(const_in, 48)
            norm_dve(0, 7, 0)
            for j in range(7):
                if j < 2:
                    take_h(j, [(memT[l][:, :, 128 * j:128 * j + 128], S("g_mem")[:, 8 * l:8 * l + 8]) for l in range(2)])
                else:
                    take_h(j, [(HT[:, :, 128 * (j - 2):128 * (j - 1)], S("g_x")[:, 0:8])])
            def page_prod0(t, first, last):
                for p in range(first, last):
                    dve.wait_ge(cp_in[p % 8], t.value(32, 16 * (p // 8 + 1)))
                    dve.wait_ge(cp_sum, t.value(NPG, p - 3, base=START.cp_sum))
                    tt(CPA[p % 4], PG[p % 8], S("pos0"), ALU.mult).then_inc(cp_a, 1)



            dve.wait_ge(pad_zero, 3)
            dve.wait_ge(product, PBASE[B_C0])
            with dve.Fori(0, CT // 2) as i:
                lk.enter(i, 2 * 10)
                for n in range(2):
                    t = Turn(i, n, 2)
                    Up, Us = U[n][:, 0:514], U[n][:, 514:594].rearrange("p (b c) -> p b c", b=NB)
                    Yp, Ys = Y[:, 0:512], Y[:, 512:576].rearrange("p (b c) -> p b c", b=NB)
                    sb = Sb.rearrange("p (q b c) -> p q b c", q=4, b=NB)
                    wj = lambda j: small[:, bass.ds(t.at(3, SMALL["conv_w"][0] + j), 1)]
                    page_prod0(t, 0, 12)
                    dve.wait_ge(product, t.value(4, 2, base=PBASE[B_CONV]))
                    dve.wait_ge(c_copied, t.value(1, 1, base=START.c_copied))
                    dve.wait_ge(state_set, t.value(1, 1))
                    dve.wait_ge(state_kept, t.value(2, -2, base=START.state_kept))
                    tt(Up[:, 2:514], Cb[:, 0:512], PS[:, 1, :], ALU.mult).then_inc(u_made, 1)
                    dve.wait_ge(u_made, t.value(2, 1, base=START.u_made))
                    lk.link(ts(Yp, Up[:, 0:512], wj(0), None, ALU.mult))
                    for j in (1, 2):
                        lk.link(nc.vector.scalar_tensor_tensor(Yp, Up[:, j:j + 512], wj(j), Yp, ALU.mult, ALU.add))
                    page_prod0(t, 12, NPG)
                    dve.wait_ge(product, t.value(4, 3, base=PBASE[B_CONV]))
                    tt(Yp, Yp, PS[:, 2, :], ALU.mult).then_inc(b_used, 1)

                    dve.wait_ge(s_copied, t.value(1, 1, base=START.s_copied))
                    tt(Us[:, :, 2:10], sb[:, 0], sb[:, 1], ALU.mult).then_inc(u_made, 1)
                    dve.wait_ge(u_made, t.value(2, 2, base=START.u_made))
                    lk.link(ts(Ys, Us[:, :, 0:8], wj(0), None, ALU.mult))
                    for j in (1, 2):
                        lk.link(nc.vector.scalar_tensor_tensor(Ys, Us[:, :, j:j + 8], wj(j), Ys, ALU.mult, ALU.add))
                    lk.did(tt(Ys, Ys, sb[:, 2], ALU.mult))
                    dve.wait_ge(z_exp, t.value(1, 1))
                    lk.link(ts(E, E, 1.0, None, ALU.add))
                    lk.link(nc.vector.reciprocal(E, E))
                    lk.did(tt(E[:, 0:512], E[:, 0:512], PS[:, 3, :], ALU.mult))
                    tt(E[:, 512:576], E[:, 512:576], Sb[:, 192:256], ALU.mult).then_inc(z_used, 1)
                    dve.wait_ge(z_used, t.value(1, 1, base=START.z_used))
                    dve.wait_ge(b_used, t.value(1, 1, base=START.b_used))
                    lk.settle()
                    tt(YT0f[:, bass.ds(t.at(TOK, 2 * TOK), 576)], Y, E, ALU.mult).then_inc(conv_y, 1)
                lk.leave(CT // 2)

            def mem_prompt_dve(l):
                b_ = mem_bufs(l)
                P0 = MQG0 if l == 0 else P1[0]
                dve.wait_ge(sig_exp, l + 1)
                lk.link(ts(b_["MG"], b_["MG"], 1.0, None, ALU.add))
                lk.link(nc.vector.reciprocal(b_["MG"], b_["MG"]))
                lk.link(tt(P0[:, :, 256:512], P0[:, :, 256:512], b_["MG"], ALU.mult))
                for n in range(PT):
                    T = l * PT + n
                    pr = n % 2
                    if n:
                        dve.wait_ge(ma_qt, T)
                    ts(b_["QS"], P0[:, n, 0:256], SCALE, None, ALU.mult).then_inc(ma_q, 1)
                    dve.wait_ge(ma_s, T + 1)
                    for k in range(2):
                        nc.vector.tensor_reduce(stats[:, 60 + 8 * pr + k:63 + 8 * pr + k:2],
                                                PS[:, 2 * pr + k, :].rearrange("p (h m) -> p h m", h=2), AX, ALU.max,
                                                negate=True).then_inc(ma_m, 1)
                    dve.wait_ge(ma_t, 2 * T + 1)
                    if T:
                        dve.wait_ge(ma_o, T)
                    tcopy(b_["PT"][:, 0:512], PS[:, 6, :]).then_inc(ma_td, 1)
                    dve.wait_ge(ma_p, 4 * (T + 1))
                    lk.link(nc.vector.reciprocal(rs(92, 96), rs(76 + 8 * pr, 80 + 8 * pr)))
                    dve.wait_ge(ma_o, T + 1)
                    if n:
                        dve.wait_ge(ma_yt, T)
                    OY = b_["OY"].rearrange("p (h c) -> p h c", h=4)
                    lk.link(tt(OY, PS[:, 4, 256 * pr:256 * pr + 256].rearrange("p (h c) -> p h c", h=4),
                               bc(rs(92, 96), 64), ALU.mult))
                    tt(b_["OY"], b_["OY"], P0[:, n, 256:512], ALU.mult).then_inc(ma_y, 1)

            def mem_sample_dve(l, YT):
                b_ = mem_bufs(l)
                YTf = HTf if l else YT0f
                P0 = MQG0 if l == 0 else P1[0]
                dve.wait_ge(ma_qt, PT * (l + 1))
                ts(b_["QS"], P0[:, PT, 0:256], SCALE, None, ALU.mult).then_inc(ms_q, 1)
                dve.wait_ge(ms_qt, l + 1)
                dve.wait_ge(ms_qz, 5 * l + 1)
                for h in range(4):
                    o = 64 * (h % 2)
                    tcopy(b_["QZ"][o:o + 64, h // 2, :, 32 * h:32 * h + 8],
                          PS[o:o + 64, 5, 128 * (h // 2):128 * (h // 2) + 64].rearrange("p (b t) -> p b t", b=NB)
                          ).then_inc(ms_qz, 1)
                with dve.Fori(0, NB // 2) as i:
                    lk.enter(i, 2 * 4)
                    for n in range(2):
                        t = Turn(i, n, 2)
                        v = lambda plus: t.value(1, plus, base=NB * l)
                        dve.wait_ge(ms_s, v(START.ms_s + 1))
                        nc.vector.tensor_reduce(rs(100 + n, 101 + n), PS[:, n, 0:256], AX, ALU.max, negate=True
                                                ).then_inc(ms_m, 1)
                        dve.wait_ge(ms_t, v(1))
                        tcopy(b_["SPT"][n], PS[:, 7, 0:256]).then_inc(ms_c, 1)
                        dve.wait_ge(ms_p, v(1))
                        lk.link(nc.vector.reciprocal(rs(108 + n, 109 + n), rs(104 + n, 105 + n)))
                        dve.wait_ge(ms_o, v(START.ms_o + 1))
                        dve.wait_ge(ms_y, v(START.ms_y - 1))
                        ts(b_["SO"][n], PS[:, 2 + n, 0:256], rs(108 + n, 109 + n), None, ALU.mult).then_inc(ms_n, 1)
                        dve.wait_ge(ms_y, v(START.ms_y + 1))
                        for h in range(4):
                            o, g = 64 * (h % 2), h // 2
                            ins = tcopy(YTf[o:o + 64, bass.ds(t.at(NT, g * TOK + SEQ), NT)],
                                        PS[o:o + 64, 4, 128 * g + 32 * h:128 * g + 32 * h + NT])
                            if h < 3:
                                lk.did(ins)
                        ins.then_inc(ms_done, 1)
                    lk.leave(NB // 2)
                lk.settle()
                dve.wait_ge(ms_g, l + 1)
                dve.wait_ge(ms_done, START.ms_done + NB * (l + 1))
                tt(YT[:, 0:2, SEQ:SEQ + NS], YT[:, 0:2, SEQ:SEQ + NS],
                   PS[:, 5, 0:256].rearrange("p (g c) -> p g c", g=2)[:, :, 0:NS], ALU.mult).then_inc(ms_gm, 1)

            def add_out(first, l):
                for n in range(2):
                    pages = Turn(0, CT + n, 1)
                    for t in range(TT):
                        if l == 0 and t < PT:
                            page_prod0(pages, 4 * t, 4 * t + 4)

                        dve.wait_ge(product, PBASE[first + n] + t + 1)
                        xs = X[:, t, 512 * n:512 * n + 512]
                        tt(xs, xs, PS[:, t, :], ALU.add).then_inc(out_added, 1)

            mem_prompt_dve(0)
            mem_sample_dve(0, YT0)
            add_out(B_OUT0, 0)
            norm_dve(7, TT, 1)
            for j in range(TT):
                take_h(7 + j, [(HT[:, :, 128 * j:128 * j + 128], S("g_x")[:, 8:16])])
            Z5 = sig[:, 0:1280].rearrange("p (t c) -> p t c", t=TT)
            Z6 = sig[:, 1280:3840].rearrange("p (t c) -> p t c", t=TT)
            dve.wait_ge(gates_taken, 1)
            lk.link(ts(Gate, Gate, 1.0, None, ALU.add))
            nc.vector.reciprocal(Gate, Gate).then_inc(sig_done, 1)
            for n, (z, dst) in enumerate(((Z5, P1[5][:, :, 256:512]), (Z6, P1[6][:, :, :]))):
                dve.wait_ge(z_exp, CT + n + 1)
                lk.link(ts(z, z, 1.0, None, ALU.add))
                lk.link(nc.vector.reciprocal(z, z))
                tt(dst, dst, z, ALU.mult).then_inc(sig_done, 1)
            def rope(c, h0, nh):
                v = P1[c][:, :, 64 * h0:64 * (h0 + nh)].rearrange("p t (h d) -> p t h d", h=nh)
                x1, x2 = v[:, :, :, 0:8], v[:, :, :, 8:16]
                cs, sn = [C(k).rearrange("p (t d) -> p t d", t=TT).unsqueeze(2).to_broadcast([128, TT, nh, 8])
                          for k in ("cos", "sin")]
                tmp = [r[:, 0:TT * nh * 8].rearrange("p (t h d) -> p t h d", t=TT, h=nh) for r in rope_t]
                lk.did(tt(tmp[0], x1, cs, ALU.mult))
                lk.did(tt(tmp[1], x2, sn, ALU.mult))
                lk.did(tt(tmp[2], x2, cs, ALU.mult))
                lk.link(tt(tmp[3], x1, sn, ALU.mult))
                lk.did(tt(x1, tmp[0], tmp[1], ALU.subtract))
                lk.link(tt(x2, tmp[2], tmp[3], ALU.add))

            mem_prompt_dve(1)
            mem_sample_dve(1, HT)
            for c, h0, nh in ((1, 0, 8), (2, 0, 8), (3, 4, 4), (4, 4, 4)):
                rope(c, h0, nh)
            for s in range(2):
                ins = tcopy(Vn[0:NS, s, :], P1[4 + s][0:NS, PT, 0:256])
                if s == 0:
                    lk.did(ins)
                else:
                    ins.then_inc(roped, 4)
            dve.wait_ge(qz_zero, 2)
            dve.wait_ge(r_turned, 11)
            for g in range(KVH):
                o, gp = 64 * (g % 2), g // 2
                for r in range(GRP):
                    ins = ts(QZ[o:o + 64, gp, :, 32 * g + 8 * r:32 * g + 8 * r + 8],
                             PS[o:o + 64, 6, 64 * (2 * r + gp):64 * (2 * r + gp) + 64].rearrange("p (b t) -> p b t", b=NB),
                             SCALE, None, ALU.mult)
                ins.then_inc(r_spread, 1)
            dve.wait_ge(r_turned, 12)
            tcopy(Kn.rearrange("p s g n -> p (s g n)"), PS[:, 7, 0:256]).then_inc(r_spread, 2)
            for p in range(PT):
                if p >= 2:
                    dve.wait_ge(cp_sum, NB * NPG + START.cp_sum + p - 1)
                tt(PA[p % 2][:, 0:256], P1[2][:, p, 256:512], S("pos0")[:, 0:256], ALU.mult)
                tt(PA[p % 2][:, 256:512], P1[3][:, p, 0:256], S("pos0")[:, 256:512], ALU.mult).then_inc(cp_a, 1)


            dve.wait_ge(cp_sum, PT + NB * NPG + START.cp_sum)
            dve.wait_ge(r_took, 10)
            stt = nc.vector.scalar_tensor_tensor
            with dve.Fori(0, GRP) as r:
                lk.enter(r, 16 * 8)
                dve.wait_ge(pa_s, START.pa_s + r * 16)
                tcopy(Qs[0].rearrange("p g c -> p (g c)"), QTf[:, bass.ds(r * 1024, 1024)]).then_inc(pa_q, 1)

                def maxes(n):
                    t = Turn(r, n, 16)
                    ti, pr = n % PT, n % 2
                    nk = 128 * (ti + 1)
                    dve.wait_ge(pa_s, t.value(1, 1, base=START.pa_s))
                    c = PS[:, 4, 0:NCP]
                    lk.did(tt(c, c, C("cmp_add")[:, 32 * ti:32 * ti + NCP], ALU.add))
                    for s in range(2):
                        d = PS[:, 2 * pr + s, 128 * ti:128 * ti + 128]
                        lk.did(tt(d, d, C("causal"), ALU.add))
                    lk.settle()
                    for s, src in enumerate((c, PS[:, 2 * pr, 0:nk], PS[:, 2 * pr + 1, 0:nk])):
                        nc.vector.tensor_reduce(rs(120 + s + 4 * pr, 121 + s + 4 * pr), src, AX, ALU.max, negate=True
                                                ).then_inc(pa_m, 1)

                def cmp_mask(n):
                    t = Turn(r, n, 16)
                    ti, pr = n % PT, n % 2
                    dve.wait_ge(pa_p, t.value(3, 1, base=START.pa_p))
                    c = PP[pr][:, 1024:1024 + NCP]
                    nc.vector.tensor_tensor_reduce(c, c, C("cmp_mul")[:, 32 * ti:32 * ti + NCP], 1.0, 0.0, ALU.mult,
                                                   ALU.add, rs(128 + 4 * pr, 129 + 4 * pr)).then_inc(pa_cm, 1)

                def mix(n):
                    t = Turn(r, n, 16)
                    g, ti, pr = n // PT, n % PT, n % 2
                    nk = 128 * (ti + 1)
                    dve.wait_ge(pa_t, t.value(3, 2, base=START.pa_t))
                    dve.wait_ge(pa_o, t.value(1, 0, base=START.pa_o))
                    tcopy(PTt[:, 0:nk], PS[:, 6, 0:nk]).then_inc(pa_ts, 1)
                    dve.wait_ge(pa_p, t.value(3, 3, base=START.pa_p))
                    dve.wait_ge(pa_cm, t.value(1, 1))
                    lk.link(ts(rs(160, 163), rs(128 + 4 * pr, 131 + 4 * pr), 1e-30, None, ALU.max))
                    lk.link(nc.vector.reciprocal(rs(160, 163), rs(160, 163)))
                    gate = Gate[:, ti, :].rearrange("p (s h) -> p s h", s=3)[:, :, bass.ds(r * KVH + g, 1)]
                    lk.link(tt(rs(164, 167), rs(160, 163), gate.squeeze(2), ALU.mult))
                    dve.wait_ge(pa_o, t.value(1, 1, base=START.pa_o))
                    o = 128
                    lk.link(ts(Om[:, 0:64], PS[:, 5, o:o + 64], rs(164, 165), None, ALU.mult))
                    lk.link(stt(Om[:, 64:128], PS[:, 5, o + 64:o + 128], rs(165, 166), Om[:, 0:64], ALU.mult, ALU.add))
                    stt(MIXf[:, bass.ds(r * 256 + (MIX * ti + 64 * g), 64)], PS[:, 5, o + 128:o + 192], rs(166, 167),
                        Om[:, 64:128], ALU.mult, ALU.add).then_inc(pa_mix, 1)

                for n in range(16):
                    maxes(n)
                    if n:
                        mix(n - 1)
                    cmp_mask(n)
                mix(15)
                lk.leave(GRP)
            dve.wait_ge(pa_mix, START.pa_mix + 48)
            for t in range(PT):
                lk.did(tt(MIXB[:, t, 0:256], MIXB[:, t, 0:256], P1[5][:, t, 256:512], ALU.mult))
                tt(MIXB[:, t, 256:768], MIXB[:, t, 256:768], P1[6][:, t, :], ALU.mult).then_inc(yg, 1)

            def front(t, prev):
                n = t.n % 2
                def took(j):
                    dve.wait_ge(sa_ft, t.value(10, j + 1, base=START.sa_ft))
                    if j < 8:
                        tcopy(SKT[:, :, 256 * j:256 * j + 256], PS[:, 7, :].rearrange("p (g c) -> p g c", g=2)
                              ).then_inc(sa_fd, 1)
                    else:
                        tcopy(SWKT[:, 1, :], PS[:, 7, :]).then_inc(sa_fd, 1)

                took(1)
                dve.wait_ge(sa_cs, t.value(1, 1))
                nc.vector.tensor_reduce(rs(140, 141), PS[:, 5, 0:NC], AX, ALU.max, negate=True).then_inc(sa_cm, 1)
                took(3)
                dve.wait_ge(sa_ce, t.value(1, 1))
                lk.link(ts(rs(155, 156), rs(141, 142), 1e-30, None, ALU.max))
                lk.link(nc.vector.reciprocal(rs(155, 156), rs(155, 156)))
                ts(SPC[n][:, 0:NC], SPC[n][:, 0:NC], rs(155, 156), None, ALU.mult).then_inc(sa_cn, 1)
                took(5)
                dve.wait_ge(sa_imp, t.value(1, 1))
                lk.link(tcopy(SIMP[:, 1:1 + NC], PS[:, 5, 384:384 + NC]))
                lk.link(tt(SCH, SIMP[:, 1:129], SIMP[:, 0:128], ALU.add))
                lk.link(nc.vector.tensor_reduce(SSC[:, 0:NSB - 1], SCH.rearrange("p (n c) -> p n c", c=4), AX, ALU.add))
                lk.link(tt(SS2[:, 0:NSB], SSC[:, 0:NSB], C("forced")[:, 0:NSB], ALU.add))
                for k in range(2):
                    step_dve()
                    lk.link(nc.vector.max(SM8, SS2[:, 0:NSB]))
                    step_dve()
                    lk.link(nc.vector.match_replace(SS2[:, 0:NSB], SM8, SS2[:, 0:NSB], -1.0))
                ts(SMB[:, 0:NSB], SS2[:, 0:NSB], 0.0, NEG, ALU.is_ge, ALU.mult).then_inc(sa_mask, 1)
                took(7)
                took(9)

            def middle(t):
                lk.settle()
                dve.wait_ge(sa_mask, t.value(1, 1))
                dve.wait_ge(sa_s, t.value(1, 1, base=START.sa_s))
                dve.wait_ge(sa_bt, t.value(6, 0, base=START.sa_bt))
                ttr = nc.vector.tensor_tensor_reduce
                lk.did(tcopy(SNM, cst[:, bass.ds(t.at(-NT, CONST["new_add"][0] + NT * (NB - 1)), 64)]))
                lk.link(tt(PS[:, 4, 0:8], PS[:, 4, 0:8], C("win_add"), ALU.add))
                step_dve()
                lk.did(ttr(SM[:, 2048:2112], PS[:, 5, 128:192], SNM, 1.0, -3e38, ALU.add, ALU.max, rs(146, 147)))
                ttr(SW[:, 512:576], PS[:, 5, 192:256], SNM, 1.0, -3e38, ALU.add, ALU.max, rs(148, 149)).then_inc(sa_new, 1)
                for c in range(4):
                    lk.did(ttr(SM[:, 512 * c:512 * c + 512].rearrange("p (n k) -> p n k", k=SB),
                               PS[:, c, :].rearrange("p (n k) -> p n k", k=SB), bc(SMB[:, 8 * c:8 * c + 8], SB), 1.0, -3e38,
                               ALU.add, ALU.max, rs(142 + c, 143 + c)))
                dve.wait_ge(sa_new, t.value(1, 1))
                lk.link(nc.vector.tensor_reduce(rs(147, 148), PS[:, 4, :], AX, ALU.max))
                nc.vector.tensor_reduce(rs(150, 151), rs(142, 147), AX, ALU.max, negate=True).then_inc(sa_m, 1)
                nc.vector.tensor_reduce(rs(151, 152), rs(147, 149), AX, ALU.max, negate=True).then_inc(sa_m, 1)

            def back(t, fronts):
                for j in range(1, 6, 2):
                    dve.wait_ge(sa_bt, t.value(6, j + 1, base=START.sa_bt))
                    dve.wait_ge(sa_used, t.value(6, j - 1, base=START.sa_used))
                    k = 4 if j < 5 else 3
                    tcopy(SPT[1][:, 0:k, :], PS[:, 7, 0:128 * k].rearrange("p (s c) -> p s c", s=k)).then_inc(sa_bd, 1)
                dve.wait_ge(sa_p, t.value(3, 3, base=START.sa_p))
                lk.link(tt(rs(153, 154), rs(153, 154), rs(154, 155), ALU.add))
                lk.link(ts(rs(156, 158), rs(152, 154), 1e-30, None, ALU.max))
                lk.link(nc.vector.reciprocal(rs(156, 158), rs(156, 158)))
                gr = Grow[:, bass.ds(t.at(1), 1), :].squeeze(1)
                lk.did(tcopy(rs(170, 173), gr))
                lk.link(tt(rs(158, 160), rs(156, 158), gr[:, 1:3], ALU.mult))
                dve.wait_ge(sa_used, t.value(6, 6, base=START.sa_used))
                dve.wait_ge(sa_y, t.value(1, 0, base=START.sa_y))
                lk.link(ts(SO, PS[:, 1, 0:256], rs(170, 171), None, ALU.mult))
                lk.link(stt(SO, PS[:, 0, 0:256], rs(158, 159), SO, ALU.mult, ALU.add))
                stt(SO, PS[:, 0, 256:512], rs(159, 160), SO, ALU.mult, ALU.add).then_inc(sa_mix, 1)
                dve.wait_ge(sa_y, t.value(1, 1, base=START.sa_y))
                for g in range(KVH):
                    o, gp = 64 * (g % 2), g // 2
                    ins = tcopy(HT[o:o + 64, 2 + gp:7 + gp:2, bass.ds(t.at(NT, SEQ), NT)],
                                PS[o:o + 64, 1, 128 * gp + 32 * g:128 * gp + 32 * g + 24].rearrange("p (r t) -> p r t", r=GRP))
                    if g < 3:
                        lk.did(ins)
                ins.then_inc(sa_done, 1)

            dve.wait_ge(kv_stored, 16 * (2 * 3 + 2 * 2 + 2 * NB))
            dve.wait_ge(gates_back, 16 * 36)
            dve.wait_ge(yg_c, PT)
            lk.did(nc.vector.memset(SIMP, 0.0))
            lk.link(nc.vector.memset(SSC, 0.0))
            sample_phase(dve, front, middle, back, lk)
            dve.wait_ge(sz_t, 1)
            dve.wait_ge(sa_done, START.sa_done + NB)
            tt(HT[:, 2:8, SEQ:SEQ + NS], HT[:, 2:8, SEQ:SEQ + NS], PS[:, 2, 0:384].rearrange("p (k c) -> p k c", k=6),
               ALU.mult).then_inc(sz_done, 1)
            add_out(B_OUT1, 1)
            norm_dve(12, TT, 2)
            dve.wait_ge(gfin_in, 16)
            for t in range(TT):
                dve.wait_ge(fin_scaled, t + 1)
                if t >= 2:
                    dve.wait_ge(y_out[t % 2], 16 * (t // 2))
                tt(fin[t % 2], H[t % 2], gfin, ALU.mult).then_inc(y_ready, 1)


def w_count(n):
    return 16 * (n // 2 + 1)


def pair_value(t, each):
    return t.i * each + (t.n // 2 + 1) * each


def constants():
    c = np.zeros((128, CONST_W), np.float32)
    p = np.arange(128)

    def put(name, v):
        a, w = CONST[name]
        c[:, a:a + w] = v

    put("ident", np.eye(128))
    put("causal", np.where(p[None, :] <= p[:, None], 0.0, NEG))
    q_pos = p[:, None, None] + 128 * np.arange(PT)[None, :, None]
    seen = (16 * np.arange(32)[None, None, :] + 31 <= q_pos).reshape(128, 128)
    put("cmp_add", np.where(seen, 0.0, NEG))
    put("cmp_mul", seen)
    real = p % 32 < 24
    put("same_gt", (p[:, None] // 32 == p[None, :] // 32) & (p[:, None] % 8 == p[None, :] % 8) & real[:, None] & real[None, :])
    new = np.full((128, 15, 8), NEG)
    new[:, NB - 1, :] = np.where(np.arange(8)[None, :] <= p[:, None] % 8, 0.0, NEG)
    put("new_add", new.reshape(128, 120))
    put("win_add", np.where(np.arange(8)[None, :] <= p[:, None] % 8, NEG, 0.0))
    put("chunk", p[:, None] // 16 + 120 == np.arange(250)[None, :])
    pos = (p[:, None] + 128 * np.arange(TT)[None, :]).astype(np.float32)
    pos[:, PT] = PAST + p % NT
    inv = (np.float32(500000.0) ** (-np.arange(8, dtype=np.float32) * np.float32(2.0) / np.float32(16))).astype(np.float32)
    ang = (pos[:, :, None] * inv).astype(np.float32)
    put("cos", np.cos(ang).reshape(128, 40))
    put("sin", np.sin(ang).reshape(128, 40))
    forced = np.zeros(NSB + 1)
    forced[[0, NSB - 2, NSB - 1]] = 1e4
    put("forced", forced)
    return c


def lay_out(x):
    f = {k: np.asarray(v) for k, v in x.items()}
    out = {"xp": f["x_prompt"][0], "xs": f["x_sample"].reshape(NS, D), "mem": f["mem_prompt"][0],
           "cmem": f["cache_mem_kv"].reshape(2, NB, NMEM, 512), "ccmp": f["cache_cmp_kv"].reshape(POOL, PAGE, 512),
           "csel": f["cache_sel_kv"].reshape(POOL, PAGE, 512), "pages": f["page_table"].reshape(1, NB * NPG),
           "win": f["state_win_kv"].reshape(NB, WIN, 512), "const": constants()}

    def rgd(a, axis):
        sh = a.shape
        a = a.reshape(sh[:axis] + (KVH, GRP, sh[axis] // 12) + sh[axis + 1:])
        return np.swapaxes(a, axis, axis + 1).reshape(sh)

    wc, wn, wo = f["w_in_conv"][0], f["w_in_nsa"][0], f["w_out"]
    blocks = [f["w_mem_kv"][0], f["w_mem_kv"][1], wc[:, 0:512]]
    for i in range(CT):
        blocks.append(np.concatenate([wc[:, 512 + MIX * q + 128 * i:640 + MIX * q + 128 * i] for q in (1, 2, 0, 3)], 1))
    blocks += [wo[0][:, 0:512], wo[0][:, 512:1024]]
    q, kv, gl, z = wn[:, 512:1280], wn[:, 1280:2816], wn[:, 2816:2852], wn[:, 2852:3620]
    n = np.concatenate([wn[:, 0:512], rgd(q, 1), kv, rgd(z, 1)], 1)
    blocks += [n[:, 512 * c:512 * c + 512] for c in range(7)]
    w1 = np.concatenate([wo[1][0:256], rgd(wo[1][256:], 0)], 0)
    blocks += [w1[:, 0:512], w1[:, 512:1024]]
    out["wall"] = np.stack([b.reshape(KD, 128, 512).transpose(1, 0, 2).reshape(128, KD * 512) for b in blocks])
    g = gl.reshape(D, 3, KVH, GRP).swapaxes(2, 3).reshape(KD, 128, 36)
    out["wg"] = g.transpose(1, 0, 2).reshape(128, KD * 36)
    parts = {
        "g_mem": f["mem_norm_g"].reshape(2, KD, 128).transpose(2, 0, 1).reshape(128, 16),
        "g_x": f["norm_g"].reshape(2, KD, 128).transpose(2, 0, 1).reshape(128, 16),
        "conv_w": f["conv_w"][0].reshape(3, CT, 128).transpose(2, 1, 0).reshape(128, 18),
        "state": f["state_conv"][0].reshape(NB, 2, CT, 128).transpose(3, 2, 0, 1).reshape(128, CT * 16),
    }
    pos = f["cmp_pos_w"][0].reshape(2, 2, 16, HD)
    for m in range(2):
        w = np.repeat(pos[:, m].transpose(1, 0, 2)[:, :, None, :], KVH, 2).reshape(16, 512)
        parts[f"pos{m}"] = np.tile(w, (8, 1))
    for s, name in enumerate(("phi_k", "phi_v")):
        d = np.zeros((128, 128), np.float32)
        for k in range(2):
            d[64 * k:64 * k + 64, 64 * k:64 * k + 64] = f["cmp_phi"][0, s]
        parts[name] = d
    out["small"] = np.concatenate([parts[k] for k in SMALL], 1)
    out["gfin"] = np.broadcast_to(f["final_norm_g"][None, :], (128, D))
    return {k: np.ascontiguousarray(v) for k, v in out.items()}


OUTS = {"yp": (SEQ, D), "ys": (NS, D), "conv": (128, CT * 18), "cmp_p": (SEQ, 512), "sel_p": (SEQ, 512),
        "win_p": (SEQ, 512), "mem": (2, NMEM, 512), "cmp_s": (NS, 512), "sel_s": (NS, 512), "win_s": (NB, WIN, 512)}


def kernel(**inputs):
    import concourse.bacc as bacc
    from concourse.bass_utils import run_bass_kernel_spmd

    arrays = {"in_" + k: v for k, v in lay_out(inputs).items()}
    nc = bacc.Bacc("TRN2", target_bir_lowering=False, num_devices=1)
    I = {k[3:]: nc.dram_tensor(k, v.shape, I32 if v.dtype == np.int32 else F32, kind="ExternalInput").ap()
         for k, v in arrays.items()}
    O = {k: nc.dram_tensor("out_" + k, s, F32, kind="ExternalOutput").ap() for k, s in OUTS.items()}
    build(nc, I, O)
    r = run_bass_kernel_spmd(nc, [arrays], core_ids=[0]).results[0]
    r = {k: r["out_" + k] for k in OUTS}
    conv = r["conv"].reshape(128, CT, 18)
    kv = lambda a, *s: a.reshape(*s, 2, KVH, HD)
    conv_p = conv[:, :, 0:2].transpose(2, 1, 0).reshape(1, 1, 2, MIX)
    conv_s = conv[:, :, 2:18].reshape(128, CT, NB, 2).transpose(2, 3, 1, 0).reshape(1, NB, 2, MIX)
    return (r["yp"].reshape(1, SEQ, D), r["ys"].reshape(NB, NT, D), conv_p,
            kv(r["cmp_p"], 1, 1, SEQ), kv(r["sel_p"], 1, 1, SEQ), kv(r["win_p"], 1, 1, SEQ),
            r["mem"].reshape(2, 1, NMEM, 2, 4, HD), conv_s,
            kv(r["cmp_s"], 1, NB, NT), kv(r["sel_s"], 1, NB, NT), kv(r["win_s"], 1, NB, WIN))
```

```python
from contextlib import ExitStack

import numpy as np
import concourse.bass as bass
from concourse import mybir

F32 = mybir.dt.float32
I32 = mybir.dt.int32
ALU = mybir.AluOpType
ACT = mybir.ActivationFunctionType
AX = mybir.AxisListType.X

D = 1024
KD = D // 128
SEQ = 512
NB, NT = 8, 8
NS = NB * NT
PT = SEQ // 128
TT = PT + 1
TOK = TT * 128
PAST = 2048
PAGE = 128
NPG = PAST // PAGE
TILE = 4
NTL = NPG // TILE
POOL = 160
HD = 64
MIX = 768
CT = MIX // 128
NMEM = 256
KVH = 4
GRP = 3
SB = 64
NSB = PAST // SB + 1
NC = PAST // 16 - 1
NCP = SEQ // 16 - 1
WIN = 512
NEG = -1e30
SCALE = HD ** -0.5
ARENA = 53080


class START:
    cp_a = 3
    cp_b = 3
    cp_ra = 1
    cp_rb = 1
    cp_sum = 3
    conv_y = 2
    ms_s = 2
    u_made = 1
    pa_t = 6
    pa_o = 1
    sa_bt = 7
    c_copied = 1
    s_copied = 1
    b_used = 1
    z_used = 1
    ms_kc = 1
    ms_c = 1
    ms_done = 1
    cp_rows = 1
    cp_cols = 1
    cp_took = 1
    pa_p = 4
    pa_mix = 1
    pa_ta = 1
    pa_td = 1
    sa_ba = 4
    sa_bd = 4
    sa_m = 1
    sa_p = 1
    sa_done = 1
    state_kept = 3
    ms_y = 2
    sa_y = 1
    pa_s = 1
    sa_used = 7
    sa_ft = 7
    sa_s = 2
    ms_o = 2


LINKS_OF_TURN = 28
EPS = 1e-6

CONST = {}
CONST_W = 0
for _n, _w in [("ident", 128), ("causal", 128), ("cmp_add", 128), ("cmp_mul", 128), ("same_gt", 128),
               ("new_add", 120), ("win_add", 8), ("chunk", 58), ("chunk4", 226), ("cos", 40), ("sin", 40),
               ("forced", NSB + 1)]:
    CONST[_n] = (CONST_W, _w)
    CONST_W += _w
SMALL = {}
SMALL_W = 0
for _n, _w in [("g_mem", 16), ("g_x", 16), ("conv_w", CT * 3), ("state", CT * 16), ("pos0", 128), ("pos1", 128),
               ("tile_pos0", 512), ("tile_pos1", 512),
               ("phi_k", 128), ("phi_v", 128)]:
    SMALL[_n] = (SMALL_W, _w)
    SMALL_W += _w

B_KV, B_C0, B_CONV, B_OUT0, B_N, B_OUT1 = 0, 2, 3, 9, 11, 18
NBLK = 20
TILES_OF = [2, 2, 5] + [4] * CT + [5, 5] + [5] * 7 + [5, 5]
PBASE = [sum(TILES_OF[:n]) + (5 if n >= B_OUT1 else 0) for n in range(NBLK + 1)]
P_GATES = sum(TILES_OF[:B_OUT1])


class Turn:

    def __init__(self, i, n, per):
        self.i, self.n, self.per = i, n, per

    def value(self, each, plus, base=0):
        rest = base + each * self.n + plus
        if isinstance(self.i, int):
            return self.i * self.per * each + rest
        assert rest > 0
        return self.i * (self.per * each) + rest

    def at(self, stride, plus=0):
        return self.i * (self.per * stride) + (self.n * stride + plus)


class Links:

    def __init__(self, eng, sem):
        self.eng, self.sem, self.n, self.i, self.per = eng, sem, 0, None, 0

    def did(self, ins):
        ins.then_inc(self.sem, 1)
        self.n += 1

    def settle(self):
        self.eng.wait_ge(self.sem, self.n if self.i is None else self.i * self.per + self.n)

    def link(self, ins):
        self.did(ins)
        self.settle()

    def enter(self, i, per):
        self.i, self.per, self.start = i, per, self.n

    def leave(self, trips):
        assert self.n - self.start == self.per, (self.n - self.start, self.per)
        self.i, self.n = None, self.start + trips * self.per


def build(nc, I, O):
    ctx = ExitStack()
    with ctx:
        def sem(name):
            return ctx.enter_context(nc.semaphore(name))

        arena = ctx.enter_context(nc.sbuf_tensor("arena", [128, ARENA], F32))
        ptab = ctx.enter_context(nc.sbuf_tensor("ptab", [1, NB * NPG], I32))
        PS = ctx.enter_context(nc.psum_tensor("PS", [128, 8, 512], F32))
        gates_dram = nc.dram_tensor("gates_scratch", [NS, 36], F32, kind="Internal").ap()

        top = [0]

        def keep(n):
            a = arena[:, top[0]:top[0] + n]
            top[0] += n
            return a

        X = keep(TT * D).rearrange("p (t c) -> p t c", t=TT)
        HT = keep(KD * TOK).rearrange("p (k c) -> p k c", k=KD)
        KC = keep(2 * NB * 128).rearrange("p (g b n) -> p g b n", g=2, b=NB)
        VC = keep(NB * 256).rearrange("p (b c) -> p b c", b=NB)
        KCp = keep(64).rearrange("p (g n) -> p g n", g=2)
        VCp = keep(256)
        cst = keep(CONST_W)
        small = keep(SMALL_W)
        stats = keep(400)
        Kn = keep(256).rearrange("p (s g n) -> p s g n", s=2, g=2)
        Vn = keep(512).rearrange("p (s c) -> p s c", s=2)
        Gate = keep(TT * 36).rearrange("p (t c) -> p t c", t=TT)
        Grow = keep(NB * 3).rearrange("p (b c) -> p b c", b=NB)
        CS = keep(CT * 18)
        QZ = keep(2 * NB * 128).rearrange("p (g b m) -> p g b m", g=2, b=NB)
        base = top[0]

        def at(off, n):
            assert base + off + n <= ARENA, (base, off, n)
            return arena[:, base + off:base + off + n]

        def C(name):
            a, w = CONST[name]
            return cst[:, a:a + w]

        def S(name):
            a, w = SMALL[name]
            return small[:, a:a + w]

        ident = C("ident")
        W = [at(4096 * n, 4096).rearrange("p (k c) -> p k c", k=KD) for n in range(2)]
        P1 = [at(8192 + 2560 * n, 2560).rearrange("p (t c) -> p t c", t=TT) for n in range(7)]
        P1all = at(8192, 7 * 2560)
        MKV = [at(26112 + 1024 * l, 1024).rearrange("p (m c) -> p m c", m=2) for l in range(2)]
        KTm = [at(28160 + 512 * l, 512).rearrange("p (g m) -> p g m", g=2) for l in range(2)]
        YT0 = at(8192, 5120).rearrange("p (k c) -> p k c", k=KD)
        YT0f = at(8192, 5120)
        MQG0 = at(13312, 2560).rearrange("p (t c) -> p t c", t=TT)
        memT = [at(15872 + 2048 * l, 2048).rearrange("p (k c) -> p k c", k=KD) for l in range(2)]
        M = at(19968, 2048).rearrange("p (t c) -> p t c", t=2)
        H = [at(22016 + 1024 * n, 1024) for n in range(2)]
        SQ = at(24064, 1024)
        Cb = at(15872, 576)
        U = [at(16448 + 600 * n, 600) for n in range(2)]
        Y = at(17648, 576)
        E = at(18224, 576)
        Sb = at(18800, 256)
        Wg = at(29184, 288).rearrange("p (k c) -> p k c", k=KD)
        MA = [15872, 0]
        QT = at(26112, 3072).rearrange("p (r g c) -> p r g c", r=3, g=2)
        QTf = at(26112, 3072)
        KTs = at(29184, 1024).rearrange("p (g c) -> p g c", g=2)
        KTw = at(30208, 1024).rearrange("p (g c) -> p g c", g=2)
        rope_t = [at(8192 + 320 * n, 320) for n in range(4)]
        sig = at(0, 3840)
        PG = [at(29472, 2048), QZ.rearrange("p g b m -> p (g b m)")]
        CPM = [at(19056 + 2048 * m, 2048) for m in range(2)]
        CPR = [[at(23152 + 1024 * m + 512 * n, 512) for n in range(2)] for m in range(2)]
        CR = at(31520, 512)
        CBL = at(25200, 512).rearrange("p (s c) -> p s c", s=4)
        PA = [at(10240 + 512 * n, 512) for n in range(2)]
        PB = [at(8192 + 512 * n, 512) for n in range(2)]
        CRp = at(9216, 512)
        BLp = at(9728, 512).rearrange("p (s c) -> p s c", s=4)
        Qz = at(0, 2048).rearrange("p (g h c) -> p g h c", g=2, h=2)
        PP = [at(2048 + 2112 * n, 2112) for n in range(2)]
        PTt = at(6272, 2304)
        MIXB = at(8576, 3072).rearrange("p (t c) -> p t c", t=PT)
        Om = at(11648, 384)
        SV = [at(4096 * n, 4096).rearrange("p (s c) -> p s c", s=NPG) for n in range(2)]
        SK = [at(8192 + 2048 * n, 2048).rearrange("p (s c) -> p s c", s=8) for n in range(2)]
        SKT = at(12288, 4096).rearrange("p (g c) -> p g c", g=2)
        SM = at(16384, 2112)
        SWKT = at(18496, 1024).rearrange("p (g c) -> p g c", g=2)
        SIMP = at(19520, 130)
        SCH = at(19650, 128)
        SSC = at(19780, 40)
        SMB = at(19820, 40)
        SS2 = at(20460, 40)
        SM8 = at(19860, 8)
        SNM = at(19868, 64)
        SQB = [at(19940 + 256 * n, 256).rearrange("p (g m) -> p g m", g=2) for n in range(2)]
        SWI = [at(26112 + 2048 * n, 2048).rearrange("p (s c) -> p s c", s=4) for n in range(2)]
        SPT = [at(30208 + 512 * n, 512).rearrange("p (s c) -> p s c", s=4) for n in range(2)]
        SW = at(31232, 576)
        SPC = [at(31808, 128), at(20756, 128)]
        SO = at(20500, 256)
        gfin = at(0, 1024)
        fin = [at(1024 + 1024 * n, 1024) for n in range(2)]
        HTf = arena[:, TT * D:TT * D + KD * TOK]

        MIXf = at(8576, 3072)
        rs = lambda a, b: stats[:, a:b]

        const_in = sem("const_in")
        mem_in = sem("mem_in")
        x_in = sem("x_in")
        pad_zero = sem("pad_zero")
        x_zero = sem("x_zero")
        w_in = [sem(f"w_in{n}") for n in range(2)]
        wg_in = sem("wg_in")
        product = sem("product")
        squared = sem("squared")
        mean_sq = sem("mean_sq")
        root = sem("root")
        rstd = sem("rstd")
        scaled = sem("scaled")
        h_turned = sem("h_turned")
        h_taken = sem("h_taken")
        kv_taken = sem("kv_taken")
        kt_turned = sem("kt_turned")
        kt_taken = sem("kt_taken")
        kv_out = sem("kv_out")
        chunk_taken = sem("chunk_taken")
        gates_taken = sem("gates_taken")
        c_copied = sem("c_copied")
        z_exp = sem("z_exp")
        s_copied = sem("s_copied")
        u_made = sem("u_made")
        b_used = sem("b_used")
        z_used = sem("z_used")
        state_set = sem("state_set")
        state_kept = sem("state_kept")
        state_out = sem("state_out")
        conv_y = sem("conv_y")
        sig_exp = sem("sig_exp")
        sig_done = sem("sig_done")
        ma_q, ma_qt, ma_qc, ma_s, ma_m, ma_p, ma_t, ma_td, ma_ta, ma_o, ma_y, ma_yt, ma_done = [
            sem("ma_" + n) for n in ("q_scaled", "q_turned", "q_copied", "scored", "max", "probs", "p_turned",
                                     "p_took_dve", "p_took_act", "out", "y", "y_turned", "y_took")]
        ms_in = [sem(f"ms_in{n}") for n in range(2)]
        ms_q, ms_qt, ms_qz, ms_qb, ms_kt, ms_kc, ms_s, ms_m, ms_p, ms_t, ms_c, ms_o, ms_n, ms_y, ms_done, ms_g, ms_gm = [
            sem("ms_" + n) for n in ("q_scaled", "q_turned", "q_spread", "q_set", "k_turned", "k_copied", "scored",
                                     "max", "probs", "p_turned", "p_copied", "out", "normed", "y_turned", "y_took",
                                     "gate_turned", "gated")]
        out_added = sem("out_added")
        roped = sem("roped")
        r_turned = sem("r_turned")
        r_took = sem("r_took")
        kv_stored = sem("kv_stored")
        gates_back = sem("gates_back")
        gates_written = sem("gates_written")
        vn_copied = sem("vn_copied")
        qz_zero = sem("qz_zero")
        win_copied = sem("win_copied")
        cp_in = [sem(f"cp_in{n}") for n in range(2)]
        cp_a, cp_b, cp_ra, cp_rb, cp_sum, cp_rows, cp_turned, cp_cols, cp_phi, cp_took = [
            sem("cp_" + n) for n in ("prod0", "prod1", "part0", "part1", "summed", "rows", "turned", "cols", "phi",
                                     "took")]
        pa_q, pa_s, pa_m, pa_p, pa_cm, pa_t, pa_td, pa_ta, pa_o, pa_mix = [
            sem("pa_" + n) for n in ("q_set", "scored", "max", "probs", "cmp_masked", "p_turned", "took_dve",
                                     "took_act", "out", "mixed")]
        sa_v = [sem(f"sa_v{n}") for n in range(2)]
        sa_k = [sem(f"sa_k{n}") for n in range(2)]
        (sa_qb, sa_cs, sa_cm, sa_ce, sa_cn, sa_imp, sa_mask, sa_ft, sa_fa, sa_fd, sa_s, sa_m, sa_p,
         sa_bt, sa_ba, sa_bd, sa_used, sa_mix, sa_y, sa_done) = [
            sem("sa_" + n) for n in ("q_set", "cmp_scored", "cmp_max", "cmp_exp", "cmp_normed", "imp",
                                     "mask", "k_turned", "k_took_act", "k_took_dve", "scored", "max", "probs",
                                     "p_turned", "p_took_act", "p_took_dve", "values_used", "mixed", "y_turned", "y_took")]
        sa_w = [sem(f"sa_w{n}") for n in range(2)]
        sa_new = sem("sa_new_read")
        sz_t = sem("sample_gate_turned")
        sz_done = sem("sample_gated")
        r_spread = sem("r_spread")
        ht_zero = sem("ht_zero")
        yg = sem("y_gated")
        yg_t = sem("y_gated_turned")
        yg_c = sem("y_gated_took")
        gfin_in = sem("gfin_in")
        fin_scaled = sem("fin_scaled")
        y_ready = sem("y_ready")
        y_out = [sem(f"y_out{n}") for n in range(2)]
        dve_links = sem("dve_links")
        act_links = sem("act_links")
        pool_links = sem("pool_links")

        block = ctx.enter_context(nc.Block())

        def step_dve():
            nc.vector.memset(rs(398, 399), 0.0)

        def heads(ap):
            return ap.rearrange("p (g d) -> p g d", g=KVH)

        def row_pos(name, s):
            return S(name)[:, HD * s:HD * s + HD].unsqueeze(1).to_broadcast([128, KVH, HD])

        def tile_view(ap):
            return ap.rearrange("p (j g d) -> p j g d", g=KVH, d=HD)

        def tile_pos(name):
            return S(name).rearrange("p (j d) -> p j d", d=HD).unsqueeze(2).to_broadcast([128, 8, KVH, HD])

        BATCHES = [(gg, s) for gg in range(2) for s in range(2)] + [None]

        def pair(n):
            return n // PT, n % PT, 128 * (n % PT + 1)

        def batch(r, n, b):
            k = len(BATCHES) * n + b
            return k % 2, Turn(r, k // 2, 20)

        def mem_bufs(l):
            o = MA[l]
            return {
                "QZ": at(o, 2048).rearrange("p (g b m) -> p g b m", g=2, b=NB),
                "QB": [at(o + 2048 + 256 * n, 256).rearrange("p (g m) -> p g m", g=2) for n in range(2)],
                "KTb": [at(o + 2560 + 512 * n, 512) for n in range(2)],
                "SP": [at(o + 3584 + 256 * n, 256) for n in range(2)],
                "SPT": [at(o + 4096 + 256 * n, 256) for n in range(2)],
                "SO": [at(o + 4608 + 256 * n, 256) for n in range(2)],
                "MC": [at(o + 5632 + 1024 * n, 1024).rearrange("p (m c) -> p m c", m=2) for n in range(2)],
                "QS": at(o + 5120, 256),
                "QT": [at(30496 + 256 * n, 256) for n in range(2)],
                "P": [HTf[:, 2560 + 1024 * n:3584 + 1024 * n].rearrange("p (h m) -> p h m", h=4) for n in range(2)],
                "PT": at(29472, 1024),
                "OY": at(o + 5376, 256),
                "MG": HTf[:, 1280:2560].rearrange("p (t c) -> p t c", t=TT),
            }

        def sample_phase(eng, front, middle, back, lk=None):
            front(Turn(0, 0, 2), None)
            with eng.Fori(0, NB // 2 - 1) as i:
                if lk is not None:
                    lk.enter(i, 2 * LINKS_OF_TURN)
                for n in range(2):
                    t, nxt = Turn(i, n, 2), Turn(i, n + 1, 2)
                    middle(t)
                    front(nxt, t)
                    back(t, 2)
                if lk is not None:
                    lk.leave(NB // 2 - 1)
            t, nxt = Turn(NB // 2 - 1, 0, 2), Turn(NB // 2 - 1, 1, 2)
            middle(t)
            front(nxt, t)
            back(t, 2)
            middle(nxt)
            back(nxt, 1)

        @block.sync
        def _(sp):
            def load_w(n, i=None, blk=None):
                src = I["wall"][n] if blk is None else I["wall"][bass.ds(blk, 1)].rearrange("a p c -> (a p) c")
                sp.dma_start(W[n % 2].rearrange("p k c -> p (k c)"), src).then_inc(w_in[n % 2], 16)

            sp.dma_start(M, I["mem"].rearrange("(t p) c -> p t c", p=128)).then_inc(mem_in, 16)
            sp.dma_start(cst, I["const"]).then_inc(const_in, 16)
            sp.dma_start(small, I["small"]).then_inc(const_in, 16)
            sp.dma_start(ptab[:, :], I["pages"]).then_inc(const_in, 16)
            load_w(0)
            sp.dma_start(X[:, 0:PT, :], I["xp"].rearrange("(t p) c -> p t c", p=128)).then_inc(x_in, 16)
            sp.dma_start(X[0:NS, PT, :], I["xs"]).then_inc(x_in, 16)
            load_w(1)
            sp.wait_ge(product, PBASE[1])
            load_w(2)
            sp.wait_ge(product, PBASE[2])
            load_w(B_CONV)
            for l in range(2):
                sp.wait_ge(kv_taken, 2 * (l + 1))
                sp.dma_start(O["mem"][l].rearrange("(m p) c -> p m c", p=128), MKV[l]).then_inc(kv_out, 16)

            def load_pages(t, first, last):
                for k in range(first, last):
                    sp.wait_ge(cp_a, t.value(NTL, k - 1, base=START.cp_a))
                    sp.wait_ge(cp_b, t.value(NTL, k - 1, base=START.cp_b))
                    for p in range(TILE):
                        page = sp.value_load(ptab[0:1, bass.ds(t.at(NPG, TILE * k + p), 1)], min_val=0, max_val=POOL - 1)
                        sp.dma_start(PG[k % 2][32 * p:32 * p + 32, :],
                                     I["ccmp"][bass.ds(page, 1)].rearrange("a (p j) c -> (a p) (j c)", j=4)
                                     ).then_inc(cp_in[k % 2], 16)

            sp.wait_ge(const_in, 48)
            sp.wait_ge(qz_zero, 1)
            with sp.Fori(0, CT // 2) as i:
                for n in range(2):
                    t = Turn(i, n, 2)
                    load_pages(t, 0, 2)
                    sp.wait_ge(product, t.value(4, 0, base=PBASE[B_CONV]))
                    sp.dma_start(W[(B_CONV + 1 + n) % 2].rearrange("p k c -> p (k c)"),
                                 I["wall"][bass.ds(t.at(1, B_CONV + 1), 1)].rearrange("a p c -> (a p) c")
                                 ).then_inc(w_in[(B_CONV + 1 + n) % 2], 16)
                    load_pages(t, 2, NTL)
            sp.wait_ge(product, PBASE[B_OUT0])
            load_w(B_OUT0 + 1)
            sp.wait_ge(state_kept, START.state_kept + 2 * CT)
            sp.dma_start(O["conv"], CS).then_inc(state_out, 16)

            def mem_loads(l):
                with sp.Fori(0, NB // 2) as i:
                    for n in range(2):
                        t = Turn(i, n, 2)
                        if l == 0:
                            sp.wait_ge(conv_y, START.conv_y + CT)
                        else:
                            sp.wait_ge(gates_taken, 1)
                        sp.wait_ge(ms_o, t.value(1, -1, base=NB * l + START.ms_o))
                        MC = at(MA[l] + 5632 + 1024 * n, 1024).rearrange("p (m c) -> p m c", m=2)
                        sp.dma_start(MC, I["cmem"][l, bass.ds(t.at(1), 1)].rearrange("a (m p) c -> (a p) m c", p=128)
                                     ).then_inc(ms_in[n], 16)

            sp.wait_ge(cp_phi, CT)
            mem_loads(0)
            sp.wait_ge(ma_done, PT)
            sp.wait_ge(ms_gm, 1)
            load_pages(Turn(0, CT, 1), 0, NTL)
            sp.wait_ge(product, PBASE[B_N - 1])
            load_w(B_N)
            load_pages(Turn(0, CT + 1, 1), 0, NTL)
            sp.dma_start(O["win_s"][:, 0:WIN - NT, :], I["win"][:, NT:WIN, :]).then_inc(win_copied, 16)
            sp.dma_start(Wg.rearrange("p k c -> p (k c)"), I["wg"]).then_inc(wg_in, 16)
            for n in range(B_N + 1, B_OUT1):
                sp.wait_ge(product, PBASE[n - 1])
                load_w(n)
            sp.wait_ge(sig_done, 3)
            sp.dma_start(gates_dram, Gate[0:NS, PT, :]).then_inc(gates_written, 16)
            mem_loads(1)
            sp.wait_ge(gates_written, 16)
            sp.wait_ge(qz_zero, 2)
            g_src = gates_dram.rearrange("(b t) (s r g) -> t b s r g", b=NB, s=3, r=GRP)
            with nc.allow_non_contiguous_dma(reason="2304 numbers in all"):
                for g in range(KVH):
                    for r in range(GRP):
                        for s in range(3):
                            sp.dma_start(Grow[32 * g + 8 * r:32 * g + 8 * r + 8, :, s:s + 1], g_src[:, :, s:s + 1, r, g]
                                         ).then_inc(gates_back, 16)
            sp.wait_ge(roped, 4)
            for s, (name, kc, ko, vc, vo) in enumerate((("cmp", 2, 256, 3, 0), ("sel", 3, 256, 4, 0), ("win", 4, 256, 5, 0))):
                for half, (c, o) in enumerate(((kc, ko), (vc, vo))):
                    sp.dma_start(O[name + "_p"][:, half * 256:half * 256 + 256].rearrange("(t p) c -> p t c", p=128),
                                 P1[c][:, 0:PT, o:o + 256]).then_inc(kv_stored, 16)
                    rows = P1[c][0:NS, PT, o:o + 256]
                    if name == "win":
                        for b in range(NB):
                            sp.dma_start(O["win_s"][b, WIN - NT:WIN, half * 256:half * 256 + 256],
                                         P1[c][NT * b:NT * b + NT, PT, o:o + 256]).then_inc(kv_stored, 16)
                    else:
                        sp.dma_start(O[name + "_s"][:, half * 256:half * 256 + 256], rows).then_inc(kv_stored, 16)



            sp.wait_ge(yg_c, PT)
            sp.wait_ge(kv_stored, 16 * (2 * 3 + 2 * 2 + 2 * NB))
            with sp.Fori(0, NB // 2) as i:
                for n in range(2):
                    t = Turn(i, n, 2)
                    b = t.at(1)
                    first = b * NPG
                    for half in range(2):
                        sp.wait_ge(sa_ft, t.value(10, -6 + 4 * half, base=START.sa_ft))
                        for p in range(8):
                            page = sp.value_load(ptab[0:1, bass.ds(first + (8 * half + p), 1)], min_val=0, max_val=POOL - 1)
                            row = I["csel"][bass.ds(page, 1)].rearrange("a p c -> (a p) c")
                            sp.dma_start(SK[half][:, p, :], row[:, 0:256]).then_inc(sa_k[half], 16)
                            if half == 0 and p == 0:
                                sp.wait_ge(sa_used, t.value(6, -6, base=START.sa_used))
                            sp.dma_start(SV[n][:, 8 * half + p, :], row[:, 256:512]).then_inc(sa_v[n], 16)
                    sp.dma_start(SWI[n], I["win"][bass.ds(b, 1)].rearrange("a (s p) c -> (a p) s c", p=128)
                                 ).then_inc(sa_w[n], 16)
            sp.wait_ge(sz_done, 1)
            for n in range(B_OUT1, NBLK):
                load_w(n)
            sp.wait_ge(product, PBASE[NBLK])
            sp.dma_start(gfin, I["gfin"]).then_inc(gfin_in, 16)
            for t in range(TT):
                sp.wait_ge(y_ready, t + 1)
                if t < PT:
                    sp.dma_start(O["yp"][128 * t:128 * t + 128, :], fin[t % 2]).then_inc(y_out[t % 2], 16)
                else:
                    sp.dma_start(O["ys"], fin[t % 2][0:NS, :]).then_inc(y_out[t % 2], 16)
            for n in range(2):
                sp.wait_ge(y_out[n], 16 * ((TT + 1 - n) // 2))
            sp.wait_ge(state_out, 16)
            sp.wait_ge(kv_out, 32)
            sp.wait_ge(win_copied, 16)

        @block.gpsimd
        def _(pool):
            for signal, start in (
                    (cp_a, START.cp_a), (cp_b, START.cp_b), (cp_sum, START.cp_sum), (cp_ra, START.cp_ra), (cp_rb, START.cp_rb), (conv_y, START.conv_y), (ms_s, START.ms_s),
                    (u_made, START.u_made), (pa_t, START.pa_t), (pa_o, START.pa_o), (sa_bt, START.sa_bt),
                    (c_copied, START.c_copied), (s_copied, START.s_copied), (b_used, START.b_used), (z_used, START.z_used),
                    (ms_kc, START.ms_kc), (ms_c, START.ms_c), (ms_done, START.ms_done), (cp_rows, START.cp_rows), (cp_cols, START.cp_cols),
                    (cp_took, START.cp_took), (pa_p, START.pa_p), (pa_mix, START.pa_mix), (pa_ta, START.pa_ta),
                    (pa_td, START.pa_td), (sa_ba, START.sa_ba), (sa_bd, START.sa_bd), (sa_m, START.sa_m),
                    (sa_p, START.sa_p), (sa_done, START.sa_done), (state_kept, START.state_kept), (ms_y, START.ms_y),
                    (sa_y, START.sa_y), (pa_s, START.pa_s), (sa_used, START.sa_used), (sa_ft, START.sa_ft),
                    (sa_s, START.sa_s), (ms_o, START.ms_o),):
                pool.sem_inc(signal, start)
            nc.gpsimd.memset(Grow, 0.0).then_inc(qz_zero, 1)
            lk = Links(pool, pool_links)
            pool.wait_ge(const_in, 48)
            pool.wait_ge(product, PBASE[B_C0])
            for n in range(2):
                nc.gpsimd.memset(U[n][:, 0:2], 0.0).then_inc(pad_zero, 1)
            for k in range(KD):
                ins = nc.gpsimd.memset(YT0[:, k, SEQ + NS:TOK], 0.0)
            ins.then_inc(pad_zero, 1)

            def page_prod1(t):
                for k in range(NTL):
                    pool.wait_ge(cp_in[k % 2], t.value(32 * TILE, 16 * TILE * (k // 2 + 1)))
                    pool.wait_ge(cp_rb, t.value(NTL, k, base=START.cp_rb))
                    nc.gpsimd.tensor_tensor(tile_view(CPM[1]), tile_view(PG[k % 2]), tile_pos("tile_pos1"), ALU.mult
                                            ).then_inc(cp_b, 1)
                    pool.wait_ge(cp_b, t.value(NTL, k + 1, base=START.cp_b))
                    lk.link(nc.gpsimd.tensor_tensor(CPM[1][:, 0:1024], CPM[1][:, 0:1024], CPM[1][:, 1024:2048], ALU.add))
                    pool.wait_ge(cp_sum, t.value(NTL, k - 1, base=START.cp_sum))
                    nc.gpsimd.tensor_tensor(CPR[1][k % 2], CPM[1][:, 0:512], CPM[1][:, 512:1024], ALU.add
                                            ).then_inc(cp_rb, 1)

            with pool.Fori(0, CT // 2) as i:
                lk.enter(i, 2 * NTL)
                for n in range(2):
                    t = Turn(i, n, 2)
                    Us = U[n][:, 514:594].rearrange("p (b c) -> p b c", b=NB)
                    pool.wait_ge(conv_y, t.value(1, -1, base=START.conv_y))
                    src = small[:, bass.ds(t.at(16, SMALL["state"][0]), 16)].rearrange("p (b c) -> p b c", b=NB)
                    nc.gpsimd.tensor_copy(Us[:, :, 0:2], src).then_inc(state_set, 1)
                    page_prod1(t)
                lk.leave(CT // 2)

            def mem_q(l):
                QZm = at(MA[l], 2048).rearrange("p (g b m) -> p g b m", g=2, b=NB)
                if l == 0:
                    pool.wait_ge(conv_y, START.conv_y + CT)
                    pool.wait_ge(state_kept, START.state_kept + 2 * CT)
                else:
                    pool.wait_ge(sig_done, 3)
                nc.gpsimd.memset(QZm, 0.0).then_inc(ms_qz, 1)
                pool.wait_ge(ms_qz, 5 * (l + 1))
                with pool.Fori(0, NB // 2) as i:
                    for n in range(2):
                        t = Turn(i, n, 2)
                        QB = at(MA[l] + 2048 + 256 * n, 256).rearrange("p (g m) -> p g m", g=2)
                        pool.wait_ge(ms_s, t.value(1, -1, base=NB * l + START.ms_s))
                        nc.gpsimd.tensor_copy(QB, QZm[:, :, bass.ds(t.at(1), 1), :].rearrange("p g a m -> p g (a m)")
                                              ).then_inc(ms_qb, 1)
            mem_q(0)
            pool.wait_ge(ma_done, PT)
            pool.wait_ge(ms_gm, 1)
            for b in range(CT, NB):
                page_prod1(Turn(0, b, 1))
            pool.wait_ge(cp_a, START.cp_a + NB * NTL)
            pool.wait_ge(cp_b, START.cp_b + NB * NTL)
            nc.gpsimd.memset(QZ, 0.0).then_inc(qz_zero, 1)
            mem_q(1)

            for p in range(PT):
                pool.wait_ge(ma_done, 2 * PT)
                pool.wait_ge(ms_gm, 2)
                pool.wait_ge(roped, 4)
                if p >= 2:
                    pool.wait_ge(cp_sum, NB * NTL + START.cp_sum + p - 1)
                nc.gpsimd.tensor_tensor(heads(PB[p % 2][:, 0:256]), heads(P1[2][:, p, 256:512]), row_pos("pos1", 0), ALU.mult)
                nc.gpsimd.tensor_tensor(heads(PB[p % 2][:, 256:512]), heads(P1[3][:, p, 0:256]), row_pos("pos1", 1),
                                        ALU.mult).then_inc(cp_rb, 1)

            pool.wait_ge(r_spread, 6)
            pool.wait_ge(yg_c, PT)
            pool.wait_ge(kv_stored, 16 * (2 * 3 + 2 * 2 + 2 * NB))
            nc.gpsimd.memset(HT[:, 2:8, SEQ + NS:TOK], 0.0).then_inc(ht_zero, 1)
            with pool.Fori(0, NB // 2) as i:
                for n in range(2):
                    t = Turn(i, n, 2)
                    pool.wait_ge(sa_s, t.value(1, -1, base=START.sa_s))
                    nc.gpsimd.tensor_copy(SQB[n], QZ[:, :, bass.ds(t.at(1), 1), :].rearrange("p g a m -> p g (a m)")
                                          ).then_inc(sa_qb, 1)

        @block.scalar
        def _(act):
            lk = Links(act, act_links)

            def norm_act(tiles, first, number):
                for j, src in enumerate(tiles):
                    if number == 0:
                        act.wait_ge(mem_in if j < 2 else x_in, 16 if j < 2 else 32)
                        if j == 6:
                            act.wait_ge(x_zero, 1)
                    elif number == 1:
                        act.wait_ge(out_added, 2 * TT)
                    else:
                        act.wait_ge(out_added, 4 * TT)
                    nc.scalar.activation(SQ, src, ACT.Square, accum_out=rs(first + j, first + j + 1)).then_inc(squared, 1)
                    act.wait_ge(squared, first + j + 1)
                act.wait_ge(mean_sq, number + 1)
                nc.scalar.activation(rs(20 + first, 20 + first + len(tiles)), rs(20 + first, 20 + first + len(tiles)),
                                     ACT.Sqrt).then_inc(root, 1)
                act.wait_ge(rstd, number + 1)

            tiles0 = [M[:, 0, :], M[:, 1, :]] + [X[:, t, :] for t in range(TT)]
            norm_act(tiles0, 0, 0)
            for j, src in enumerate(tiles0):
                if j >= 2:
                    act.wait_ge(h_turned, 2 * (j - 1))
                nc.scalar.activation(H[j % 2], src, ACT.Copy, scale=rs(20 + j, 21 + j)).then_inc(scaled, 1)
            for l in range(2):
                for m in range(2):
                    act.wait_ge(product, 2 * l + m + 1)
                    nc.scalar.copy(MKV[l][:, m, :], PS[:, 2 * l + m, :]).then_inc(kv_taken, 1)
            for l in range(2):
                act.wait_ge(kt_turned, l + 1)
                nc.scalar.copy(KTm[l].rearrange("p g m -> p (g m)"), PS[:, 4 + l, :]).then_inc(kt_taken, 1)

            def take_chunk(c, P, first):
                for t in range(TT):
                    act.wait_ge(product, first + t + 1)
                    nc.scalar.copy(P[:, t, :], PS[:, t, :]).then_inc(chunk_taken, 1)

            take_chunk(0, MQG0, PBASE[B_C0])

            def copy_rows(t):
                act.wait_ge(cp_sum, t.value(NTL, NTL, base=START.cp_sum))
                nc.scalar.copy(CR[0:NC, :], PS[0:NC, 5, :]).then_inc(cp_rows, 1)

            def keep_blocks(t):
                act.wait_ge(cp_turned, t.value(1, 1))
                nc.scalar.copy(CBL[:, :, 0:NC], PS[:, 6, :].rearrange("p (s c) -> p s c", s=4)[:, :, 0:NC]
                               ).then_inc(cp_cols, 1)
                act.wait_ge(cp_phi, t.value(1, 1))
                nc.scalar.copy(KC[:, :, bass.ds(t.at(1), 1), 0:NC].rearrange("p g a n -> p g (a n)"),
                               PS[:, 7, 0:256].rearrange("p (g n) -> p g n", g=2)[:, :, 0:NC])
                nc.scalar.copy(VC[0:NC, bass.ds(t.at(1), 1), :].rearrange("p a n -> p (a n)"),
                               PS[0:NC, 7, 256:512]).then_inc(cp_took, 1)

            with act.Fori(0, CT // 2) as i:
                for n in range(2):
                    t = Turn(i, n, 2)
                    act.wait_ge(product, t.value(4, 1, base=PBASE[B_CONV]))
                    act.wait_ge(u_made, t.value(2, 0, base=START.u_made))
                    nc.scalar.copy(Cb[:, 0:512], PS[:, 0, :]).then_inc(c_copied, 1)
                    copy_rows(t)
                    act.wait_ge(product, t.value(4, 4, base=PBASE[B_CONV]))
                    act.wait_ge(conv_y, t.value(1, 0, base=START.conv_y))
                    nc.scalar.copy(Sb, PS[:, 4, 0:256]).then_inc(s_copied, 1)
                    nc.scalar.activation(E[:, 0:512], PS[:, 3, :], ACT.Exp, scale=-1.0)
                    act.wait_ge(s_copied, t.value(1, 1, base=START.s_copied))
                    nc.scalar.activation(E[:, 512:576], Sb[:, 192:256], ACT.Exp, scale=-1.0).then_inc(z_exp, 1)
                    keep_blocks(t)

            def mem_prompt_act(l, YT):
                QTt, P, PTb, MG = (mem_bufs(l)[k] for k in ("QT", "P", "PT", "MG"))
                act.wait_ge(chunk_taken, TT if l == 0 else 8 * TT)
                if l == 0:
                    act.wait_ge(conv_y, START.conv_y + CT)
                else:
                    act.wait_ge(gates_taken, 1)
                P0 = MQG0 if l == 0 else P1[0]
                nc.scalar.activation(MG, P0[:, :, 256:512], ACT.Exp, scale=-1.0).then_inc(sig_exp, 1)
                for n in range(PT):
                    T = l * PT + n
                    act.wait_ge(ma_qt, T + 1)
                    nc.scalar.copy(QTt[n % 2], PS[:, 5, 256 * (n % 2):256 * (n % 2) + 256]).then_inc(ma_qc, 1)
                    act.wait_ge(ma_m, 2 * (T + 1))
                    if T >= 2:
                        act.wait_ge(ma_t, 2 * (T - 1))
                    for h in range(4):
                        nc.scalar.activation(P[n % 2][:, h, :], PS[:, 2 * (n % 2) + h % 2, 256 * (h // 2):256 * (h // 2) + 256],
                                             ACT.Exp, bias=rs(60 + 8 * (n % 2) + h, 61 + 8 * (n % 2) + h),
                                             accum_out=rs(76 + 8 * (n % 2) + h, 77 + 8 * (n % 2) + h)).then_inc(ma_p, 1)
                    act.wait_ge(ma_t, 2 * (T + 1))
                    act.wait_ge(ma_o, T)
                    nc.scalar.copy(PTb[:, 512:1024], PS[:, 7, :]).then_inc(ma_ta, 1)
                    act.wait_ge(ma_yt, T + 1)
                    nc.scalar.copy(YT[:, 0:2, 128 * n:128 * n + 128],
                                   PS[:, 5, 256 * (n % 2):256 * (n % 2) + 256].rearrange("p (g c) -> p g c", g=2)
                                   ).then_inc(ma_done, 1)

            def mem_sample_act(l):
                b_ = mem_bufs(l)
                with act.Fori(0, NB // 2) as i:
                    for n in range(2):
                        t = Turn(i, n, 2)
                        v = lambda plus: t.value(1, plus, base=NB * l)
                        act.wait_ge(ms_kt, v(1))
                        nc.scalar.copy(b_["KTb"][n], PS[:, 6, :]).then_inc(ms_kc, 1)
                        act.wait_ge(ms_m, v(1))
                        nc.scalar.activation(b_["SP"][n], PS[:, n, 0:256], ACT.Exp, bias=rs(100 + n, 101 + n),
                                             accum_out=rs(104 + n, 105 + n)).then_inc(ms_p, 1)

            mem_prompt_act(0, YT0)
            mem_sample_act(0)
            for b in range(CT, NB):
                copy_rows(Turn(0, b, 1))
                keep_blocks(Turn(0, b, 1))
            norm_act([X[:, t, :] for t in range(TT)], 7, 1)
            for j in range(TT):
                act.wait_ge(h_turned, 2 * (7 + j - 1))
                nc.scalar.activation(H[(7 + j) % 2], X[:, j, :], ACT.Copy, scale=rs(27 + j, 28 + j)).then_inc(scaled, 1)
            with act.Fori(0, 3) as i:
                for n in range(2):
                    t = Turn(i, n, 2)
                    for j in range(TT):
                        act.wait_ge(product, t.value(TT, j + 1, base=PBASE[B_N]))
                        nc.scalar.copy(P1all[:, bass.ds(t.at(2560, 512 * j), 512)], PS[:, j, :]).then_inc(chunk_taken, 1)
            take_chunk(6, P1[6], PBASE[B_N + 6])
            act.wait_ge(product, P_GATES + TT)
            nc.scalar.activation(Gate[:, :, :], PS[:, 5, 0:180].rearrange("p (t c) -> p t c", t=TT), ACT.Exp,
                                 scale=-1.0).then_inc(gates_taken, 1)
            Z5 = sig[:, 0:1280].rearrange("p (t c) -> p t c", t=TT)
            Z6 = sig[:, 1280:3840].rearrange("p (t c) -> p t c", t=TT)
            act.wait_ge(gates_taken, 1)
            act.wait_ge(chunk_taken, 8 * TT)
            nc.scalar.activation(Z5, P1[5][:, :, 256:512], ACT.Exp, scale=-1.0).then_inc(z_exp, 1)
            nc.scalar.activation(Z6, P1[6], ACT.Exp, scale=-1.0).then_inc(z_exp, 1)
            mem_prompt_act(1, HT)
            mem_sample_act(1)
            for j in range(10):
                act.wait_ge(r_turned, j + 1)
                if j < 6:
                    nc.scalar.activation(QT[:, j // 2, j % 2, :], PS[:, j % 4, :], ACT.Copy, scale=SCALE).then_inc(r_took, 1)
                else:
                    K = (KTs, KTw)[(j - 6) // 2]
                    nc.scalar.copy(K[:, j % 2, :], PS[:, j % 4, :]).then_inc(r_took, 1)
            act.wait_ge(cp_sum, NB * NTL + PT + START.cp_sum)
            nc.scalar.copy(CRp[0:NCP, :], PS[0:NCP, 2, :]).then_inc(cp_rows, 1)
            act.wait_ge(cp_turned, NB + 1)
            nc.scalar.copy(BLp[:, :, 0:NCP], PS[:, 3, :].rearrange("p (s c) -> p s c", s=4)[:, :, 0:NCP]
                           ).then_inc(cp_cols, 1)
            act.wait_ge(cp_phi, NB + 1)
            nc.scalar.copy(KCp[:, :, 0:NCP], PS[:, 5, 0:256].rearrange("p (g n) -> p g n", g=2)[:, :, 0:NCP])
            nc.scalar.copy(VCp[0:NCP, :], PS[0:NCP, 5, 256:512]).then_inc(cp_took, 1)
            with act.Fori(0, GRP) as r:
                def exps(n):
                    t = Turn(r, n, 8)
                    gp, ti, nk = pair(n)
                    P, m = PP[n % 2], 200 + 8 * (n % 2)
                    act.wait_ge(pa_t, t.value(5, -5, base=START.pa_t))
                    for gg in range(2):
                        act.wait_ge(pa_m, t.value(3, gg + 1))
                        for s in range(2):
                            c = 2 + 2 * s + gg
                            ins = nc.scalar.activation(P[:, 1024 * gg + 512 * s:1024 * gg + 512 * s + nk],
                                                       PS[:, 2 * gg + s, 0:nk], ACT.Exp, bias=rs(m + c, m + c + 1),
                                                       accum_out=rs(m + 20 + c, m + 21 + c))
                        ins.then_inc(pa_p, 1)
                    act.wait_ge(pa_m, t.value(3, 3))
                    for gg in range(2):
                        ins = nc.scalar.activation(P[:, 2048 + 32 * gg:2048 + 32 * gg + NCP], PS[:, 7, 32 * gg:32 * gg + NCP],
                                                   ACT.Exp, bias=rs(m + gg, m + gg + 1),
                                                   accum_out=rs(m + 20 + gg, m + 21 + gg))
                    ins.then_inc(pa_p, 1)

                def took(n):
                    gp, ti, nk = pair(n)
                    act.wait_ge(pa_o, Turn(r, n, 8).value(1, 0, base=START.pa_o))
                    for b, what in enumerate(BATCHES):
                        bank, before = batch(r, n, b)
                        if bank == 1:
                            act.wait_ge(pa_t, Turn(r, n, 8).value(5, b + 1, base=START.pa_t))
                            if what is None:
                                nc.scalar.copy(PTt[0:NCP, 2048:2304], PS[0:NCP, 6, 0:256]).then_inc(pa_ta, 1)
                            else:
                                o = 1024 * what[0] + 512 * what[1]
                                nc.scalar.copy(PTt[:, o:o + nk], PS[:, 6, 0:nk]).then_inc(pa_ta, 1)

                for n in range(8):
                    exps(n)
                    if n:
                        took(n - 1)
                took(7)
            for t in range(PT):
                act.wait_ge(yg_t, 2 * t + 1)
                nc.scalar.copy(HT[:, 2:6, 128 * t:128 * t + 128], PS[:, 6, :].rearrange("p (k c) -> p k c", k=4))
                act.wait_ge(yg_t, 2 * t + 2)
                nc.scalar.copy(HT[:, 6:8, 128 * t:128 * t + 128], PS[:, 7, 0:256].rearrange("p (k c) -> p k c", k=2)
                               ).then_inc(yg_c, 1)

            def front(t, prev):
                act.wait_ge(sa_cm, t.value(1, 1))
                act.wait_ge(sa_bt, t.value(6, -6, base=START.sa_bt))
                nc.scalar.activation(SPC[t.n % 2][:, 0:NC], PS[:, 5, 0:NC], ACT.Exp, bias=rs(140, 141),
                                     accum_out=rs(141, 142)).then_inc(sa_ce, 1)
                for j in range(0, 10, 2):
                    act.wait_ge(sa_ft, t.value(10, j + 1, base=START.sa_ft))
                    if j < 8:
                        nc.scalar.copy(SKT[:, :, 256 * j:256 * j + 256], PS[:, 6, :].rearrange("p (g c) -> p g c", g=2)
                                       ).then_inc(sa_fa, 1)
                    else:
                        nc.scalar.copy(SWKT[:, 0, :], PS[:, 6, :]).then_inc(sa_fa, 1)

            def middle(t):
                act.wait_ge(sa_m, t.value(2, 1, base=START.sa_m))
                nc.scalar.activation(SM, SM, ACT.Exp, bias=rs(150, 151), accum_out=rs(152, 153)).then_inc(sa_p, 1)
                act.wait_ge(sa_m, t.value(2, 2, base=START.sa_m))
                nc.scalar.activation(SW[:, 0:512], PS[:, 4, :], ACT.Exp, bias=rs(151, 152), accum_out=rs(153, 154)
                                     ).then_inc(sa_p, 1)
                nc.scalar.activation(SW[:, 512:576], SW[:, 512:576], ACT.Exp, bias=rs(151, 152),
                                     accum_out=rs(154, 155)).then_inc(sa_p, 1)

            def back(t, fronts):
                for j in range(0, 6, 2):
                    act.wait_ge(sa_bt, t.value(6, j + 1, base=START.sa_bt))
                    act.wait_ge(sa_used, t.value(6, j - 1, base=START.sa_used))
                    nc.scalar.copy(SPT[0], PS[:, 6, :].rearrange("p (s c) -> p s c", s=4)).then_inc(sa_ba, 1)

            sample_phase(act, front, middle, back)
            norm_act([X[:, t, :] for t in range(TT)], 12, 2)
            for j in range(TT):
                if j >= 2:
                    act.wait_ge(y_ready, j - 1)
                nc.scalar.activation(H[j % 2], X[:, j, :], ACT.Copy, scale=rs(32 + j, 33 + j)).then_inc(fin_scaled, 1)

        @block.tensor
        def _(pe):
            def mm(out, lhsT, rhs, start=True, stop=True):
                return nc.tensor.matmul(out, lhsT, rhs, start=start, stop=stop, skip_group_check=True)

            def turn(out, in_):
                return nc.tensor.transpose(out, in_, ident[0:in_.shape[0], 0:in_.shape[0]])

            pe.wait_ge(const_in, 48)

            def norm_turns(first, count):
                for j in range(first, first + count):
                    pe.wait_ge(scaled, j + 1)
                    for half in range(2):
                        n = 2 * j + half
                        if n >= 4:
                            pe.wait_ge(h_taken, n - 3)
                        for k in range(4):
                            ins = turn(PS[:, n % 4, 128 * k:128 * k + 128],
                                       H[j % 2][:, 512 * half + 128 * k:512 * half + 128 * k + 128])
                        ins.then_inc(h_turned, 1)

            norm_turns(0, 7)
            pe.wait_ge(h_taken, 14)
            for l in range(2):
                pe.wait_ge(w_in[l], 16)
                for m in range(2):
                    for k in range(KD):
                        ins = mm(PS[:, 2 * l + m, :], memT[l][:, k, 128 * m:128 * m + 128], W[l][:, k, :],
                                 k == 0, k == KD - 1)
                    ins.then_inc(product, 1)
            for l in range(2):
                pe.wait_ge(kv_taken, 2 * (l + 1))
                for g in range(2):
                    for m in range(2):
                        ins = turn(PS[:, 4 + l, 256 * g + 128 * m:256 * g + 128 * m + 128],
                                   MKV[l][:, m, 128 * g:128 * g + 128])
                ins.then_inc(kt_turned, 1)

            def chunk(src, Wb, taken, beside=None):
                for t in range(TT):
                    if taken is not None:
                        pe.wait_ge(*taken(t))
                    for k in range(KD):
                        ins = mm(PS[:, t, :], src[:, k, 128 * t:128 * t + 128], Wb[:, k, :], k == 0, k == KD - 1)
                    ins.then_inc(product, 1)
                    if beside is not None:
                        beside(t)

            pe.wait_ge(w_in[0], 32)
            pe.wait_ge(kv_taken, 4)
            pe.wait_ge(kt_taken, 2)
            chunk(HT, W[0], None)
            pe.wait_ge(kt_taken, 2)
            pe.wait_ge(chunk_taken, TT)

            def sums(A, Bp, p, tiles, per, name, out):
                n, o = per * tiles, per * (tiles - 1 - p)
                mm(out, C(name)[:, o:o + n], A, p == 0, False)
                mm(out, C(name)[:, o + 1:o + 1 + n], Bp, False, p == tiles - 1).then_inc(cp_sum, 1)

            def turn_blocks(rows, bank, nch):
                for s in range(4):
                    ins = turn(PS[:, bank, 128 * s:128 * s + nch], rows[0:nch, 128 * s:128 * s + 128])
                ins.then_inc(cp_turned, 1)

            def phi(BL, bank, nch):
                for g in range(2):
                    mm(PS[:, bank, 128 * g:128 * g + nch], S("phi_k"), BL[:, g, 0:nch])
                for g in range(2):
                    ins = mm(PS[0:nch, bank, 256 + 128 * g:384 + 128 * g], BL[:, 2 + g, 0:nch], S("phi_v"))
                ins.then_inc(cp_phi, 1)

            def page_sums(t, first, last):
                if first == 0:
                    pe.wait_ge(cp_rows, t.value(1, 0, base=START.cp_rows))
                for k in range(first, last):
                    pe.wait_ge(cp_ra, t.value(NTL, k + 1, base=START.cp_ra))
                    pe.wait_ge(cp_rb, t.value(NTL, k + 1, base=START.cp_rb))
                    sums(CPR[0][k % 2], CPR[1][k % 2], k, NTL, 8 * TILE, "chunk4", PS[:, 5, :])

            def page_turn(t):
                pe.wait_ge(cp_rows, t.value(1, 1, base=START.cp_rows))
                pe.wait_ge(cp_cols, t.value(1, 0, base=START.cp_cols))
                turn_blocks(CR, 6, NC)

            def page_phi(t):
                pe.wait_ge(cp_cols, t.value(1, 1, base=START.cp_cols))
                pe.wait_ge(cp_took, t.value(1, 0, base=START.cp_took))
                phi(CBL, 7, NC)

            between = {(1, 3): (0, 1), (1, 7): (1, 2), (2, 7): (2, 3), (3, 1): (3, 4)}
            with pe.Fori(0, CT // 2) as i:
                for n in range(2):
                    t = Turn(i, n, 2)
                    w = (n + 1) % 2
                    pe.wait_ge(w_in[w], i * 16 + (32 if w == 1 else 48))
                    for q in range(4):
                        if q == 0:
                            pe.wait_ge(c_copied, t.value(1, 0, base=START.c_copied))
                            pe.wait_ge(s_copied, t.value(1, 0, base=START.s_copied))
                        elif q == 1:
                            pe.wait_ge(u_made, t.value(2, 0, base=START.u_made))
                        elif q == 2:
                            pe.wait_ge(b_used, t.value(1, 0, base=START.b_used))
                        else:
                            pe.wait_ge(z_used, t.value(1, 0, base=START.z_used))
                        for k in range(KD):
                            mm(PS[:, q, :], W[w][:, k, 128 * q:128 * q + 128], HT[:, k, 0:512], k == 0, k == KD - 1)
                            if (q, k) in between:
                                page_sums(t, *between[q, k])
                            if (q, k) == (3, 6):
                                page_turn(t)
                        for k in range(KD):
                            ins = mm(PS[:, 4, 64 * q:64 * q + 64], W[w][:, k, 128 * q:128 * q + 128],
                                     HT[:, k, 512:576], k == 0, k == KD - 1)
                        ins.then_inc(product, 1)
                    page_phi(t)

            def mem_prompt(l):
                b_ = mem_bufs(l)
                QTt, P, PTb = b_["QT"], b_["P"], b_["PT"]
                for n in range(PT):
                    T = l * PT + n
                    pr = n % 2
                    pe.wait_ge(ma_q, T + 1)
                    pe.wait_ge(ma_done, T)
                    for g in range(2):
                        ins = turn(PS[:, 5, 256 * pr + 128 * g:256 * pr + 128 * g + 128], b_["QS"][:, 128 * g:128 * g + 128])
                    ins.then_inc(ma_qt, 1)
                    pe.wait_ge(ma_qc, T + 1)
                    if T >= 2:
                        pe.wait_ge(ma_p, 4 * (T - 1))
                    for h in range(4):
                        o = 64 * (h % 2)
                        ins = mm(PS[:, 2 * pr + h % 2, 256 * (h // 2):256 * (h // 2) + 256],
                                 QTt[pr][o:o + 64, 128 * (h // 2):128 * (h // 2) + 128], KTm[l][o:o + 64, h // 2, :])
                    ins.then_inc(ma_s, 1)
                    pe.wait_ge(ma_p, 4 * (T + 1))
                    pe.wait_ge(ma_td, T)
                    pe.wait_ge(ma_ta, T)
                    for h in range(4):
                        for m in range(2):
                            ins = turn(PS[:, 6 + h // 2, 256 * (h % 2) + 128 * m:256 * (h % 2) + 128 * m + 128],
                                       P[pr][:, h, 128 * m:128 * m + 128])
                        if h % 2:
                            ins.then_inc(ma_t, 1)
                    if T >= 2:
                        pe.wait_ge(ma_y, T - 1)
                    pe.wait_ge(ma_td, T + 1)
                    pe.wait_ge(ma_ta, T + 1)
                    for h in range(4):
                        for m in range(2):
                            ins = mm(PS[:, 4, 256 * pr + 64 * h:256 * pr + 64 * h + 64],
                                     PTb[:, 256 * h + 128 * m:256 * h + 128 * m + 128],
                                     MKV[l][:, m, 256 + 64 * h:256 + 64 * h + 64], m == 0, m == 1)
                    ins.then_inc(ma_o, 1)
                    pe.wait_ge(ma_y, T + 1)
                    for g in range(2):
                        ins = turn(PS[:, 5, 256 * pr + 128 * g:256 * pr + 128 * g + 128], b_["OY"][:, 128 * g:128 * g + 128])
                    ins.then_inc(ma_yt, 1)

            def mem_sample(l):
                b_ = mem_bufs(l)
                pe.wait_ge(ms_q, l + 1)
                pe.wait_ge(ma_done, PT * (l + 1))
                for g in range(2):
                    ins = turn(PS[:, 5, 128 * g:128 * g + 128], b_["QS"][:, 128 * g:128 * g + 128])
                ins.then_inc(ms_qt, 1)
                pe.wait_ge(ma_y, PT * (l + 1))
                with pe.Fori(0, NB // 2) as i:
                    for n in range(2):
                        t = Turn(i, n, 2)
                        v = lambda plus: t.value(1, plus, base=NB * l)
                        pe.wait_ge(ms_in[n], i * 16 + 16 * (1 + l * NB // 2))
                        pe.wait_ge(ms_kc, v(START.ms_kc))
                        for g in range(2):
                            for m in range(2):
                                ins = turn(PS[:, 6, 256 * g + 128 * m:256 * g + 128 * m + 128],
                                           b_["MC"][n][:, m, 128 * g:128 * g + 128])
                        ins.then_inc(ms_kt, 1)
                        pe.wait_ge(ms_kc, v(START.ms_kc + 1))
                        pe.wait_ge(ms_qb, v(1))
                        for g in range(2):
                            ins = mm(PS[:, n, 0:256], b_["QB"][n][:, g, :], b_["KTb"][n][:, 256 * g:256 * g + 256],
                                     g == 0, g == 1)
                        ins.then_inc(ms_s, 1)
                        pe.wait_ge(ms_p, v(1))
                        pe.wait_ge(ms_c, v(START.ms_c))
                        for m in range(2):
                            ins = turn(PS[:, 7, 128 * m:128 * m + 128], b_["SP"][n][:, 128 * m:128 * m + 128])
                        ins.then_inc(ms_t, 1)
                        pe.wait_ge(ms_c, v(START.ms_c + 1))
                        for m in range(2):
                            ins = mm(PS[:, 2 + n, 0:256], b_["SPT"][n][:, 128 * m:128 * m + 128],
                                     b_["MC"][n][:, m, 256:512], m == 0, m == 1)
                        ins.then_inc(ms_o, 1)
                        pe.wait_ge(ms_n, v(1))
                        pe.wait_ge(ms_done, v(START.ms_done))
                        for g in range(2):
                            ins = turn(PS[:, 4, 128 * g:128 * g + 128], b_["SO"][n][:, 128 * g:128 * g + 128])
                        ins.then_inc(ms_y, 1)
                pe.wait_ge(ms_qz, 5 * (l + 1))
                P0 = MQG0 if l == 0 else P1[0]
                for g in range(2):
                    ins = turn(PS[:, 5, 128 * g:128 * g + 128], P0[:, PT, 256 + 128 * g:256 + 128 * g + 128])
                ins.then_inc(ms_g, 1)

            def out_proj(YT, first, l):
                for n in range(2):
                    def beside(j):
                        t = Turn(0, CT + n, 1)
                        if j < PT:
                            page_sums(t, j, j + 1)
                        else:
                            page_turn(t)
                            page_phi(t)

                    pe.wait_ge(w_in[(first + n) % 2], w_count(first + n))
                    chunk(YT, W[(first + n) % 2],
                          lambda t, n=n: (out_added, 2 * TT * l + t + 1 if n else 2 * TT * l),
                          beside if l == 0 else None)

            pe.wait_ge(conv_y, START.conv_y + CT)
            pe.wait_ge(cp_took, START.cp_took + CT)
            mem_prompt(0)
            mem_sample(0)
            pe.wait_ge(ms_gm, 1)
            pe.wait_ge(pad_zero, 3)
            pe.wait_ge(ma_done, PT)
            out_proj(YT0, B_OUT0, 0)
            pe.wait_ge(out_added, 2 * TT)
            norm_turns(7, TT)
            pe.wait_ge(h_taken, 2 * 12)
            with pe.Fori(0, 3) as i:
                for n in range(2):
                    t = Turn(i, n, 2)
                    w = (B_N + n) % 2
                    pe.wait_ge(w_in[w], i * 16 + w_count(B_N + n))
                    chunk(HT, W[w], lambda j: (chunk_taken, t.value(TT, j - 4, base=TT)))
            pe.wait_ge(w_in[(B_N + 6) % 2], w_count(B_N + 6))
            chunk(HT, W[(B_N + 6) % 2], lambda j: (chunk_taken, 7 * TT + j - 4))
            pe.wait_ge(wg_in, 16)
            for j in range(TT):
                for k in range(KD):
                    ins = mm(PS[:, 5, 36 * j:36 * j + 36], HT[:, k, 128 * j:128 * j + 128], Wg[:, k, :], k == 0, k == KD - 1)
                ins.then_inc(product, 1)
            pe.wait_ge(chunk_taken, 8 * TT)
            pe.wait_ge(gates_taken, 1)
            mem_prompt(1)
            mem_sample(1)
            pe.wait_ge(roped, 4)
            pe.wait_ge(ms_gm, 2)
            pe.wait_ge(ms_p, 2 * NB)
            pe.wait_ge(ms_n, 2 * NB)
            for j in range(10):
                if j >= 4:
                    pe.wait_ge(r_took, j - 3)
                for t in range(PT):
                    if j < 6:
                        r, g = j // 2, j % 2
                        src = P1[1 + r // 2][:, t, 256 * (r % 2) + 128 * g:256 * (r % 2) + 128 * g + 128]
                    else:
                        src = P1[3 + (j - 6) // 2][:, t, 256 + 128 * (j % 2):384 + 128 * (j % 2)]
                    ins = turn(PS[:, j % 4, 128 * t:128 * t + 128], src)
                ins.then_inc(r_turned, 1)
            for j in range(6):
                r, g = j // 2, j % 2
                src = P1[1 + r // 2][0:NS, PT, 256 * (r % 2) + 128 * g:256 * (r % 2) + 128 * g + 128]
                ins = turn(PS[:, 6, 64 * j:64 * j + 64], src)
            ins.then_inc(r_turned, 1)
            for j in range(4):
                src = P1[3 + j // 2][0:NS, PT, 256 + 128 * (j % 2):384 + 128 * (j % 2)]
                ins = turn(PS[:, 7, 64 * j:64 * j + 64], src)
            ins.then_inc(r_turned, 1)
            pe.wait_ge(r_took, 10)
            for p in range(PT):
                pe.wait_ge(cp_ra, START.cp_ra + NB * NTL + p + 1)
                pe.wait_ge(cp_rb, START.cp_rb + NB * NTL + p + 1)
                sums(PA[p % 2], PB[p % 2], p, PT, 8, "chunk", PS[0:8 * PT, 2, :])
            pe.wait_ge(cp_rows, START.cp_rows + NB + 1)
            turn_blocks(CRp, 3, NCP)
            pe.wait_ge(cp_cols, START.cp_cols + NB + 1)
            phi(BLp, 5, NCP)
            pe.wait_ge(cp_took, START.cp_took + NB + 1)
            with pe.Fori(0, GRP) as r:
                def scores(n):
                    t = Turn(r, n, 8)
                    gp, ti, nk = pair(n)
                    for gg in range(2):
                        pe.wait_ge(pa_p, t.value(3, gg - 2, base=START.pa_p))
                        q = Qz[:, gp, gg, 128 * ti:128 * ti + 128]
                        for s, K in enumerate((KTs, KTw)):
                            mm(PS[:, 2 * gg + s, 0:nk], q, K[:, gp, 0:nk], True, False)
                            ins = mm(PS[:, 2 * gg + s, 128 * ti:nk], ident, C("causal"), False, True)
                        ins.then_inc(pa_s, 1)
                    pe.wait_ge(pa_p, t.value(3, 0, base=START.pa_p))
                    for gg in range(2):
                        out = PS[:, 7, 32 * gg:32 * gg + NCP]
                        mm(out, Qz[:, gp, gg, 128 * ti:128 * ti + 128], KCp[:, gp, 0:NCP], True, False)
                        ins = mm(out, ident, C("cmp_add")[:, 32 * ti:32 * ti + NCP], False, True)
                    ins.then_inc(pa_s, 1)

                def turns(n, b):
                    t = Turn(r, n, 8)
                    gp, ti, nk = pair(n)
                    P, what = PP[n % 2], BATCHES[b]
                    bank, before = batch(r, n, b)
                    if what is None:
                        pe.wait_ge(pa_p, t.value(3, 3, base=START.pa_p))
                        if ti == 0:
                            pe.wait_ge(pa_cm, r * 2 + (n // PT + 1))
                    else:
                        pe.wait_ge(pa_p, t.value(3, what[0] + 1, base=START.pa_p))
                    pe.wait_ge(*[(pa_td, before.value(1, 0, base=START.pa_td)), (pa_ta, before.value(1, 0, base=START.pa_ta))][bank])
                    if what is None:
                        for gg in range(2):
                            ins = turn(PS[0:NCP, 5 + bank, 128 * gg:128 * gg + 128], P[:, 2048 + 32 * gg:2048 + 32 * gg + NCP])
                    else:
                        o = 1024 * what[0] + 512 * what[1]
                        for j in range(ti + 1):
                            ins = turn(PS[:, 5 + bank, 128 * j:128 * j + 128], P[:, o + 128 * j:o + 128 * j + 128])
                    ins.then_inc(pa_t, 1)

                def outs(n, b):
                    t = Turn(r, n, 8)
                    gp, ti, nk = pair(n)
                    what = BATCHES[b]
                    bank, before = batch(r, n, b)
                    if b == 0:
                        pe.wait_ge(pa_mix, t.value(1, 0, base=START.pa_mix))
                    pe.wait_ge(*[(pa_td, before.value(1, 1, base=START.pa_td)), (pa_ta, before.value(1, 1, base=START.pa_ta))][bank])
                    if what is None:
                        for gg in range(2):
                            h = 128 * gp + 64 * gg
                            ins = mm(PS[:, 4, 64 * gg:64 * gg + 64], PTt[0:NCP, 2048 + 128 * gg:2176 + 128 * gg],
                                     VCp[0:NCP, h:h + 64])
                        ins.then_inc(pa_o, 1)
                    else:
                        gg, s = what
                        o, h, c = 1024 * gg + 512 * s, 128 * gp + 64 * gg, 128 * (s + 1) + 64 * gg
                        for j in range(ti + 1):
                            mm(PS[:, 4, c:c + 64], PTt[:, o + 128 * j:o + 128 * j + 128], P1[4 + s][:, j, h:h + 64],
                               j == 0, j == ti)

                def attend(n):
                    for b in range(len(BATCHES) + 2):
                        if b < len(BATCHES):
                            turns(n, b)
                        if b >= 2:
                            outs(n, b - 2)

                pe.wait_ge(pa_q, r * 2 + 2)
                for n in range(8):
                    scores(n)
                    if n:
                        attend(n - 1)
                attend(7)
            for t in range(PT):
                pe.wait_ge(yg, t + 1)
                pe.wait_ge(yg_c, t)
                for k in range(4):
                    ins = turn(PS[:, 6, 128 * k:128 * k + 128], MIXB[:, t, 128 * k:128 * k + 128])
                ins.then_inc(yg_t, 1)
                for k in range(4, 6):
                    ins = turn(PS[:, 7, 128 * (k - 4):128 * (k - 3)], MIXB[:, t, 128 * k:128 * k + 128])
                ins.then_inc(yg_t, 1)
            pe.wait_ge(yg_c, PT)

            def front(t, prev):
                n = t.n % 2
                pe.wait_ge(sa_qb, t.value(1, 1))
                pe.wait_ge(sa_ba, t.value(3, -3, base=START.sa_ba))
                pe.wait_ge(sa_bd, t.value(3, -3, base=START.sa_bd))
                for j in range(10):
                    pe.wait_ge(sa_fa if j % 2 == 0 else sa_fd, t.value(5, j // 2))
                    if j < 8:
                        if j % 4 == 0:
                            pe.wait_ge(sa_k[j // 4], t.value(128, 128))
                        for g in range(2):
                            for q in range(2):
                                p = 2 * j + q
                                ins = turn(PS[:, 6 + j % 2, 256 * g + 128 * q:256 * g + 128 * q + 128],
                                           SK[p // 8][:, p % 8, 128 * g:128 * g + 128])
                    else:
                        if j == 8:
                            pe.wait_ge(sa_w[n], pair_value(t, 16))
                        for p in range(4):
                            ins = turn(PS[:, 6 + j % 2, 128 * p:128 * p + 128], SWI[n][:, p, 128 * (j - 8):128 * (j - 7)])
                    ins.then_inc(sa_ft, 1)
                    if j == 1:
                        pe.wait_ge(sa_new, t.value(1, 0))
                        for g in range(2):
                            ins = mm(PS[:, 5, 0:NC], SQB[n][:, g, :],
                                     KC[:, g, bass.ds(t.at(1), 1), 0:NC].rearrange("p a n -> p (a n)"), g == 0, g == 1)
                        ins.then_inc(sa_cs, 1)
                    if j == 5:
                        pe.wait_ge(sa_cn, t.value(1, 1))
                        mm(PS[:, 5, 384:384 + NC], C("same_gt"), SPC[n][:, 0:NC]).then_inc(sa_imp, 1)

            def middle(t):
                n = t.n % 2
                pe.wait_ge(sa_fa, t.value(5, 5))
                pe.wait_ge(sa_fd, t.value(5, 5))
                pe.wait_ge(sa_mask, t.value(1, 1))
                pe.wait_ge(sa_m, t.value(2, 0, base=START.sa_m))
                pe.wait_ge(sa_p, t.value(3, 0, base=START.sa_p))
                pe.wait_ge(sa_done, t.value(1, 0, base=START.sa_done))
                for c in range(4):
                    for g in range(2):
                        mm(PS[:, c, :], SQB[n][:, g, :], SKT[:, g, 512 * c:512 * c + 512], g == 0, g == 1)
                for g in range(2):
                    mm(PS[:, 4, :], SQB[n][:, g, :], SWKT[:, g, :], g == 0, g == 1)
                for s in range(2):
                    for g in range(2):
                        ins = mm(PS[:, 5, 128 + 64 * s:192 + 64 * s], SQB[n][:, g, :], Kn[:, s, g, :], g == 0, g == 1)
                ins.then_inc(sa_s, 1)

            def back(t, fronts):
                n = t.n % 2
                sel, win, cmp = PS[:, 0, 0:256], PS[:, 0, 256:512], PS[:, 1, 0:256]
                tiles = [(SM[:, 128 * j:128 * j + 128], SV[n][:, j, :], sel, j == 0, j == NPG - 1) for j in range(NPG)]
                tiles.insert(1, (SM[:, 2048:2112], Vn[0:NS, 0, :], sel, False, False))
                tiles += [(SW[:, 128 * j:128 * j + 128], SWI[n][:, j, 256:512], win, j == 0, j == 3) for j in range(4)]
                tiles.insert(18, (SW[:, 512:576], Vn[0:NS, 1, :], win, False, False))
                tiles += [(SPC[n][:, 0:NC], VC[0:NC, bass.ds(t.at(1), 1), :].rearrange("p a c -> p (a c)"), cmp, True, True)]

                def turns(j):
                    if j < 2:
                        pe.wait_ge(sa_fa if j % 2 == 0 else sa_fd, t.value(5, 5 * fronts))
                    pe.wait_ge(sa_ba if j % 2 == 0 else sa_bd, t.value(3, j // 2, base=START.sa_ba))
                    for q, (p, _, _, _, _) in enumerate(tiles[4 * j:4 * j + 4]):
                        ins = turn(PS[0:p.shape[1], 6 + j % 2, 128 * q:128 * q + 128], p)
                    ins.then_inc(sa_bt, 1)

                pe.wait_ge(sa_p, t.value(3, 3, base=START.sa_p))
                pe.wait_ge(sa_v[n], pair_value(t, 256))
                turns(0)
                for j in range(6):
                    if j < 5:
                        turns(j + 1)
                    pe.wait_ge(sa_ba if j % 2 == 0 else sa_bd, t.value(3, j // 2 + 1, base=START.sa_ba))
                    for q, (p, v, out, first, last) in enumerate(tiles[4 * j:4 * j + 4]):
                        ins = mm(out, SPT[j % 2][0:p.shape[1], q, :], v, first, last)
                    ins.then_inc(sa_used, 1)
                pe.wait_ge(sa_mix, t.value(1, 1))
                for gp in range(2):
                    ins = turn(PS[:, 1, 128 * gp:128 * gp + 128], SO[:, 128 * gp:128 * gp + 128])
                ins.then_inc(sa_y, 1)

            pe.wait_ge(r_spread, 6)
            pe.wait_ge(pa_mix, START.pa_mix + 24)
            sample_phase(pe, front, middle, back)
            for k in range(6):
                src = P1[5][0:NS, PT, 256 + 128 * k:384 + 128 * k] if k < 2 else P1[6][0:NS, PT, 128 * (k - 2):128 * (k - 1)]
                ins = turn(PS[:, 2, 64 * k:64 * k + 64], src)
            ins.then_inc(sz_t, 1)
            pe.wait_ge(sz_done, 1)
            pe.wait_ge(ht_zero, 1)
            out_proj(HT, B_OUT1, 1)

        @block.vector
        def _(dve):
            lk = Links(dve, dve_links)
            tt, tcopy, ts = nc.vector.tensor_tensor, nc.vector.tensor_copy, nc.vector.tensor_scalar
            bc = lambda ap, n: ap.unsqueeze(len(ap.shape)).to_broadcast(list(ap.shape) + [n])

            def norm_dve(first, count, number):
                a, b = 20 + first, 20 + first + count
                dve.wait_ge(squared, first + count)
                ts(rs(a, b), rs(first, first + count), 1.0 / D, EPS, ALU.mult, ALU.add).then_inc(mean_sq, 1)
                dve.wait_ge(root, number + 1)
                nc.vector.reciprocal(rs(a, b), rs(a, b)).then_inc(rstd, 1)

            def take_h(j, outs):
                for half in range(2):
                    n = 2 * j + half
                    dve.wait_ge(h_turned, n + 1)
                    for dst, g in outs:
                        ins = tt(dst[:, 4 * half:4 * half + 4, :],
                                 PS[:, n % 4, :].rearrange("p (k c) -> p k c", k=4), bc(g[:, 4 * half:4 * half + 4], 128),
                                 ALU.mult)
                    ins.then_inc(h_taken, 1)

            nc.vector.memset(X[NS:128, PT, :], 0.0).then_inc(x_zero, 1)
            dve.wait_ge(const_in, 48)
            norm_dve(0, 7, 0)
            for j in range(7):
                if j < 2:
                    take_h(j, [(memT[l][:, :, 128 * j:128 * j + 128], S("g_mem")[:, 8 * l:8 * l + 8]) for l in range(2)])
                else:
                    take_h(j, [(HT[:, :, 128 * (j - 2):128 * (j - 1)], S("g_x")[:, 0:8])])
            def page_prod0(t, first, last):
                for k in range(first, last):
                    dve.wait_ge(cp_in[k % 2], t.value(32 * TILE, 16 * TILE * (k // 2 + 1)))
                    dve.wait_ge(cp_ra, t.value(NTL, k, base=START.cp_ra))
                    tt(tile_view(CPM[0]), tile_view(PG[k % 2]), tile_pos("tile_pos0"), ALU.mult).then_inc(cp_a, 1)
                    dve.wait_ge(cp_a, t.value(NTL, k + 1, base=START.cp_a))
                    lk.link(tt(CPM[0][:, 0:1024], CPM[0][:, 0:1024], CPM[0][:, 1024:2048], ALU.add))
                    dve.wait_ge(cp_sum, t.value(NTL, k - 1, base=START.cp_sum))
                    tt(CPR[0][k % 2], CPM[0][:, 0:512], CPM[0][:, 512:1024], ALU.add).then_inc(cp_ra, 1)



            dve.wait_ge(pad_zero, 3)
            dve.wait_ge(product, PBASE[B_C0])
            with dve.Fori(0, CT // 2) as i:
                lk.enter(i, 2 * (10 + NTL))
                for n in range(2):
                    t = Turn(i, n, 2)
                    Up, Us = U[n][:, 0:514], U[n][:, 514:594].rearrange("p (b c) -> p b c", b=NB)
                    Yp, Ys = Y[:, 0:512], Y[:, 512:576].rearrange("p (b c) -> p b c", b=NB)
                    sb = Sb.rearrange("p (q b c) -> p q b c", q=4, b=NB)
                    wj = lambda j: small[:, bass.ds(t.at(3, SMALL["conv_w"][0] + j), 1)]
                    page_prod0(t, 0, 2)
                    dve.wait_ge(product, t.value(4, 2, base=PBASE[B_CONV]))
                    dve.wait_ge(c_copied, t.value(1, 1, base=START.c_copied))
                    dve.wait_ge(state_set, t.value(1, 1))
                    dve.wait_ge(state_kept, t.value(2, -2, base=START.state_kept))
                    tt(Up[:, 2:514], Cb[:, 0:512], PS[:, 1, :], ALU.mult).then_inc(u_made, 1)
                    dve.wait_ge(u_made, t.value(2, 1, base=START.u_made))
                    tcopy(CS[:, bass.ds(t.at(18), 2)], Up[:, 512:514]).then_inc(state_kept, 1)
                    lk.link(ts(Yp, Up[:, 0:512], wj(0), None, ALU.mult))
                    for j in (1, 2):
                        lk.link(nc.vector.scalar_tensor_tensor(Yp, Up[:, j:j + 512], wj(j), Yp, ALU.mult, ALU.add))
                    page_prod0(t, 2, NTL)
                    dve.wait_ge(product, t.value(4, 3, base=PBASE[B_CONV]))
                    tt(Yp, Yp, PS[:, 2, :], ALU.mult).then_inc(b_used, 1)

                    dve.wait_ge(s_copied, t.value(1, 1, base=START.s_copied))
                    tt(Us[:, :, 2:10], sb[:, 0], sb[:, 1], ALU.mult).then_inc(u_made, 1)
                    dve.wait_ge(u_made, t.value(2, 2, base=START.u_made))
                    tcopy(CS[:, bass.ds(t.at(18, 2), 16)].rearrange("p (b c) -> p b c", b=NB), Us[:, :, 8:10]
                          ).then_inc(state_kept, 1)
                    lk.link(ts(Ys, Us[:, :, 0:8], wj(0), None, ALU.mult))
                    for j in (1, 2):
                        lk.link(nc.vector.scalar_tensor_tensor(Ys, Us[:, :, j:j + 8], wj(j), Ys, ALU.mult, ALU.add))
                    lk.did(tt(Ys, Ys, sb[:, 2], ALU.mult))
                    dve.wait_ge(z_exp, t.value(1, 1))
                    lk.link(ts(E, E, 1.0, None, ALU.add))
                    lk.link(nc.vector.reciprocal(E, E))
                    lk.did(tt(E[:, 0:512], E[:, 0:512], PS[:, 3, :], ALU.mult))
                    tt(E[:, 512:576], E[:, 512:576], Sb[:, 192:256], ALU.mult).then_inc(z_used, 1)
                    dve.wait_ge(z_used, t.value(1, 1, base=START.z_used))
                    dve.wait_ge(b_used, t.value(1, 1, base=START.b_used))
                    lk.settle()
                    tt(YT0f[:, bass.ds(t.at(TOK, 2 * TOK), 576)], Y, E, ALU.mult).then_inc(conv_y, 1)
                lk.leave(CT // 2)

            def mem_prompt_dve(l):
                b_ = mem_bufs(l)
                P0 = MQG0 if l == 0 else P1[0]
                dve.wait_ge(sig_exp, l + 1)
                lk.link(ts(b_["MG"], b_["MG"], 1.0, None, ALU.add))
                lk.link(nc.vector.reciprocal(b_["MG"], b_["MG"]))
                lk.link(tt(P0[:, :, 256:512], P0[:, :, 256:512], b_["MG"], ALU.mult))
                for n in range(PT):
                    T = l * PT + n
                    pr = n % 2
                    if n:
                        dve.wait_ge(ma_qt, T)
                    ts(b_["QS"], P0[:, n, 0:256], SCALE, None, ALU.mult).then_inc(ma_q, 1)
                    dve.wait_ge(ma_s, T + 1)
                    for k in range(2):
                        nc.vector.tensor_reduce(stats[:, 60 + 8 * pr + k:63 + 8 * pr + k:2],
                                                PS[:, 2 * pr + k, :].rearrange("p (h m) -> p h m", h=2), AX, ALU.max,
                                                negate=True).then_inc(ma_m, 1)
                    dve.wait_ge(ma_t, 2 * T + 1)
                    if T:
                        dve.wait_ge(ma_o, T)
                    tcopy(b_["PT"][:, 0:512], PS[:, 6, :]).then_inc(ma_td, 1)
                    dve.wait_ge(ma_p, 4 * (T + 1))
                    lk.link(nc.vector.reciprocal(rs(92, 96), rs(76 + 8 * pr, 80 + 8 * pr)))
                    dve.wait_ge(ma_o, T + 1)
                    if n:
                        dve.wait_ge(ma_yt, T)
                    OY = b_["OY"].rearrange("p (h c) -> p h c", h=4)
                    lk.link(tt(OY, PS[:, 4, 256 * pr:256 * pr + 256].rearrange("p (h c) -> p h c", h=4),
                               bc(rs(92, 96), 64), ALU.mult))
                    tt(b_["OY"], b_["OY"], P0[:, n, 256:512], ALU.mult).then_inc(ma_y, 1)

            def mem_sample_dve(l, YT):
                b_ = mem_bufs(l)
                YTf = HTf if l else YT0f
                P0 = MQG0 if l == 0 else P1[0]
                dve.wait_ge(ma_qt, PT * (l + 1))
                ts(b_["QS"], P0[:, PT, 0:256], SCALE, None, ALU.mult).then_inc(ms_q, 1)
                dve.wait_ge(ms_qt, l + 1)
                dve.wait_ge(ms_qz, 5 * l + 1)
                for h in range(4):
                    o = 64 * (h % 2)
                    tcopy(b_["QZ"][o:o + 64, h // 2, :, 32 * h:32 * h + 8],
                          PS[o:o + 64, 5, 128 * (h // 2):128 * (h // 2) + 64].rearrange("p (b t) -> p b t", b=NB)
                          ).then_inc(ms_qz, 1)
                with dve.Fori(0, NB // 2) as i:
                    lk.enter(i, 2 * 4)
                    for n in range(2):
                        t = Turn(i, n, 2)
                        v = lambda plus: t.value(1, plus, base=NB * l)
                        dve.wait_ge(ms_s, v(START.ms_s + 1))
                        nc.vector.tensor_reduce(rs(100 + n, 101 + n), PS[:, n, 0:256], AX, ALU.max, negate=True
                                                ).then_inc(ms_m, 1)
                        dve.wait_ge(ms_t, v(1))
                        tcopy(b_["SPT"][n], PS[:, 7, 0:256]).then_inc(ms_c, 1)
                        dve.wait_ge(ms_p, v(1))
                        lk.link(nc.vector.reciprocal(rs(108 + n, 109 + n), rs(104 + n, 105 + n)))
                        dve.wait_ge(ms_o, v(START.ms_o + 1))
                        dve.wait_ge(ms_y, v(START.ms_y - 1))
                        ts(b_["SO"][n], PS[:, 2 + n, 0:256], rs(108 + n, 109 + n), None, ALU.mult).then_inc(ms_n, 1)
                        dve.wait_ge(ms_y, v(START.ms_y + 1))
                        for h in range(4):
                            o, g = 64 * (h % 2), h // 2
                            ins = tcopy(YTf[o:o + 64, bass.ds(t.at(NT, g * TOK + SEQ), NT)],
                                        PS[o:o + 64, 4, 128 * g + 32 * h:128 * g + 32 * h + NT])
                            if h < 3:
                                lk.did(ins)
                        ins.then_inc(ms_done, 1)
                    lk.leave(NB // 2)
                lk.settle()
                dve.wait_ge(ms_g, l + 1)
                dve.wait_ge(ms_done, START.ms_done + NB * (l + 1))
                tt(YT[:, 0:2, SEQ:SEQ + NS], YT[:, 0:2, SEQ:SEQ + NS],
                   PS[:, 5, 0:256].rearrange("p (g c) -> p g c", g=2)[:, :, 0:NS], ALU.mult).then_inc(ms_gm, 1)

            def add_out(first, l):
                for n in range(2):
                    pages = Turn(0, CT + n, 1)
                    for t in range(TT):
                        if l == 0 and t < PT:
                            page_prod0(pages, t, t + 1)

                        dve.wait_ge(product, PBASE[first + n] + t + 1)
                        xs = X[:, t, 512 * n:512 * n + 512]
                        tt(xs, xs, PS[:, t, :], ALU.add).then_inc(out_added, 1)

            mem_prompt_dve(0)
            mem_sample_dve(0, YT0)
            add_out(B_OUT0, 0)
            norm_dve(7, TT, 1)
            for j in range(TT):
                take_h(7 + j, [(HT[:, :, 128 * j:128 * j + 128], S("g_x")[:, 8:16])])
            Z5 = sig[:, 0:1280].rearrange("p (t c) -> p t c", t=TT)
            Z6 = sig[:, 1280:3840].rearrange("p (t c) -> p t c", t=TT)
            dve.wait_ge(gates_taken, 1)
            lk.link(ts(Gate, Gate, 1.0, None, ALU.add))
            nc.vector.reciprocal(Gate, Gate).then_inc(sig_done, 1)
            for n, (z, dst) in enumerate(((Z5, P1[5][:, :, 256:512]), (Z6, P1[6][:, :, :]))):
                dve.wait_ge(z_exp, CT + n + 1)
                lk.link(ts(z, z, 1.0, None, ALU.add))
                lk.link(nc.vector.reciprocal(z, z))
                tt(dst, dst, z, ALU.mult).then_inc(sig_done, 1)
            def rope(c, h0, nh):
                v = P1[c][:, :, 64 * h0:64 * (h0 + nh)].rearrange("p t (h d) -> p t h d", h=nh)
                x1, x2 = v[:, :, :, 0:8], v[:, :, :, 8:16]
                cs, sn = [C(k).rearrange("p (t d) -> p t d", t=TT).unsqueeze(2).to_broadcast([128, TT, nh, 8])
                          for k in ("cos", "sin")]
                tmp = [r[:, 0:TT * nh * 8].rearrange("p (t h d) -> p t h d", t=TT, h=nh) for r in rope_t]
                lk.did(tt(tmp[0], x1, cs, ALU.mult))
                lk.did(tt(tmp[1], x2, sn, ALU.mult))
                lk.did(tt(tmp[2], x2, cs, ALU.mult))
                lk.link(tt(tmp[3], x1, sn, ALU.mult))
                lk.did(tt(x1, tmp[0], tmp[1], ALU.subtract))
                lk.link(tt(x2, tmp[2], tmp[3], ALU.add))

            mem_prompt_dve(1)
            mem_sample_dve(1, HT)
            for c, h0, nh in ((1, 0, 8), (2, 0, 8), (3, 4, 4), (4, 4, 4)):
                rope(c, h0, nh)
            for s in range(2):
                ins = tcopy(Vn[0:NS, s, :], P1[4 + s][0:NS, PT, 0:256])
                if s == 0:
                    lk.did(ins)
                else:
                    ins.then_inc(roped, 4)
            dve.wait_ge(qz_zero, 2)
            dve.wait_ge(r_turned, 11)
            for g in range(KVH):
                o, gp = 64 * (g % 2), g // 2
                for r in range(GRP):
                    ins = ts(QZ[o:o + 64, gp, :, 32 * g + 8 * r:32 * g + 8 * r + 8],
                             PS[o:o + 64, 6, 64 * (2 * r + gp):64 * (2 * r + gp) + 64].rearrange("p (b t) -> p b t", b=NB),
                             SCALE, None, ALU.mult)
                ins.then_inc(r_spread, 1)
            dve.wait_ge(r_turned, 12)
            tcopy(Kn.rearrange("p s g n -> p (s g n)"), PS[:, 7, 0:256]).then_inc(r_spread, 2)
            for p in range(PT):
                if p >= 2:
                    dve.wait_ge(cp_sum, NB * NTL + START.cp_sum + p - 1)
                tt(heads(PA[p % 2][:, 0:256]), heads(P1[2][:, p, 256:512]), row_pos("pos0", 0), ALU.mult)
                tt(heads(PA[p % 2][:, 256:512]), heads(P1[3][:, p, 0:256]), row_pos("pos0", 1), ALU.mult
                   ).then_inc(cp_ra, 1)


            dve.wait_ge(cp_sum, PT + NB * NTL + START.cp_sum)
            dve.wait_ge(r_took, 10)
            stt = nc.vector.scalar_tensor_tensor
            lk.link(nc.vector.memset(Qz, 0.0))
            with dve.Fori(0, GRP) as r:
                lk.enter(r, 8 * 4)
                dve.wait_ge(pa_s, START.pa_s + r * 24)
                for gg in range(2):
                    o = 64 * gg
                    tcopy(Qz[o:o + 64, :, gg, :],
                          QTf[o:o + 64, bass.ds(r * 1024, 1024)].rearrange("p (g c) -> p g c", g=2)).then_inc(pa_q, 1)

                def maxes(n):
                    t = Turn(r, n, 8)
                    gp, ti, nk = pair(n)
                    m = 200 + 8 * (n % 2)
                    for gg in range(2):
                        dve.wait_ge(pa_s, t.value(3, gg + 1, base=START.pa_s))
                        nc.vector.tensor_reduce(rs(m + 2 + gg, m + 5 + gg)[:, 0:3:2], PS[:, 2 * gg:2 * gg + 2, 0:nk], AX, ALU.max,
                                                negate=True).then_inc(pa_m, 1)
                    dve.wait_ge(pa_s, t.value(3, 3, base=START.pa_s))
                    nc.vector.tensor_reduce(rs(m, m + 2), PS[:, 7, 0:64].rearrange("p (g n) -> p g n", g=2)[:, :, 0:NCP],
                                            AX, ALU.max, negate=True).then_inc(pa_m, 1)

                def cmp_mask(n):
                    m = 220 + 8 * (n % 2)
                    dve.wait_ge(pa_p, Turn(r, n, 8).value(3, 3, base=START.pa_p))
                    for gg in range(2):
                        c = PP[n % 2][:, 2048 + 32 * gg:2048 + 32 * gg + NCP]
                        ins = nc.vector.tensor_tensor_reduce(c, c, C("cmp_mul")[:, 0:NCP], 1.0, 0.0, ALU.mult,
                                                             ALU.add, rs(m + gg, m + gg + 1))
                    ins.then_inc(pa_cm, 1)

                def took(n):
                    gp, ti, nk = pair(n)
                    dve.wait_ge(pa_o, Turn(r, n, 8).value(1, 0, base=START.pa_o))
                    for b, what in enumerate(BATCHES):
                        bank, before = batch(r, n, b)
                        if bank == 0:
                            dve.wait_ge(pa_t, Turn(r, n, 8).value(5, b + 1, base=START.pa_t))
                            if what is None:
                                tcopy(PTt[0:NCP, 2048:2304], PS[0:NCP, 5, 0:256]).then_inc(pa_td, 1)
                            else:
                                o = 1024 * what[0] + 512 * what[1]
                                tcopy(PTt[:, o:o + nk], PS[:, 5, 0:nk]).then_inc(pa_td, 1)

                def mix(n):
                    t = Turn(r, n, 8)
                    gp, ti, nk = pair(n)
                    m = 220 + 8 * (n % 2)
                    if ti == 0:
                        dve.wait_ge(pa_cm, r * 2 + (n // PT + 1))
                    lk.link(ts(rs(240, 246), rs(m, m + 6), 1e-30, None, ALU.max))
                    lk.link(nc.vector.reciprocal(rs(240, 246), rs(240, 246)))
                    gate = Gate[:, ti, :].rearrange("p (s h) -> p s h", s=3)[:, :, bass.ds(r * KVH + 2 * gp, 2)]
                    lk.link(tt(rs(250, 256).rearrange("p (s g) -> p s g", s=3), rs(240, 246).rearrange("p (s g) -> p s g", s=3),
                               gate, ALU.mult))
                    dve.wait_ge(pa_o, t.value(1, 1, base=START.pa_o))
                    lk.link(tt(Om.rearrange("p (h d) -> p h d", d=HD), PS[:, 4, 0:384].rearrange("p (h d) -> p h d", d=HD),
                               bc(rs(250, 256), HD), ALU.mult))
                    nc.vector.tensor_reduce(MIXf[:, bass.ds(r * 256 + (MIX * ti + 128 * gp), 128)],
                                            Om.rearrange("p (s x) -> p x s", s=3), AX, ALU.add).then_inc(pa_mix, 1)

                for n in range(8):
                    maxes(n)
                    if n:
                        took(n - 1)
                    if n % PT == 0:
                        cmp_mask(n)
                    if n:
                        mix(n - 1)
                took(7)
                mix(7)
                lk.leave(GRP)
            dve.wait_ge(pa_mix, START.pa_mix + 24)
            for t in range(PT):
                lk.did(tt(MIXB[:, t, 0:256], MIXB[:, t, 0:256], P1[5][:, t, 256:512], ALU.mult))
                tt(MIXB[:, t, 256:768], MIXB[:, t, 256:768], P1[6][:, t, :], ALU.mult).then_inc(yg, 1)

            def front(t, prev):
                n = t.n % 2
                def took(j):
                    dve.wait_ge(sa_ft, t.value(10, j + 1, base=START.sa_ft))
                    if j < 8:
                        tcopy(SKT[:, :, 256 * j:256 * j + 256], PS[:, 7, :].rearrange("p (g c) -> p g c", g=2)
                              ).then_inc(sa_fd, 1)
                    else:
                        tcopy(SWKT[:, 1, :], PS[:, 7, :]).then_inc(sa_fd, 1)

                took(1)
                dve.wait_ge(sa_cs, t.value(1, 1))
                nc.vector.tensor_reduce(rs(140, 141), PS[:, 5, 0:NC], AX, ALU.max, negate=True).then_inc(sa_cm, 1)
                took(3)
                dve.wait_ge(sa_ce, t.value(1, 1))
                lk.link(ts(rs(155, 156), rs(141, 142), 1e-30, None, ALU.max))
                lk.link(nc.vector.reciprocal(rs(155, 156), rs(155, 156)))
                ts(SPC[n][:, 0:NC], SPC[n][:, 0:NC], rs(155, 156), None, ALU.mult).then_inc(sa_cn, 1)
                took(5)
                dve.wait_ge(sa_imp, t.value(1, 1))
                lk.link(tcopy(SIMP[:, 1:1 + NC], PS[:, 5, 384:384 + NC]))
                lk.link(tt(SCH, SIMP[:, 1:129], SIMP[:, 0:128], ALU.add))
                lk.link(nc.vector.tensor_reduce(SSC[:, 0:NSB - 1], SCH.rearrange("p (n c) -> p n c", c=4), AX, ALU.add))
                lk.link(tt(SS2[:, 0:NSB], SSC[:, 0:NSB], C("forced")[:, 0:NSB], ALU.add))
                for k in range(2):
                    step_dve()
                    lk.link(nc.vector.max(SM8, SS2[:, 0:NSB]))
                    step_dve()
                    lk.link(nc.vector.match_replace(SS2[:, 0:NSB], SM8, SS2[:, 0:NSB], -1.0))
                ts(SMB[:, 0:NSB], SS2[:, 0:NSB], 0.0, NEG, ALU.is_ge, ALU.mult).then_inc(sa_mask, 1)
                took(7)
                took(9)

            def middle(t):
                lk.settle()
                dve.wait_ge(sa_mask, t.value(1, 1))
                dve.wait_ge(sa_s, t.value(1, 1, base=START.sa_s))
                dve.wait_ge(sa_bt, t.value(6, 0, base=START.sa_bt))
                ttr = nc.vector.tensor_tensor_reduce
                lk.did(tcopy(SNM, cst[:, bass.ds(t.at(-NT, CONST["new_add"][0] + NT * (NB - 1)), 64)]))
                lk.link(tt(PS[:, 4, 0:8], PS[:, 4, 0:8], C("win_add"), ALU.add))
                step_dve()
                lk.did(ttr(SM[:, 2048:2112], PS[:, 5, 128:192], SNM, 1.0, -3e38, ALU.add, ALU.max, rs(146, 147)))
                ttr(SW[:, 512:576], PS[:, 5, 192:256], SNM, 1.0, -3e38, ALU.add, ALU.max, rs(148, 149)).then_inc(sa_new, 1)
                for c in range(4):
                    lk.did(ttr(SM[:, 512 * c:512 * c + 512].rearrange("p (n k) -> p n k", k=SB),
                               PS[:, c, :].rearrange("p (n k) -> p n k", k=SB), bc(SMB[:, 8 * c:8 * c + 8], SB), 1.0, -3e38,
                               ALU.add, ALU.max, rs(142 + c, 143 + c)))
                dve.wait_ge(sa_new, t.value(1, 1))
                lk.link(nc.vector.tensor_reduce(rs(147, 148), PS[:, 4, :], AX, ALU.max))
                nc.vector.tensor_reduce(rs(150, 151), rs(142, 147), AX, ALU.max, negate=True).then_inc(sa_m, 1)
                nc.vector.tensor_reduce(rs(151, 152), rs(147, 149), AX, ALU.max, negate=True).then_inc(sa_m, 1)

            def back(t, fronts):
                for j in range(1, 6, 2):
                    dve.wait_ge(sa_bt, t.value(6, j + 1, base=START.sa_bt))
                    dve.wait_ge(sa_used, t.value(6, j - 1, base=START.sa_used))
                    k = 4 if j < 5 else 3
                    tcopy(SPT[1][:, 0:k, :], PS[:, 7, 0:128 * k].rearrange("p (s c) -> p s c", s=k)).then_inc(sa_bd, 1)
                dve.wait_ge(sa_p, t.value(3, 3, base=START.sa_p))
                lk.link(tt(rs(153, 154), rs(153, 154), rs(154, 155), ALU.add))
                lk.link(ts(rs(156, 158), rs(152, 154), 1e-30, None, ALU.max))
                lk.link(nc.vector.reciprocal(rs(156, 158), rs(156, 158)))
                gr = Grow[:, bass.ds(t.at(1), 1), :].squeeze(1)
                lk.did(tcopy(rs(170, 173), gr))
                lk.link(tt(rs(158, 160), rs(156, 158), gr[:, 1:3], ALU.mult))
                dve.wait_ge(sa_used, t.value(6, 6, base=START.sa_used))
                dve.wait_ge(sa_y, t.value(1, 0, base=START.sa_y))
                lk.link(ts(SO, PS[:, 1, 0:256], rs(170, 171), None, ALU.mult))
                lk.link(stt(SO, PS[:, 0, 0:256], rs(158, 159), SO, ALU.mult, ALU.add))
                stt(SO, PS[:, 0, 256:512], rs(159, 160), SO, ALU.mult, ALU.add).then_inc(sa_mix, 1)
                dve.wait_ge(sa_y, t.value(1, 1, base=START.sa_y))
                for g in range(KVH):
                    o, gp = 64 * (g % 2), g // 2
                    ins = tcopy(HT[o:o + 64, 2 + gp:7 + gp:2, bass.ds(t.at(NT, SEQ), NT)],
                                PS[o:o + 64, 1, 128 * gp + 32 * g:128 * gp + 32 * g + 24].rearrange("p (r t) -> p r t", r=GRP))
                    if g < 3:
                        lk.did(ins)
                ins.then_inc(sa_done, 1)

            dve.wait_ge(kv_stored, 16 * (2 * 3 + 2 * 2 + 2 * NB))
            dve.wait_ge(gates_back, 16 * 36)
            dve.wait_ge(yg_c, PT)
            lk.did(nc.vector.memset(SIMP, 0.0))
            lk.link(nc.vector.memset(SSC, 0.0))
            sample_phase(dve, front, middle, back, lk)
            dve.wait_ge(sz_t, 1)
            dve.wait_ge(sa_done, START.sa_done + NB)
            tt(HT[:, 2:8, SEQ:SEQ + NS], HT[:, 2:8, SEQ:SEQ + NS], PS[:, 2, 0:384].rearrange("p (k c) -> p k c", k=6),
               ALU.mult).then_inc(sz_done, 1)
            add_out(B_OUT1, 1)
            norm_dve(12, TT, 2)
            dve.wait_ge(gfin_in, 16)
            for t in range(TT):
                dve.wait_ge(fin_scaled, t + 1)
                if t >= 2:
                    dve.wait_ge(y_out[t % 2], 16 * (t // 2))
                tt(fin[t % 2], H[t % 2], gfin, ALU.mult).then_inc(y_ready, 1)


def w_count(n):
    return 16 * (n // 2 + 1)


def pair_value(t, each):
    return t.i * each + (t.n // 2 + 1) * each


def constants():
    c = np.zeros((128, CONST_W), np.float32)
    p = np.arange(128)

    def put(name, v):
        a, w = CONST[name]
        c[:, a:a + w] = v

    put("ident", np.eye(128))
    put("causal", np.where(p[None, :] <= p[:, None], 0.0, NEG))
    q_pos = p[:, None, None] + 128 * np.arange(PT)[None, :, None]
    seen = (16 * np.arange(32)[None, None, :] + 31 <= q_pos).reshape(128, 128)
    put("cmp_add", np.where(seen, 0.0, NEG))
    put("cmp_mul", seen)
    real = p % 32 < 24
    put("same_gt", (p[:, None] // 32 == p[None, :] // 32) & (p[:, None] % 8 == p[None, :] % 8) & real[:, None] & real[None, :])
    new = np.full((128, 15, 8), NEG)
    new[:, NB - 1, :] = np.where(np.arange(8)[None, :] <= p[:, None] % 8, 0.0, NEG)
    put("new_add", new.reshape(128, 120))
    put("win_add", np.where(np.arange(8)[None, :] <= p[:, None] % 8, NEG, 0.0))
    put("chunk", p[:, None] // 16 + 8 * (PT - 1) == np.arange(58)[None, :])
    put("chunk4", p[:, None] // 4 + 8 * TILE * (NTL - 1) == np.arange(226)[None, :])
    pos = (p[:, None] + 128 * np.arange(TT)[None, :]).astype(np.float32)
    pos[:, PT] = PAST + p % NT
    inv = (np.float32(500000.0) ** (-np.arange(8, dtype=np.float32) * np.float32(2.0) / np.float32(16))).astype(np.float32)
    ang = (pos[:, :, None] * inv).astype(np.float32)
    put("cos", np.cos(ang).reshape(128, 40))
    put("sin", np.sin(ang).reshape(128, 40))
    forced = np.zeros(NSB + 1)
    forced[[0, NSB - 2, NSB - 1]] = 1e4
    put("forced", forced)
    return c


def lay_out(x):
    f = {k: np.asarray(v) for k, v in x.items()}
    out = {"xp": f["x_prompt"][0], "xs": f["x_sample"].reshape(NS, D), "mem": f["mem_prompt"][0],
           "cmem": f["cache_mem_kv"].reshape(2, NB, NMEM, 512), "ccmp": f["cache_cmp_kv"].reshape(POOL, PAGE, 512),
           "csel": f["cache_sel_kv"].reshape(POOL, PAGE, 512), "pages": f["page_table"].reshape(1, NB * NPG),
           "win": f["state_win_kv"].reshape(NB, WIN, 512), "const": constants()}

    def rgd(a, axis):
        sh = a.shape
        a = a.reshape(sh[:axis] + (KVH, GRP, sh[axis] // 12) + sh[axis + 1:])
        return np.swapaxes(a, axis, axis + 1).reshape(sh)

    wc, wn, wo = f["w_in_conv"][0], f["w_in_nsa"][0], f["w_out"]
    blocks = [f["w_mem_kv"][0], f["w_mem_kv"][1], wc[:, 0:512]]
    for i in range(CT):
        blocks.append(np.concatenate([wc[:, 512 + MIX * q + 128 * i:640 + MIX * q + 128 * i] for q in (1, 2, 0, 3)], 1))
    blocks += [wo[0][:, 0:512], wo[0][:, 512:1024]]
    q, kv, gl, z = wn[:, 512:1280], wn[:, 1280:2816], wn[:, 2816:2852], wn[:, 2852:3620]
    n = np.concatenate([wn[:, 0:512], rgd(q, 1), kv, rgd(z, 1)], 1)
    blocks += [n[:, 512 * c:512 * c + 512] for c in range(7)]
    w1 = np.concatenate([wo[1][0:256], rgd(wo[1][256:], 0)], 0)
    blocks += [w1[:, 0:512], w1[:, 512:1024]]
    out["wall"] = np.stack([b.reshape(KD, 128, 512).transpose(1, 0, 2).reshape(128, KD * 512) for b in blocks])
    g = gl.reshape(D, 3, KVH, GRP).swapaxes(2, 3).reshape(KD, 128, 36)
    out["wg"] = g.transpose(1, 0, 2).reshape(128, KD * 36)
    parts = {
        "g_mem": f["mem_norm_g"].reshape(2, KD, 128).transpose(2, 0, 1).reshape(128, 16),
        "g_x": f["norm_g"].reshape(2, KD, 128).transpose(2, 0, 1).reshape(128, 16),
        "conv_w": f["conv_w"][0].reshape(3, CT, 128).transpose(2, 1, 0).reshape(128, 18),
        "state": f["state_conv"][0].reshape(NB, 2, CT, 128).transpose(3, 2, 0, 1).reshape(128, CT * 16),
    }
    pos = f["cmp_pos_w"][0].reshape(2, 2, 16, HD)
    for m in range(2):
        w = pos[:, m].transpose(1, 0, 2).reshape(16, 2 * HD)
        parts[f"pos{m}"] = np.tile(w, (8, 1))
        parts[f"tile_pos{m}"] = np.tile(w.reshape(4, 4 * 2 * HD), (32, 1))
    for s, name in enumerate(("phi_k", "phi_v")):
        d = np.zeros((128, 128), np.float32)
        for k in range(2):
            d[64 * k:64 * k + 64, 64 * k:64 * k + 64] = f["cmp_phi"][0, s]
        parts[name] = d
    out["small"] = np.concatenate([parts[k] for k in SMALL], 1)
    out["gfin"] = np.broadcast_to(f["final_norm_g"][None, :], (128, D))
    return {k: np.ascontiguousarray(v) for k, v in out.items()}


OUTS = {"yp": (SEQ, D), "ys": (NS, D), "conv": (128, CT * 18), "cmp_p": (SEQ, 512), "sel_p": (SEQ, 512),
        "win_p": (SEQ, 512), "mem": (2, NMEM, 512), "cmp_s": (NS, 512), "sel_s": (NS, 512), "win_s": (NB, WIN, 512)}


def kernel(**inputs):
    import concourse.bacc as bacc
    from concourse.bass_utils import run_bass_kernel_spmd

    arrays = {"in_" + k: v for k, v in lay_out(inputs).items()}
    nc = bacc.Bacc("TRN2", target_bir_lowering=False, num_devices=1)
    I = {k[3:]: nc.dram_tensor(k, v.shape, I32 if v.dtype == np.int32 else F32, kind="ExternalInput").ap()
         for k, v in arrays.items()}
    O = {k: nc.dram_tensor("out_" + k, s, F32, kind="ExternalOutput").ap() for k, s in OUTS.items()}
    build(nc, I, O)
    r = run_bass_kernel_spmd(nc, [arrays], core_ids=[0]).results[0]
    r = {k: r["out_" + k] for k in OUTS}
    conv = r["conv"].reshape(128, CT, 18)
    kv = lambda a, *s: a.reshape(*s, 2, KVH, HD)
    conv_p = conv[:, :, 0:2].transpose(2, 1, 0).reshape(1, 1, 2, MIX)
    conv_s = conv[:, :, 2:18].reshape(128, CT, NB, 2).transpose(2, 3, 1, 0).reshape(1, NB, 2, MIX)
    return (r["yp"].reshape(1, SEQ, D), r["ys"].reshape(NB, NT, D), conv_p,
            kv(r["cmp_p"], 1, 1, SEQ), kv(r["sel_p"], 1, 1, SEQ), kv(r["win_p"], 1, 1, SEQ),
            r["mem"].reshape(2, 1, NMEM, 2, 4, HD), conv_s,
            kv(r["cmp_s"], 1, NB, NT), kv(r["sel_s"], 1, NB, NT), kv(r["win_s"], 1, NB, WIN))
```

```python
from contextlib import ExitStack

import numpy as np
import concourse.bass as bass
from concourse import mybir

F32 = mybir.dt.float32
I32 = mybir.dt.int32
ALU = mybir.AluOpType
ACT = mybir.ActivationFunctionType
AX = mybir.AxisListType.X

D = 1024
KD = D // 128
SEQ = 512
NB, NT = 8, 8
NS = NB * NT
PT = SEQ // 128
TT = PT + 1
TOK = TT * 128
PAST = 2048
PAGE = 128
NPG = PAST // PAGE
TILE = 4
NTL = NPG // TILE
POOL = 160
HD = 64
MIX = 768
CT = MIX // 128
NMEM = 256
KVH = 4
GRP = 3
SB = 64
NSB = PAST // SB + 1
NC = PAST // 16 - 1
NCP = SEQ // 16 - 1
WIN = 512
NEG = -1e30
SCALE = HD ** -0.5
ARENA = 53080


class START:
    cp_a = 3
    cp_b = 3
    cp_ra = 1
    cp_rb = 1
    cp_sum = 3
    conv_y = 2
    ms_s = 2
    ms_kt = 2
    u_made = 1
    pa_t = 6
    pa_o = 1
    sa_bt = 7
    c_copied = 1
    s_copied = 1
    b_used = 1
    z_used = 1
    ms_kc = 1
    ms_c = 1
    ms_done = 1
    cp_rows = 1
    cp_cols = 1
    cp_took = 1
    pa_p = 4
    pa_mix = 1
    pa_ta = 1
    pa_td = 2
    sa_ba = 4
    sa_bd = 4
    sa_m = 1
    sa_p = 1
    sa_done = 1
    state_kept = 3
    ms_y = 2
    sa_y = 1
    pa_s = 1
    sa_used = 7
    sa_ft = 7
    sa_s = 2
    ms_o = 2


FRONT = "AAAAADDAAA"
LINKS_OF_TURN = 28
EPS = 1e-6

CONST = {}
CONST_W = 0
for _n, _w in [("ident", 128), ("causal", 128), ("cmp_add", 128), ("cmp_mul", 128), ("same_gt", 128),
               ("new_add", 120), ("win_add", 8), ("chunk", 58), ("chunk4", 226), ("cos", 40), ("sin", 40),
               ("forced", NSB + 1)]:
    CONST[_n] = (CONST_W, _w)
    CONST_W += _w
SMALL = {}
SMALL_W = 0
for _n, _w in [("g_mem", 16), ("g_x", 16), ("conv_w", CT * 3), ("state", CT * 16), ("pos0", 128), ("pos1", 128),
               ("tile_pos0", 512), ("tile_pos1", 512),
               ("phi_k", 128), ("phi_v", 128)]:
    SMALL[_n] = (SMALL_W, _w)
    SMALL_W += _w

B_KV, B_C0, B_CONV, B_OUT0, B_N, B_OUT1 = 0, 2, 3, 9, 11, 18
NBLK = 20
TILES_OF = [2, 2, 5] + [4] * CT + [5, 5] + [5] * 7 + [5, 5]
PBASE = [sum(TILES_OF[:n]) + (5 if n >= B_OUT1 else 0) for n in range(NBLK + 1)]
P_GATES = sum(TILES_OF[:B_OUT1])
KV_STORED = 16 * (2 * 3 + 2 * 2 + 2 * NB)
CHUNK_ORDER = [4, 0, 5, 1, 6, 2, 3]


class Turn:

    def __init__(self, i, n, per):
        self.i, self.n, self.per = i, n, per

    def value(self, each, plus, base=0):
        rest = base + each * self.n + plus
        if isinstance(self.i, int):
            return self.i * self.per * each + rest
        assert rest > 0
        return self.i * (self.per * each) + rest

    def at(self, stride, plus=0):
        return self.i * (self.per * stride) + (self.n * stride + plus)


class Links:

    def __init__(self, eng, sem):
        self.eng, self.sem, self.n, self.i, self.per = eng, sem, 0, None, 0

    def did(self, ins):
        ins.then_inc(self.sem, 1)
        self.n += 1

    def settle(self):
        self.eng.wait_ge(self.sem, self.n if self.i is None else self.i * self.per + self.n)

    def link(self, ins):
        self.did(ins)
        self.settle()

    def enter(self, i, per):
        self.i, self.per, self.start = i, per, self.n

    def leave(self, trips):
        assert self.n - self.start == self.per, (self.n - self.start, self.per)
        self.i, self.n = None, self.start + trips * self.per


def build(nc, I, O):
    ctx = ExitStack()
    with ctx:
        def sem(name):
            return ctx.enter_context(nc.semaphore(name))

        arena = ctx.enter_context(nc.sbuf_tensor("arena", [128, ARENA], F32))
        ptab = ctx.enter_context(nc.sbuf_tensor("ptab", [1, NB * NPG], I32))
        PS = ctx.enter_context(nc.psum_tensor("PS", [128, 8, 512], F32))
        gates_dram = nc.dram_tensor("gates_scratch", [NS, 36], F32, kind="Internal").ap()

        top = [0]

        def keep(n):
            a = arena[:, top[0]:top[0] + n]
            top[0] += n
            return a

        X = keep(TT * D).rearrange("p (t c) -> p t c", t=TT)
        HT = keep(KD * TOK).rearrange("p (k c) -> p k c", k=KD)
        KC = keep(2 * NB * 128).rearrange("p (g b n) -> p g b n", g=2, b=NB)
        VC = keep(NB * 256).rearrange("p (b c) -> p b c", b=NB)
        KCp = keep(64).rearrange("p (g n) -> p g n", g=2)
        VCp = keep(256)
        cst = keep(CONST_W)
        small = keep(SMALL_W)
        stats = keep(400)
        Kn = keep(256).rearrange("p (s g n) -> p s g n", s=2, g=2)
        Vn = keep(512).rearrange("p (s c) -> p s c", s=2)
        Gate = keep(TT * 36).rearrange("p (t c) -> p t c", t=TT)
        Grow = keep(NB * 3).rearrange("p (b c) -> p b c", b=NB)
        CS = keep(CT * 18)
        QZ = keep(2 * NB * 128).rearrange("p (g b m) -> p g b m", g=2, b=NB)
        base = top[0]

        def at(off, n):
            assert base + off + n <= ARENA, (base, off, n)
            return arena[:, base + off:base + off + n]

        def C(name):
            a, w = CONST[name]
            return cst[:, a:a + w]

        def S(name):
            a, w = SMALL[name]
            return small[:, a:a + w]

        ident = C("ident")
        W = [at(4096 * n, 4096).rearrange("p (k c) -> p k c", k=KD) for n in range(2)]
        P1 = [at(8192 + 2560 * n, 2560).rearrange("p (t c) -> p t c", t=TT) for n in range(7)]
        P1all = at(8192, 7 * 2560)
        MKV = [at(26112 + 1024 * l, 1024).rearrange("p (m c) -> p m c", m=2) for l in range(2)]
        KTm = [at(28160 + 512 * l, 512).rearrange("p (g m) -> p g m", g=2) for l in range(2)]
        YT0 = at(8192, 5120).rearrange("p (k c) -> p k c", k=KD)
        YT0f = at(8192, 5120)
        MQG0 = at(13312, 2560).rearrange("p (t c) -> p t c", t=TT)
        memT = [at(15872 + 2048 * l, 2048).rearrange("p (k c) -> p k c", k=KD) for l in range(2)]
        M = at(19968, 2048).rearrange("p (t c) -> p t c", t=2)
        H = [at(22016 + 1024 * n, 1024) for n in range(2)]
        SQ = at(24064, 1024)
        Cb = at(15872, 576)
        U = [at(16448 + 600 * n, 600) for n in range(2)]
        Y = at(17648, 576)
        E = at(18224, 576)
        Sb = at(18800, 256)
        Wg = at(29184, 288).rearrange("p (k c) -> p k c", k=KD)
        MA = [15872, 0]
        QT = at(26112, 3072).rearrange("p (r g c) -> p r g c", r=3, g=2)
        QTf = at(26112, 3072)
        KTs = at(29184, 1024).rearrange("p (g c) -> p g c", g=2)
        KTw = at(30208, 1024).rearrange("p (g c) -> p g c", g=2)
        GE0 = at(19056, 1280).rearrange("p (t c) -> p t c", t=TT)
        GE = [at(29472 + 1280 * n, 1280).rearrange("p (t c) -> p t c", t=TT) for n in range(2)]
        PG = [at(29472, 2048), QZ.rearrange("p g b m -> p (g b m)")]
        CPM = [at(19056 + 2048 * m, 2048) for m in range(2)]
        CPR = [[at(23152 + 1024 * m + 512 * n, 512) for n in range(2)] for m in range(2)]
        CR = at(31520, 512)
        CBL = at(25200, 512).rearrange("p (s c) -> p s c", s=4)
        PA = [at(10240 + 512 * n, 512) for n in range(2)]
        PB = [at(8192 + 512 * n, 512) for n in range(2)]
        CRp = at(9216, 512)
        BLp = at(9728, 512).rearrange("p (s c) -> p s c", s=4)
        Qz = at(0, 2048).rearrange("p (g h c) -> p g h c", g=2, h=2)
        PP = [at(2048 + 2112 * n, 2112) for n in range(2)]
        PTt = at(15744, 2304)
        MIXB = at(12288, 3072).rearrange("p (t c) -> p t c", t=PT)
        Om = at(15360, 384)
        SV = [at(4096 * n, 4096).rearrange("p (s c) -> p s c", s=NPG) for n in range(2)]
        SK = [at(8192 + 2048 * n, 2048).rearrange("p (s c) -> p s c", s=8) for n in range(2)]
        SKT = at(12288, 4096).rearrange("p (g c) -> p g c", g=2)
        SM = at(16384, 2112)
        SWKT = at(18496, 1024).rearrange("p (g c) -> p g c", g=2)
        SIMP = at(19520, 130)
        SCH = at(19650, 128)
        SSC = at(19780, 40)
        SMB = at(19820, 40)
        SS2 = at(20460, 40)
        SM8 = at(19860, 8)
        SNM = at(19868, 64)
        SQB = [at(19940 + 256 * n, 256).rearrange("p (g m) -> p g m", g=2) for n in range(2)]
        SWI = [at(26112 + 2048 * n, 2048).rearrange("p (s c) -> p s c", s=4) for n in range(2)]
        SPT = [at(30208 + 512 * n, 512).rearrange("p (s c) -> p s c", s=4) for n in range(2)]
        SW = at(31232, 576)
        SPC = [at(31808, 128), at(20756, 128)]
        SO = at(20500, 256)
        gfin = at(8192, 1024)
        fin = [at(9216 + 1024 * n, 1024) for n in range(2)]
        HTf = arena[:, TT * D:TT * D + KD * TOK]
        rope_t = [HTf[:, 1280 + 320 * n:1600 + 320 * n] for n in range(4)]

        MIXf = at(12288, 3072)
        rs = lambda a, b: stats[:, a:b]

        const_in = sem("const_in")
        mem_in = sem("mem_in")
        x_in = sem("x_in")
        pad_zero = sem("pad_zero")
        x_zero = sem("x_zero")
        w_in = [sem(f"w_in{n}") for n in range(2)]
        wg_in = sem("wg_in")
        product = sem("product")
        squared = sem("squared")
        mean_sq = sem("mean_sq")
        root = sem("root")
        rstd = sem("rstd")
        scaled = sem("scaled")
        h_turned = sem("h_turned")
        h_taken = sem("h_taken")
        kv_taken = sem("kv_taken")
        kt_turned = sem("kt_turned")
        kt_taken = sem("kt_taken")
        kv_out = sem("kv_out")
        chunk_taken = sem("chunk_taken")
        gates_taken = sem("gates_taken")
        c_copied = sem("c_copied")
        z_exp = sem("z_exp")
        s_copied = sem("s_copied")
        u_made = sem("u_made")
        b_used = sem("b_used")
        z_used = sem("z_used")
        state_set = sem("state_set")
        state_kept = sem("state_kept")
        state_out = sem("state_out")
        conv_y = sem("conv_y")
        sig_exp = sem("sig_exp")
        sig_done = sem("sig_done")
        ma_q, ma_qt, ma_qc, ma_s, ma_m, ma_p, ma_t, ma_td, ma_ta, ma_o, ma_y, ma_yt, ma_done = [
            sem("ma_" + n) for n in ("q_scaled", "q_turned", "q_copied", "scored", "max", "probs", "p_turned",
                                     "p_took_dve", "p_took_act", "out", "y", "y_turned", "y_took")]
        ms_in = [sem(f"ms_in{n}") for n in range(2)]
        ms_vin = [sem(f"ms_vin{n}") for n in range(2)]
        ms_q, ms_qt, ms_qz, ms_qb, ms_kt, ms_kc, ms_s, ms_m, ms_p, ms_t, ms_c, ms_o, ms_n, ms_y, ms_done, ms_g, ms_gm = [
            sem("ms_" + n) for n in ("q_scaled", "q_turned", "q_spread", "q_set", "k_turned", "k_copied", "scored",
                                     "max", "probs", "p_turned", "p_copied", "out", "normed", "y_turned", "y_took",
                                     "gate_turned", "gated")]
        out_added = sem("out_added")
        roped = sem("roped")
        r_turned = sem("r_turned")
        r_took = sem("r_took")
        kv_stored = sem("kv_stored")
        gates_back = sem("gates_back")
        gates_written = sem("gates_written")
        qz_zero = sem("qz_zero")
        win_copied = sem("win_copied")
        cp_in = [sem(f"cp_in{n}") for n in range(2)]
        cp_a, cp_b, cp_ra, cp_rb, cp_sum, cp_rows, cp_turned, cp_cols, cp_phi, cp_took = [
            sem("cp_" + n) for n in ("prod0", "prod1", "part0", "part1", "summed", "rows", "turned", "cols", "phi",
                                     "took")]
        pa_q, pa_s, pa_m, pa_p, pa_cm, pa_t, pa_td, pa_ta, pa_o, pa_mix = [
            sem("pa_" + n) for n in ("q_set", "scored", "max", "probs", "cmp_masked", "p_turned", "took_dve",
                                     "took_act", "out", "mixed")]
        sa_v = [sem(f"sa_v{n}") for n in range(2)]
        sa_k = [sem(f"sa_k{n}") for n in range(2)]
        (sa_qb, sa_cs, sa_cm, sa_ce, sa_cn, sa_imp, sa_mask, sa_ft, sa_fa, sa_fd, sa_s, sa_m, sa_p,
         sa_bt, sa_ba, sa_bd, sa_used, sa_mix, sa_y, sa_done) = [
            sem("sa_" + n) for n in ("q_set", "cmp_scored", "cmp_max", "cmp_exp", "cmp_normed", "imp",
                                     "mask", "k_turned", "k_took_act", "k_took_dve", "scored", "max", "probs",
                                     "p_turned", "p_took_act", "p_took_dve", "values_used", "mixed", "y_turned", "y_took")]
        sa_w = [sem(f"sa_w{n}") for n in range(2)]
        sa_part = sem("sa_part_scored")
        sa_new = sem("sa_new_read")
        sz_t = sem("sample_gate_turned")
        sz_done = sem("sample_gated")
        r_spread = sem("r_spread")
        ht_zero = sem("ht_zero")
        yg = sem("y_gated")
        yg_t = sem("y_gated_turned")
        yg_c = sem("y_gated_took")
        gfin_in = sem("gfin_in")
        y_ready = sem("y_ready")
        y_out = [sem(f"y_out{n}") for n in range(2)]
        dve_links = sem("dve_links")
        pool_links = sem("pool_links")

        block = ctx.enter_context(nc.Block())

        def step_dve(cell=398):
            nc.vector.memset(rs(cell, cell + 1), 0.0)

        def heads(ap):
            return ap.rearrange("p (g d) -> p g d", g=KVH)

        def row_pos(name, s):
            return S(name)[:, HD * s:HD * s + HD].unsqueeze(1).to_broadcast([128, KVH, HD])

        def tile_view(ap):
            return ap.rearrange("p (j g d) -> p j g d", g=KVH, d=HD)

        def tile_pos(name):
            return S(name).rearrange("p (j d) -> p j d", d=HD).unsqueeze(2).to_broadcast([128, 8, KVH, HD])

        BATCHES = [(gg, s) for gg in range(2) for s in range(2)] + [None]

        def pair(n):
            return n // PT, n % PT, 128 * (n % PT + 1)

        def bank_of(n, b):
            return 5 + (len(BATCHES) * n + b) % 2

        def taken(r, n, b):
            t = Turn(r, n, 8)
            if b < 0:
                return pa_td, t.value(2, b + 1, base=START.pa_td)
            if b < 3:
                return pa_ta, t.value(3, b + 1, base=START.pa_ta)
            return pa_td, t.value(2, b - 2, base=START.pa_td)

        def mem_bufs(l):
            o = MA[l]
            return {
                "QZ": at(o, 2048).rearrange("p (g b m) -> p g b m", g=2, b=NB),
                "QB": [at(o + 2048 + 256 * n, 256).rearrange("p (g m) -> p g m", g=2) for n in range(2)],
                "KTb": [at(o + 2560 + 512 * n, 512) for n in range(2)],
                "SP": [at(o + 3584 + 256 * n, 256) for n in range(2)],
                "SPT": [at(o + 4096 + 256 * n, 256) for n in range(2)],
                "SO": [at(o + 4608 + 256 * n, 256) for n in range(2)],
                "MC": [[at(o + 5632 + 1024 * n + 512 * kv, 512).rearrange("p (m c) -> p m c", m=2) for kv in range(2)]
                       for n in range(2)],
                "QS": at(o + 5120, 256),
                "QT": [at(30496 + 256 * n, 256) for n in range(2)],
                "P": [HTf[:, 2560 + 1024 * n:3584 + 1024 * n].rearrange("p (h m) -> p h m", h=4) for n in range(2)],
                "PT": at(29472, 1024),
                "OY": at(o + 5376, 256),

            }

        def mem_prompt_steps(steps):
            for n in range(PT + 2):
                for step, lag in steps:
                    if 0 <= n - lag < PT:
                        step(n - lag)

        def mem_sample_steps(eng, steps, lk=None, links=0):
            def run(i, n):
                for step, lag in steps:
                    if i is not None:
                        step(Turn(i, n - lag, 2))
                    elif 0 <= n - lag < NB:
                        step(Turn(0, n - lag, 2))

            run(None, -1)
            run(None, 0)
            with eng.Fori(0, NB // 2 - 1) as i:
                if lk is not None:
                    lk.enter(i, 2 * links)
                for n in (1, 2):
                    run(i, n)
                if lk is not None:
                    lk.leave(NB // 2 - 1)
            run(None, NB - 1)
            run(None, NB)

        def sample_phase(eng, front, middle, back, lk=None):
            front(Turn(0, 0, 2), None)
            with eng.Fori(0, NB // 2 - 1) as i:
                if lk is not None:
                    lk.enter(i, 2 * LINKS_OF_TURN)
                for n in range(2):
                    t, nxt = Turn(i, n, 2), Turn(i, n + 1, 2)
                    middle(t)
                    front(nxt, t)
                    back(t, 2)
                if lk is not None:
                    lk.leave(NB // 2 - 1)
            t, nxt = Turn(NB // 2 - 1, 0, 2), Turn(NB // 2 - 1, 1, 2)
            middle(t)
            front(nxt, t)
            back(t, 2)
            middle(nxt)
            back(nxt, 1)

        @block.sync
        def _(sp):
            def load_w(n):
                sp.dma_start(W[n % 2].rearrange("p k c -> p (k c)"), I["wall"][n]).then_inc(w_in[n % 2], 16)

            sp.dma_start(M, I["mem"].rearrange("(t p) c -> p t c", p=128)).then_inc(mem_in, 16)
            sp.dma_start(cst, I["const"]).then_inc(const_in, 16)
            sp.dma_start(small, I["small"]).then_inc(const_in, 16)
            sp.dma_start(ptab[:, :], I["pages"]).then_inc(const_in, 16)
            load_w(0)
            sp.dma_start(X[:, 0:PT, :], I["xp"].rearrange("(t p) c -> p t c", p=128)).then_inc(x_in, 16)
            sp.dma_start(X[0:NS, PT, :], I["xs"]).then_inc(x_in, 16)
            load_w(1)
            sp.wait_ge(product, PBASE[1])
            load_w(2)
            sp.wait_ge(product, PBASE[2])
            load_w(B_CONV)
            for l in range(2):
                sp.wait_ge(kv_taken, 2 * (l + 1))
                sp.dma_start(O["mem"][l].rearrange("(m p) c -> p m c", p=128), MKV[l]).then_inc(kv_out, 16)

            def load_pages(t, first, last):
                for k in range(first, last):
                    sp.wait_ge(cp_a, t.value(NTL, k - 1, base=START.cp_a))
                    sp.wait_ge(cp_b, t.value(NTL, k - 1, base=START.cp_b))
                    for p in range(TILE):
                        page = sp.value_load(ptab[0:1, bass.ds(t.at(NPG, TILE * k + p), 1)], min_val=0, max_val=POOL - 1)
                        sp.dma_start(PG[k % 2][32 * p:32 * p + 32, :],
                                     I["ccmp"][bass.ds(page, 1)].rearrange("a (p j) c -> (a p) (j c)", j=4)
                                     ).then_inc(cp_in[k % 2], 16)

            sp.wait_ge(const_in, 48)
            with sp.Fori(0, CT // 2) as i:
                for n in range(2):
                    t = Turn(i, n, 2)
                    load_pages(t, 0, 2)
                    sp.wait_ge(product, t.value(4, 0, base=PBASE[B_CONV]))
                    sp.dma_start(W[(B_CONV + 1 + n) % 2].rearrange("p k c -> p (k c)"),
                                 I["wall"][bass.ds(t.at(1, B_CONV + 1), 1)].rearrange("a p c -> (a p) c")
                                 ).then_inc(w_in[(B_CONV + 1 + n) % 2], 16)
                    load_pages(t, 2, NTL)
            sp.wait_ge(product, PBASE[B_OUT0])
            load_w(B_OUT0 + 1)
            sp.wait_ge(state_kept, START.state_kept + 2 * CT)
            sp.dma_start(O["conv"], CS).then_inc(state_out, 16)

            def mem_loads(l):
                with sp.Fori(0, NB // 2) as i:
                    for n in range(2):
                        t = Turn(i, n, 2)
                        if l == 0:
                            sp.wait_ge(conv_y, START.conv_y + CT)
                        else:
                            sp.wait_ge(gates_taken, 1)
                        for used, base, kv, loaded in ((ms_kt, START.ms_kt, 0, ms_in), (ms_o, START.ms_o, 1, ms_vin)):
                            sp.wait_ge(used, t.value(1, -1, base=NB * l + base))
                            half = at(MA[l] + 5632 + 1024 * n + 512 * kv, 512).rearrange("p (m c) -> p m c", m=2)
                            sp.dma_start(half, I["cmem"][l, bass.ds(t.at(1), 1), :, 256 * kv:256 * kv + 256]
                                         .rearrange("a (m p) c -> (a p) m c", p=128)).then_inc(loaded[n], 16)

            sp.wait_ge(cp_phi, CT)
            mem_loads(0)
            sp.wait_ge(ma_done, PT)
            sp.wait_ge(ms_gm, 1)
            load_pages(Turn(0, CT, 1), 0, NTL)
            sp.wait_ge(product, PBASE[B_N - 1])
            load_w(B_N)
            load_pages(Turn(0, CT + 1, 1), 0, NTL)
            sp.dma_start(O["win_s"][:, 0:WIN - NT, :], I["win"][:, NT:WIN, :]).then_inc(win_copied, 16)
            sp.dma_start(Wg.rearrange("p k c -> p (k c)"), I["wg"]).then_inc(wg_in, 16)
            for n in range(B_N + 1, B_OUT1):
                sp.wait_ge(product, PBASE[n - 1])
                load_w(n)
            sp.wait_ge(sig_done, 5)
            sp.dma_start(gates_dram, Gate[0:NS, PT, :]).then_inc(gates_written, 16)
            mem_loads(1)
            sp.wait_ge(roped, 4)
            for s, (name, kc, ko, vc, vo) in enumerate((("cmp", 2, 256, 3, 0), ("sel", 3, 256, 4, 0), ("win", 4, 256, 5, 0))):
                for half, (c, o) in enumerate(((kc, ko), (vc, vo))):
                    sp.dma_start(O[name + "_p"][:, half * 256:half * 256 + 256].rearrange("(t p) c -> p t c", p=128),
                                 P1[c][:, 0:PT, o:o + 256]).then_inc(kv_stored, 16)
                    rows = P1[c][0:NS, PT, o:o + 256]
                    if name == "win":
                        for b in range(NB):
                            sp.dma_start(O["win_s"][b, WIN - NT:WIN, half * 256:half * 256 + 256],
                                         P1[c][NT * b:NT * b + NT, PT, o:o + 256]).then_inc(kv_stored, 16)
                    else:
                        sp.dma_start(O[name + "_s"][:, half * 256:half * 256 + 256], rows).then_inc(kv_stored, 16)

            sp.wait_ge(gates_written, 16)
            sp.wait_ge(qz_zero, 2)
            g_src = gates_dram.rearrange("(b t) (s r g) -> t b s r g", b=NB, s=3, r=GRP)
            with nc.allow_non_contiguous_dma(reason="2304 numbers in all"):
                for g in range(KVH):
                    for r in range(GRP):
                        for s in range(3):
                            sp.dma_start(Grow[32 * g + 8 * r:32 * g + 8 * r + 8, :, s:s + 1], g_src[:, :, s:s + 1, r, g]
                                         ).then_inc(gates_back, 16)
            sp.wait_ge(cp_phi, NB + 1)
            sp.wait_ge(r_turned, 12)
            sp.wait_ge(kv_stored, KV_STORED)
            with sp.Fori(0, NB // 2) as i:
                for n in range(2):
                    t = Turn(i, n, 2)
                    b = t.at(1)
                    first = b * NPG
                    for half in range(2):
                        sp.wait_ge(sa_ft, t.value(10, -6 + 4 * half, base=START.sa_ft))
                        for p in range(8):
                            page = sp.value_load(ptab[0:1, bass.ds(first + (8 * half + p), 1)], min_val=0, max_val=POOL - 1)
                            sp.dma_start(SK[half][:, p, :], I["csel"][bass.ds(page, 1), :, 0:256].rearrange("a p c -> (a p) c")
                                         ).then_inc(sa_k[half], 16)
                    sp.wait_ge(yg_c, PT)
                    sp.wait_ge(sa_used, t.value(6, -6, base=START.sa_used))
                    sp.dma_start(SWI[n], I["win"][bass.ds(b, 1)].rearrange("a (s p) c -> (a p) s c", p=128)
                                 ).then_inc(sa_w[n], 16)
            for n in range(2):
                sp.wait_ge(sa_used, START.sa_used + 6 * (NB - 1 + n))
                load_w(B_OUT1 + n)
            sp.wait_ge(sz_done, 1)
            sp.dma_start(gfin, I["gfin"]).then_inc(gfin_in, 16)
            for t in range(TT):
                sp.wait_ge(y_ready, t + 1)
                if t < PT:
                    sp.dma_start(O["yp"][128 * t:128 * t + 128, :], fin[t % 2]).then_inc(y_out[t % 2], 16)
                else:
                    sp.dma_start(O["ys"], fin[t % 2][0:NS, :]).then_inc(y_out[t % 2], 16)
            for n in range(2):
                sp.wait_ge(y_out[n], 16 * ((TT + 1 - n) // 2))
            sp.wait_ge(state_out, 16)
            sp.wait_ge(kv_out, 32)
            sp.wait_ge(win_copied, 16)

        @block.gpsimd
        def _(pool):
            for signal, start in (
                    (cp_a, START.cp_a), (cp_b, START.cp_b), (cp_sum, START.cp_sum), (cp_ra, START.cp_ra), (cp_rb, START.cp_rb), (conv_y, START.conv_y), (ms_s, START.ms_s), (ms_kt, START.ms_kt),
                    (u_made, START.u_made), (pa_t, START.pa_t), (pa_o, START.pa_o), (sa_bt, START.sa_bt),
                    (c_copied, START.c_copied), (s_copied, START.s_copied), (b_used, START.b_used), (z_used, START.z_used),
                    (ms_kc, START.ms_kc), (ms_c, START.ms_c), (ms_done, START.ms_done), (cp_rows, START.cp_rows), (cp_cols, START.cp_cols),
                    (cp_took, START.cp_took), (pa_p, START.pa_p), (pa_mix, START.pa_mix), (pa_ta, START.pa_ta),
                    (pa_td, START.pa_td), (sa_ba, START.sa_ba), (sa_bd, START.sa_bd), (sa_m, START.sa_m),
                    (sa_p, START.sa_p), (sa_done, START.sa_done), (state_kept, START.state_kept), (ms_y, START.ms_y),
                    (sa_y, START.sa_y), (pa_s, START.pa_s), (sa_used, START.sa_used), (sa_ft, START.sa_ft),
                    (sa_s, START.sa_s), (ms_o, START.ms_o),):
                pool.sem_inc(signal, start)
            nc.gpsimd.memset(Grow, 0.0).then_inc(qz_zero, 1)
            lk = Links(pool, pool_links)
            pool.wait_ge(const_in, 48)
            pool.wait_ge(product, PBASE[B_C0])
            pool.wait_ge(h_turned, 14)
            for n in range(2):
                nc.gpsimd.memset(U[n][:, 0:2], 0.0).then_inc(pad_zero, 1)
            for k in range(KD):
                ins = nc.gpsimd.memset(YT0[:, k, SEQ + NS:TOK], 0.0)
            ins.then_inc(pad_zero, 1)

            def page_prod1(t):
                for k in range(NTL):
                    pool.wait_ge(cp_in[k % 2], t.value(32 * TILE, 16 * TILE * (k // 2 + 1)))
                    pool.wait_ge(cp_rb, t.value(NTL, k, base=START.cp_rb))
                    nc.gpsimd.tensor_tensor(tile_view(CPM[1]), tile_view(PG[k % 2]), tile_pos("tile_pos1"), ALU.mult
                                            ).then_inc(cp_b, 1)
                    pool.wait_ge(cp_b, t.value(NTL, k + 1, base=START.cp_b))
                    lk.link(nc.gpsimd.tensor_tensor(CPM[1][:, 0:1024], CPM[1][:, 0:1024], CPM[1][:, 1024:2048], ALU.add))
                    pool.wait_ge(cp_sum, t.value(NTL, k - 1, base=START.cp_sum))
                    nc.gpsimd.tensor_tensor(CPR[1][k % 2], CPM[1][:, 0:512], CPM[1][:, 512:1024], ALU.add
                                            ).then_inc(cp_rb, 1)

            with pool.Fori(0, CT // 2) as i:
                lk.enter(i, 2 * NTL)
                for n in range(2):
                    t = Turn(i, n, 2)
                    Us = U[n][:, 514:594].rearrange("p (b c) -> p b c", b=NB)
                    pool.wait_ge(conv_y, t.value(1, -1, base=START.conv_y))
                    src = small[:, bass.ds(t.at(16, SMALL["state"][0]), 16)].rearrange("p (b c) -> p b c", b=NB)
                    nc.gpsimd.tensor_copy(Us[:, :, 0:2], src).then_inc(state_set, 1)
                    page_prod1(t)
                lk.leave(CT // 2)

            def mem_q(l):
                QZm = at(MA[l], 2048).rearrange("p (g b m) -> p g b m", g=2, b=NB)
                if l == 0:
                    pool.wait_ge(conv_y, START.conv_y + CT)
                    pool.wait_ge(state_kept, START.state_kept + 2 * CT)
                else:
                    pool.wait_ge(gates_taken, 1)
                nc.gpsimd.memset(QZm, 0.0).then_inc(ms_qz, 1)
                pool.wait_ge(ms_qz, 5 * (l + 1))
                with pool.Fori(0, NB // 2) as i:
                    for n in range(2):
                        t = Turn(i, n, 2)
                        QB = at(MA[l] + 2048 + 256 * n, 256).rearrange("p (g m) -> p g m", g=2)
                        pool.wait_ge(ms_s, t.value(1, -1, base=NB * l + START.ms_s))
                        nc.gpsimd.tensor_copy(QB, QZm[:, :, bass.ds(t.at(1), 1), :].rearrange("p g a m -> p g (a m)")
                                              ).then_inc(ms_qb, 1)
            mem_q(0)
            pool.wait_ge(ma_done, PT)
            pool.wait_ge(ms_gm, 1)
            for b in range(CT, NB):
                page_prod1(Turn(0, b, 1))
            pool.wait_ge(cp_a, START.cp_a + NB * NTL)
            pool.wait_ge(cp_b, START.cp_b + NB * NTL)
            nc.gpsimd.memset(QZ, 0.0).then_inc(qz_zero, 1)
            mul_add = nc.gpsimd.tensor_tensor

            def rope(c, h0, nh):
                v = P1[c][:, :, 64 * h0:64 * (h0 + nh)].rearrange("p t (h d) -> p t h d", h=nh)
                x1, x2 = v[:, :, :, 0:8], v[:, :, :, 8:16]
                cs, sn = [C(k).rearrange("p (t d) -> p t d", t=TT).unsqueeze(2).to_broadcast([128, TT, nh, 8])
                          for k in ("cos", "sin")]
                tmp = [r[:, 0:TT * nh * 8].rearrange("p (t h d) -> p t h d", t=TT, h=nh) for r in rope_t]
                lk.did(mul_add(tmp[0], x1, cs, ALU.mult))
                lk.did(mul_add(tmp[1], x2, sn, ALU.mult))
                lk.did(mul_add(tmp[2], x2, cs, ALU.mult))
                lk.link(mul_add(tmp[3], x1, sn, ALU.mult))
                lk.did(mul_add(x1, tmp[0], tmp[1], ALU.subtract))
                lk.link(mul_add(x2, tmp[2], tmp[3], ALU.add))

            pool.wait_ge(chunk_taken, 8 * TT)
            pool.wait_ge(gates_taken, 1)
            for c, h0, nh in ((1, 0, 8), (2, 0, 8), (3, 4, 4), (4, 4, 4)):
                rope(c, h0, nh)
            for s in range(2):
                ins = nc.gpsimd.tensor_copy(Vn[0:NS, s, :], P1[4 + s][0:NS, PT, 0:256])
            ins.then_inc(roped, 4)
            mem_q(1)

            for p in range(PT):
                pool.wait_ge(ma_done, 2 * PT)
                pool.wait_ge(ms_gm, 2)
                pool.wait_ge(roped, 4)
                if p >= 2:
                    pool.wait_ge(cp_sum, NB * NTL + START.cp_sum + p - 1)
                nc.gpsimd.tensor_tensor(heads(PB[p % 2][:, 0:256]), heads(P1[2][:, p, 256:512]), row_pos("pos1", 0), ALU.mult)
                nc.gpsimd.tensor_tensor(heads(PB[p % 2][:, 256:512]), heads(P1[3][:, p, 0:256]), row_pos("pos1", 1),
                                        ALU.mult).then_inc(cp_rb, 1)

            pool.wait_ge(r_spread, 6)
            pool.wait_ge(yg_c, PT)
            pool.wait_ge(kv_stored, KV_STORED)
            nc.gpsimd.memset(HT[:, 2:8, SEQ + NS:TOK], 0.0).then_inc(ht_zero, 1)
            with pool.Fori(0, NB // 2) as i:
                for n in range(2):
                    t = Turn(i, n, 2)
                    pool.wait_ge(sa_s, t.value(1, -1, base=START.sa_s))
                    nc.gpsimd.tensor_copy(SQB[n], QZ[:, :, bass.ds(t.at(1), 1), :].rearrange("p g a m -> p g (a m)")
                                          ).then_inc(sa_qb, 1)
                    pool.wait_ge(sa_used, t.value(6, -6, base=START.sa_used))
                    for p in range(NPG):
                        page = pool.value_load(ptab[0:1, bass.ds(t.at(NPG, p), 1)], min_val=0, max_val=POOL - 1)
                        pool.dma_start(SV[n][:, p, :], I["csel"][bass.ds(page, 1), :, 256:512].rearrange("a p c -> (a p) c")
                                       ).then_inc(sa_v[n], 16)

        @block.scalar
        def _(act):
            def norm_act(tiles, first, number):
                for j, src in enumerate(tiles):
                    if number == 0:
                        act.wait_ge(mem_in, 16)
                    elif number == 1:
                        act.wait_ge(x_in, 32)
                        if j == PT:
                            act.wait_ge(x_zero, 1)
                    elif number == 2:
                        if j == TT - 1:
                            copy_rows(Turn(0, NB - 1, 1))
                            keep_blocks(Turn(0, NB - 1, 1))
                        act.wait_ge(out_added, TT + j + 1)
                    nc.scalar.activation(HTf[:, 0:1024] if number == 2 else SQ, src, ACT.Square, accum_out=rs(first + j, first + j + 1)).then_inc(squared, 1)
                    act.wait_ge(squared, first + j + 1)
                act.wait_ge(mean_sq, number + 1)
                nc.scalar.activation(rs(20 + first, 20 + first + len(tiles)), rs(20 + first, 20 + first + len(tiles)),
                                     ACT.Sqrt).then_inc(root, 1)
                act.wait_ge(rstd, number + 1)

            tiles0 = [M[:, 0, :], M[:, 1, :]] + [X[:, t, :] for t in range(TT)]
            def scale_rows(first, last):
                for j in range(first, last):
                    if j >= 2:
                        act.wait_ge(h_turned, 2 * (j - 1))
                    nc.scalar.activation(H[j % 2], tiles0[j], ACT.Copy, scale=rs(20 + j, 21 + j)).then_inc(scaled, 1)

            norm_act(tiles0[0:2], 0, 0)
            scale_rows(0, 2)
            norm_act(tiles0[2:7], 2, 1)
            scale_rows(2, 4)
            for l in range(2):
                for m in range(2):
                    act.wait_ge(product, 2 * l + m + 1)
                    nc.scalar.copy(MKV[l][:, m, :], PS[:, 2 * l + m, :]).then_inc(kv_taken, 1)
            for l in range(2):
                act.wait_ge(kt_turned, l + 1)
                nc.scalar.copy(KTm[l].rearrange("p g m -> p (g m)"), PS[:, 4 + l, :]).then_inc(kt_taken, 1)
            scale_rows(4, 7)



            for t in range(TT):
                act.wait_ge(product, PBASE[B_C0] + t + 1)
                nc.scalar.copy(MQG0[:, t, :], PS[:, t, :]).then_inc(chunk_taken, 1)
                act.wait_ge(chunk_taken, t + 1)
                nc.scalar.activation(GE0[:, t, :], MQG0[:, t, 256:512], ACT.Exp, scale=-1.0).then_inc(sig_exp, 1)

            def copy_rows(t):
                act.wait_ge(cp_sum, t.value(NTL, NTL, base=START.cp_sum))
                nc.scalar.copy(CR[0:NC, :], PS[0:NC, 5, :]).then_inc(cp_rows, 1)

                act.wait_ge(cp_turned, t.value(1, 1))
                nc.scalar.copy(CBL[:, :, 0:NC], PS[:, 6, :].rearrange("p (s c) -> p s c", s=4)[:, :, 0:NC]
                               ).then_inc(cp_cols, 1)

            def keep_blocks(t):
                act.wait_ge(cp_phi, t.value(1, 1))
                nc.scalar.copy(KC[:, :, bass.ds(t.at(1), 1), 0:NC].rearrange("p g a n -> p g (a n)"),
                               PS[:, 7, 0:256].rearrange("p (g n) -> p g n", g=2)[:, :, 0:NC])
                nc.scalar.copy(VC[0:NC, bass.ds(t.at(1), 1), :].rearrange("p a n -> p (a n)"),
                               PS[0:NC, 7, 256:512]).then_inc(cp_took, 1)

            with act.Fori(0, CT // 2) as i:
                for n in range(2):
                    t = Turn(i, n, 2)
                    act.wait_ge(product, t.value(4, 1, base=PBASE[B_CONV]))
                    act.wait_ge(u_made, t.value(2, 0, base=START.u_made))
                    nc.scalar.copy(Cb[:, 0:512], PS[:, 0, :]).then_inc(c_copied, 1)
                    copy_rows(t)
                    act.wait_ge(product, t.value(4, 4, base=PBASE[B_CONV]))
                    act.wait_ge(conv_y, t.value(1, 0, base=START.conv_y))
                    nc.scalar.copy(Sb, PS[:, 4, 0:256]).then_inc(s_copied, 1)
                    nc.scalar.activation(E[:, 0:512], PS[:, 3, :], ACT.Exp, scale=-1.0)
                    act.wait_ge(s_copied, t.value(1, 1, base=START.s_copied))
                    nc.scalar.activation(E[:, 512:576], Sb[:, 192:256], ACT.Exp, scale=-1.0).then_inc(z_exp, 1)
                    keep_blocks(t)

            def mem_prompt_act(l, YT):
                QTt, P, PTb = (mem_bufs(l)[k] for k in ("QT", "P", "PT"))
                if l == 0:
                    act.wait_ge(conv_y, START.conv_y + CT)
                else:
                    act.wait_ge(sig_done, 5)
                def take_q(n):
                    T = l * PT + n
                    act.wait_ge(ma_qt, T + 1)
                    nc.scalar.copy(QTt[n % 2], PS[:, 5, 256 * (n % 2):256 * (n % 2) + 256]).then_inc(ma_qc, 1)

                def take_p(n):
                    T = l * PT + n
                    act.wait_ge(ma_t, 2 * (T + 1))
                    act.wait_ge(ma_o, T)
                    nc.scalar.copy(PTb[:, 512:1024], PS[:, 7, :]).then_inc(ma_ta, 1)

                def take_y(n):
                    T = l * PT + n
                    act.wait_ge(ma_yt, T + 1)
                    nc.scalar.copy(YT[:, 0:2, 128 * n:128 * n + 128],
                                   PS[:, 5, 256 * (n % 2):256 * (n % 2) + 256].rearrange("p (g c) -> p g c", g=2)
                                   ).then_inc(ma_done, 1)

                def exps(n):
                    T = l * PT + n
                    act.wait_ge(ma_m, 2 * (T + 1))
                    if T >= 2:
                        act.wait_ge(ma_t, 2 * (T - 1))
                    for h in range(4):
                        nc.scalar.activation(P[n % 2][:, h, :], PS[:, 2 * (n % 2) + h % 2, 256 * (h // 2):256 * (h // 2) + 256],
                                             ACT.Exp, bias=rs(60 + 8 * (n % 2) + h, 61 + 8 * (n % 2) + h),
                                             accum_out=rs(76 + 8 * (n % 2) + h, 77 + 8 * (n % 2) + h)).then_inc(ma_p, 1)

                mem_prompt_steps([(take_q, 0), (take_p, 1), (take_y, 2), (exps, 0)])

            def mem_sample_act(l):
                b_ = mem_bufs(l)

                def take_k(t):
                    act.wait_ge(ms_kt, t.value(1, 1, base=NB * l + START.ms_kt))
                    nc.scalar.copy(b_["KTb"][t.n % 2], PS[:, 6, :]).then_inc(ms_kc, 1)

                def exps(t):
                    n = t.n % 2
                    act.wait_ge(ms_m, t.value(1, 1, base=NB * l))
                    nc.scalar.activation(b_["SP"][n], PS[:, n, 0:256], ACT.Exp, bias=rs(100 + n, 101 + n),
                                         accum_out=rs(104 + n, 105 + n)).then_inc(ms_p, 1)

                mem_sample_steps(act, [(take_k, -1), (exps, -1)])

            mem_prompt_act(0, YT0)
            mem_sample_act(0)
            copy_rows(Turn(0, CT, 1))
            keep_blocks(Turn(0, CT, 1))
            norm_act([X[:, t, :] for t in range(TT)], 7, 2)
            for j in range(TT):
                act.wait_ge(h_turned, 2 * (7 + j - 1))
                nc.scalar.activation(H[(7 + j) % 2], X[:, j, :], ACT.Copy, scale=rs(27 + j, 28 + j)).then_inc(scaled, 1)
            with act.Fori(0, 3) as i:
                for n in range(2):
                    t = Turn(i, n, 2)
                    for j in range(TT):
                        act.wait_ge(product, t.value(TT, j + 1, base=PBASE[B_N]))
                        nc.scalar.copy(P1all[:, bass.ds(i * 2560 + (2560 * CHUNK_ORDER[n] + 512 * j), 512)], PS[:, j, :]
                                       ).then_inc(chunk_taken, 1)
            act.wait_ge(chunk_taken, 7 * TT)
            for j, z in enumerate((P1[0][:, :, 256:512], P1[5][:, :, 256:512], P1[6][:, :, 0:256], P1[6][:, :, 256:512])):
                if j >= 2:
                    act.wait_ge(sig_done, j - 1)
                nc.scalar.activation(GE[j % 2], z, ACT.Exp, scale=-1.0).then_inc(sig_exp, 1)
                for t in range(j, TT if j == 3 else j + 1):
                    act.wait_ge(product, PBASE[B_N + 6] + t + 1)
                    nc.scalar.copy(P1[CHUNK_ORDER[6]][:, t, :], PS[:, t, :]).then_inc(chunk_taken, 1)
            act.wait_ge(product, P_GATES + TT)
            nc.scalar.activation(Gate[:, :, :], PS[:, 5, 0:180].rearrange("p (t c) -> p t c", t=TT), ACT.Exp,
                                 scale=-1.0).then_inc(gates_taken, 1)

            mem_prompt_act(1, HT)
            mem_sample_act(1)
            for j in range(10):
                act.wait_ge(r_turned, j + 1)
                if j < 6:
                    nc.scalar.activation(QT[:, j // 2, j % 2, :], PS[:, j % 4, :], ACT.Copy, scale=SCALE).then_inc(r_took, 1)
                else:
                    K = (KTs, KTw)[(j - 6) // 2]
                    nc.scalar.copy(K[:, j % 2, :], PS[:, j % 4, :]).then_inc(r_took, 1)
            act.wait_ge(cp_sum, NB * NTL + PT + START.cp_sum)
            nc.scalar.copy(CRp[0:NCP, :], PS[0:NCP, 2, :]).then_inc(cp_rows, 1)
            act.wait_ge(cp_turned, NB + 1)
            nc.scalar.copy(BLp[:, :, 0:NCP], PS[:, 3, :].rearrange("p (s c) -> p s c", s=4)[:, :, 0:NCP]
                           ).then_inc(cp_cols, 1)
            act.wait_ge(cp_phi, NB + 1)
            nc.scalar.copy(KCp[:, :, 0:NCP], PS[:, 5, 0:256].rearrange("p (g n) -> p g n", g=2)[:, :, 0:NCP])
            nc.scalar.copy(VCp[0:NCP, :], PS[0:NCP, 5, 256:512]).then_inc(cp_took, 1)
            with act.Fori(0, GRP) as r:
                def exps(n):
                    t = Turn(r, n, 8)
                    gp, ti, nk = pair(n)
                    P, m = PP[n % 2], 200 + 8 * (n % 2)
                    act.wait_ge(pa_t, t.value(5, -5, base=START.pa_t))
                    for gg in range(2):
                        act.wait_ge(pa_m, t.value(3, gg + 1))
                        for s in range(2):
                            c = 2 + 2 * s + gg
                            ins = nc.scalar.activation(P[:, 1024 * gg + 512 * s:1024 * gg + 512 * s + nk],
                                                       PS[:, 2 * gg + s, 0:nk], ACT.Exp, bias=rs(m + c, m + c + 1),
                                                       accum_out=rs(m + 20 + c, m + 21 + c))
                        ins.then_inc(pa_p, 1)
                    act.wait_ge(pa_m, t.value(3, 3))
                    for gg in range(2):
                        ins = nc.scalar.activation(P[:, 2048 + 32 * gg:2048 + 32 * gg + NCP], PS[:, 7, 32 * gg:32 * gg + NCP],
                                                   ACT.Exp, bias=rs(m + gg, m + gg + 1),
                                                   accum_out=rs(m + 20 + gg, m + 21 + gg))
                    ins.then_inc(pa_p, 1)

                def took(n):
                    gp, ti, nk = pair(n)
                    act.wait_ge(pa_o, Turn(r, n, 8).value(1, 0, base=START.pa_o))
                    for b, (gg, s) in enumerate(BATCHES[0:3]):
                        act.wait_ge(pa_t, Turn(r, n, 8).value(5, b + 1, base=START.pa_t))
                        o = 1024 * gg + 512 * s
                        nc.scalar.copy(PTt[:, o:o + nk], PS[:, bank_of(n, b), 0:nk]).then_inc(pa_ta, 1)

                for n in range(8):
                    if n:
                        took(n - 1)
                    exps(n)
                took(7)
            for t in range(PT):
                act.wait_ge(yg_t, 2 * t + 1)
                nc.scalar.copy(HT[:, 2:6, 128 * t:128 * t + 128], PS[:, 6, :].rearrange("p (k c) -> p k c", k=4))
                act.wait_ge(yg_t, 2 * t + 2)
                nc.scalar.copy(HT[:, 6:8, 128 * t:128 * t + 128], PS[:, 7, 0:256].rearrange("p (k c) -> p k c", k=2)
                               ).then_inc(yg_c, 1)

            def front(t, prev):
                def took(first, last):
                    for j in range(first, last):
                        act.wait_ge(sa_ft, t.value(10, j + 1, base=START.sa_ft))
                        if j < 8:
                            nc.scalar.copy(SKT[:, :, 256 * j:256 * j + 256],
                                           PS[:, 6 + j % 2, :].rearrange("p (g c) -> p g c", g=2)).then_inc(sa_fa, 1)
                        else:
                            nc.scalar.copy(SWKT[:, j - 8, :], PS[:, 6 + j % 2, :]).then_inc(sa_fa, 1)

                if prev is not None:
                    exps_win(prev)
                took(0, 5)
                act.wait_ge(sa_cm, t.value(1, 1))
                act.wait_ge(sa_bt, t.value(6, -6, base=START.sa_bt))
                nc.scalar.activation(SPC[t.n % 2][:, 0:NC], PS[:, 5, 0:NC], ACT.Exp, bias=rs(140, 141),
                                     accum_out=rs(141, 142)).then_inc(sa_ce, 1)
                if prev is not None:
                    exps_sel(prev)
                took(7, 10)

            def exps_win(t):
                act.wait_ge(sa_m, t.value(2, 1, base=START.sa_m))
                nc.scalar.activation(SW[:, 0:512], PS[:, 4, :], ACT.Exp, bias=rs(151, 152), accum_out=rs(153, 154)
                                     ).then_inc(sa_p, 1)
                nc.scalar.activation(SW[:, 512:576], SW[:, 512:576], ACT.Exp, bias=rs(151, 152),
                                     accum_out=rs(154, 155)).then_inc(sa_p, 1)

            def exps_sel(t):
                act.wait_ge(sa_m, t.value(2, 2, base=START.sa_m))
                nc.scalar.activation(SM, SM, ACT.Exp, bias=rs(150, 151), accum_out=rs(152, 153)).then_inc(sa_p, 1)

            def middle(t):
                if last_turn(t):
                    exps_win(t)
                    exps_sel(t)

            def back(t, fronts):
                for j in range(0, 6, 2):
                    act.wait_ge(sa_bt, t.value(6, j + 1, base=START.sa_bt))
                    act.wait_ge(sa_used, t.value(6, j - 1, base=START.sa_used))
                    nc.scalar.copy(SPT[0], PS[:, 6, :].rearrange("p (s c) -> p s c", s=4)).then_inc(sa_ba, 1)

            sample_phase(act, front, middle, back)
            for j in range(TT):
                act.wait_ge(out_added, 3 * TT + j + 1)
                nc.scalar.activation(SQ, X[:, j, :], ACT.Square, accum_out=rs(12 + j, 13 + j)).then_inc(squared, 1)
                act.wait_ge(mean_sq, 3 + j + 1)
                nc.scalar.activation(rs(32 + j, 33 + j), rs(32 + j, 33 + j), ACT.Sqrt).then_inc(root, 1)

        @block.tensor
        def _(pe):
            def mm(out, lhsT, rhs, start=True, stop=True):
                return nc.tensor.matmul(out, lhsT, rhs, start=start, stop=stop, skip_group_check=True)

            def turn(out, in_):
                return nc.tensor.transpose(out, in_, ident[0:in_.shape[0], 0:in_.shape[0]])

            pe.wait_ge(const_in, 48)

            def norm_turns(first, count):
                for j in range(first, first + count):
                    pe.wait_ge(scaled, j + 1)
                    for half in range(2):
                        n = 2 * j + half
                        if n >= 4:
                            pe.wait_ge(h_taken, n - 3)
                        for k in range(4):
                            ins = turn(PS[:, n % 4, 128 * k:128 * k + 128],
                                       H[j % 2][:, 512 * half + 128 * k:512 * half + 128 * k + 128])
                        ins.then_inc(h_turned, 1)

            norm_turns(0, 2)
            pe.wait_ge(h_taken, 4)
            for l in range(2):
                pe.wait_ge(w_in[l], 16)
                for m in range(2):
                    for k in range(KD):
                        ins = mm(PS[:, 2 * l + m, :], memT[l][:, k, 128 * m:128 * m + 128], W[l][:, k, :],
                                 k == 0, k == KD - 1)
                    ins.then_inc(product, 1)
            for l in range(2):
                pe.wait_ge(kv_taken, 2 * (l + 1))
                for g in range(2):
                    for m in range(2):
                        ins = turn(PS[:, 4 + l, 256 * g + 128 * m:256 * g + 128 * m + 128],
                                   MKV[l][:, m, 128 * g:128 * g + 128])
                ins.then_inc(kt_turned, 1)

            def chunk(src, Wb, taken, beside=None):
                for t in range(TT):
                    if taken is not None:
                        pe.wait_ge(*taken(t))
                    for k in range(KD):
                        ins = mm(PS[:, t, :], src[:, k, 128 * t:128 * t + 128], Wb[:, k, :], k == 0, k == KD - 1)
                    ins.then_inc(product, 1)
                    if beside is not None:
                        beside(t)

            norm_turns(2, TT)
            pe.wait_ge(h_taken, 14)
            pe.wait_ge(w_in[0], 32)
            pe.wait_ge(kt_taken, 2)
            chunk(HT, W[0], None)
            pe.wait_ge(kt_taken, 2)
            pe.wait_ge(chunk_taken, TT)

            def sums(A, Bp, p, tiles, per, name, out):
                n, o = per * tiles, per * (tiles - 1 - p)
                mm(out, C(name)[:, o:o + n], A, p == 0, False)
                mm(out, C(name)[:, o + 1:o + 1 + n], Bp, False, p == tiles - 1).then_inc(cp_sum, 1)

            def turn_blocks(rows, bank, nch):
                for s in range(4):
                    ins = turn(PS[:, bank, 128 * s:128 * s + nch], rows[0:nch, 128 * s:128 * s + 128])
                ins.then_inc(cp_turned, 1)

            def phi(BL, bank, nch):
                for g in range(2):
                    mm(PS[:, bank, 128 * g:128 * g + nch], S("phi_k"), BL[:, g, 0:nch])
                for g in range(2):
                    ins = mm(PS[0:nch, bank, 256 + 128 * g:384 + 128 * g], BL[:, 2 + g, 0:nch], S("phi_v"))
                ins.then_inc(cp_phi, 1)

            def page_sums(t, first, last):
                if first == 0:
                    pe.wait_ge(cp_rows, t.value(1, 0, base=START.cp_rows))
                for k in range(first, last):
                    pe.wait_ge(cp_ra, t.value(NTL, k + 1, base=START.cp_ra))
                    pe.wait_ge(cp_rb, t.value(NTL, k + 1, base=START.cp_rb))
                    sums(CPR[0][k % 2], CPR[1][k % 2], k, NTL, 8 * TILE, "chunk4", PS[:, 5, :])

            def page_turn(t):
                pe.wait_ge(cp_rows, t.value(1, 1, base=START.cp_rows))
                pe.wait_ge(cp_cols, t.value(1, 0, base=START.cp_cols))
                turn_blocks(CR, 6, NC)

            def page_phi(t):
                pe.wait_ge(cp_cols, t.value(1, 1, base=START.cp_cols))
                pe.wait_ge(cp_took, t.value(1, 0, base=START.cp_took))
                phi(CBL, 7, NC)

            between = {(1, 5): (0, 1), (2, 1): (1, 2), (2, 7): (2, 3), (3, 2): (3, 4)}
            with pe.Fori(0, CT // 2) as i:
                for n in range(2):
                    t = Turn(i, n, 2)
                    w = (n + 1) % 2
                    pe.wait_ge(w_in[w], i * 16 + (32 if w == 1 else 48))
                    for q in range(4):
                        if q == 0:
                            pe.wait_ge(c_copied, t.value(1, 0, base=START.c_copied))
                            pe.wait_ge(s_copied, t.value(1, 0, base=START.s_copied))
                        elif q == 1:
                            pe.wait_ge(u_made, t.value(2, 0, base=START.u_made))
                        elif q == 2:
                            pe.wait_ge(b_used, t.value(1, 0, base=START.b_used))
                        else:
                            pe.wait_ge(z_used, t.value(1, 0, base=START.z_used))
                        for k in range(KD):
                            mm(PS[:, q, :], W[w][:, k, 128 * q:128 * q + 128], HT[:, k, 0:512], k == 0, k == KD - 1)
                            if (q, k) in between:
                                page_sums(t, *between[q, k])
                            if (q, k) == (3, 6):
                                page_turn(t)
                        for k in range(KD):
                            ins = mm(PS[:, 4, 64 * q:64 * q + 64], W[w][:, k, 128 * q:128 * q + 128],
                                     HT[:, k, 512:576], k == 0, k == KD - 1)
                        ins.then_inc(product, 1)
                    page_phi(t)

            def mem_prompt(l):
                b_ = mem_bufs(l)
                QTt, P, PTb = b_["QT"], b_["P"], b_["PT"]

                def q(n):
                    T, pr = l * PT + n, n % 2
                    pe.wait_ge(ma_q, T + 1)
                    if T >= 2:
                        pe.wait_ge(ma_done, T - 2)
                    if n == 0:
                        pe.wait_ge(ma_done, l * PT)
                    for g in range(2):
                        ins = turn(PS[:, 5, 256 * pr + 128 * g:256 * pr + 128 * g + 128], b_["QS"][:, 128 * g:128 * g + 128])
                    ins.then_inc(ma_qt, 1)

                def p(n):
                    T, pr = l * PT + n, n % 2
                    pe.wait_ge(ma_p, 4 * (T + 1))
                    pe.wait_ge(ma_td, T)
                    pe.wait_ge(ma_ta, T)
                    for h in range(4):
                        for m in range(2):
                            ins = turn(PS[:, 6 + h // 2, 256 * (h % 2) + 128 * m:256 * (h % 2) + 128 * m + 128],
                                       P[pr][:, h, 128 * m:128 * m + 128])
                        if h % 2:
                            ins.then_inc(ma_t, 1)

                def y(n):
                    T, pr = l * PT + n, n % 2
                    pe.wait_ge(ma_y, T + 1)
                    pe.wait_ge(ma_qc, min(T + 3, (l + 1) * PT))
                    pe.wait_ge(ma_done, T)
                    for g in range(2):
                        ins = turn(PS[:, 5, 256 * pr + 128 * g:256 * pr + 128 * g + 128], b_["OY"][:, 128 * g:128 * g + 128])
                    ins.then_inc(ma_yt, 1)

                def s(n):
                    T, pr = l * PT + n, n % 2
                    pe.wait_ge(ma_qc, T + 1)
                    if T >= 2:
                        pe.wait_ge(ma_p, 4 * (T - 1))
                    for h in range(4):
                        o = 64 * (h % 2)
                        ins = mm(PS[:, 2 * pr + h % 2, 256 * (h // 2):256 * (h // 2) + 256],
                                 QTt[pr][o:o + 64, 128 * (h // 2):128 * (h // 2) + 128], KTm[l][o:o + 64, h // 2, :])
                    ins.then_inc(ma_s, 1)

                def o(n):
                    T, pr = l * PT + n, n % 2
                    pe.wait_ge(ma_y, T)
                    pe.wait_ge(ma_td, T + 1)
                    pe.wait_ge(ma_ta, T + 1)
                    for h in range(4):
                        for m in range(2):
                            ins = mm(PS[:, 4, 256 * pr + 64 * h:256 * pr + 64 * h + 64],
                                     PTb[:, 256 * h + 128 * m:256 * h + 128 * m + 128],
                                     MKV[l][:, m, 256 + 64 * h:256 + 64 * h + 64], m == 0, m == 1)
                    ins.then_inc(ma_o, 1)

                mem_prompt_steps([(q, 0), (p, 1), (y, 2), (s, 0), (o, 1)])

            def mem_sample(l):
                b_ = mem_bufs(l)
                pe.wait_ge(ms_q, l + 1)
                pe.wait_ge(ma_done, PT * (l + 1))
                for g in range(2):
                    ins = turn(PS[:, 5, 128 * g:128 * g + 128], b_["QS"][:, 128 * g:128 * g + 128])
                ins.then_inc(ms_qt, 1)
                pe.wait_ge(ma_y, PT * (l + 1))

                def value(t, plus):
                    return t.value(1, plus, base=NB * l)

                def k(t):
                    n = t.n % 2
                    pe.wait_ge(ms_in[n], pair_value(t, 16) + 16 * l * NB // 2)
                    pe.wait_ge(ms_kc, value(t, START.ms_kc))
                    for g in range(2):
                        for m in range(2):
                            ins = turn(PS[:, 6, 256 * g + 128 * m:256 * g + 128 * m + 128],
                                       b_["MC"][n][0][:, m, 128 * g:128 * g + 128])
                    ins.then_inc(ms_kt, 1)

                def y(t):
                    n = t.n % 2
                    pe.wait_ge(ms_n, value(t, 1))
                    pe.wait_ge(ms_done, value(t, START.ms_done))
                    for g in range(2):
                        ins = turn(PS[:, 4, 128 * g:128 * g + 128], b_["SO"][n][:, 128 * g:128 * g + 128])
                    ins.then_inc(ms_y, 1)

                def p(t):
                    n = t.n % 2
                    pe.wait_ge(ms_p, value(t, 1))
                    pe.wait_ge(ms_c, value(t, START.ms_c))
                    for m in range(2):
                        ins = turn(PS[:, 7, 128 * m:128 * m + 128], b_["SP"][n][:, 128 * m:128 * m + 128])
                    ins.then_inc(ms_t, 1)

                def s(t):
                    n = t.n % 2
                    pe.wait_ge(ms_kc, value(t, START.ms_kc + 1))
                    pe.wait_ge(ms_qb, value(t, 1))
                    for g in range(2):
                        ins = mm(PS[:, n, 0:256], b_["QB"][n][:, g, :], b_["KTb"][n][:, 256 * g:256 * g + 256],
                                 g == 0, g == 1)
                    ins.then_inc(ms_s, 1)

                def o(t):
                    n = t.n % 2
                    pe.wait_ge(ms_vin[n], pair_value(t, 16) + 16 * l * NB // 2)
                    pe.wait_ge(ms_c, value(t, START.ms_c + 1))
                    for m in range(2):
                        ins = mm(PS[:, 2 + n, 0:256], b_["SPT"][n][:, 128 * m:128 * m + 128],
                                 b_["MC"][n][1][:, m, :], m == 0, m == 1)
                    ins.then_inc(ms_o, 1)

                mem_sample_steps(pe, [(k, -1), (y, 1), (p, 0), (s, -1), (o, 0)])
                pe.wait_ge(ms_qz, 5 * (l + 1))
                P0 = MQG0 if l == 0 else P1[0]
                for g in range(2):
                    ins = turn(PS[:, 5, 128 * g:128 * g + 128], P0[:, PT, 256 + 128 * g:256 + 128 * g + 128])
                ins.then_inc(ms_g, 1)

            def out_proj(YT, first, l):
                for n in range(2):
                    def beside(j):
                        t = Turn(0, CT + n, 1)
                        if j > 0:
                            page_sums(t, j - 1, j)
                        elif n == 1:
                            page_turn(Turn(0, CT, 1))
                            page_phi(Turn(0, CT, 1))

                    pe.wait_ge(w_in[(first + n) % 2], w_count(first + n))
                    chunk(YT, W[(first + n) % 2],
                          lambda t, n=n: (out_added, 2 * TT * l + t + 1 if n else 2 * TT * l),
                          beside if l == 0 else None)

            pe.wait_ge(conv_y, START.conv_y + CT)
            pe.wait_ge(cp_took, START.cp_took + CT)
            mem_prompt(0)
            mem_sample(0)
            pe.wait_ge(ms_gm, 1)
            pe.wait_ge(pad_zero, 3)
            pe.wait_ge(ma_done, PT)
            out_proj(YT0, B_OUT0, 0)
            page_turn(Turn(0, NB - 1, 1))
            page_phi(Turn(0, NB - 1, 1))
            pe.wait_ge(out_added, 2 * TT)
            norm_turns(7, TT)
            pe.wait_ge(h_taken, 2 * 12)
            with pe.Fori(0, 3) as i:
                for n in range(2):
                    t = Turn(i, n, 2)
                    w = (B_N + n) % 2
                    pe.wait_ge(w_in[w], i * 16 + w_count(B_N + n))
                    chunk(HT, W[w], lambda j: (chunk_taken, t.value(TT, j - 4, base=TT)))
            pe.wait_ge(w_in[(B_N + 6) % 2], w_count(B_N + 6))
            chunk(HT, W[(B_N + 6) % 2], lambda j: (chunk_taken, 7 * TT + j - 4))
            pe.wait_ge(wg_in, 16)
            for j in range(TT):
                for k in range(KD):
                    ins = mm(PS[:, 5, 36 * j:36 * j + 36], HT[:, k, 128 * j:128 * j + 128], Wg[:, k, :], k == 0, k == KD - 1)
                ins.then_inc(product, 1)
            pe.wait_ge(chunk_taken, 8 * TT)
            pe.wait_ge(gates_taken, 1)
            mem_prompt(1)
            mem_sample(1)
            pe.wait_ge(roped, 4)
            pe.wait_ge(ms_gm, 2)
            pe.wait_ge(ms_p, 2 * NB)
            pe.wait_ge(ms_n, 2 * NB)
            for j in range(10):
                if j >= 4:
                    pe.wait_ge(r_took, j - 3)
                for t in range(PT):
                    if j < 6:
                        r, g = j // 2, j % 2
                        src = P1[1 + r // 2][:, t, 256 * (r % 2) + 128 * g:256 * (r % 2) + 128 * g + 128]
                    else:
                        src = P1[3 + (j - 6) // 2][:, t, 256 + 128 * (j % 2):384 + 128 * (j % 2)]
                    ins = turn(PS[:, j % 4, 128 * t:128 * t + 128], src)
                ins.then_inc(r_turned, 1)
            for j in range(6):
                r, g = j // 2, j % 2
                src = P1[1 + r // 2][0:NS, PT, 256 * (r % 2) + 128 * g:256 * (r % 2) + 128 * g + 128]
                ins = turn(PS[:, 6, 64 * j:64 * j + 64], src)
            ins.then_inc(r_turned, 1)
            for j in range(4):
                src = P1[3 + j // 2][0:NS, PT, 256 + 128 * (j % 2):384 + 128 * (j % 2)]
                ins = turn(PS[:, 7, 64 * j:64 * j + 64], src)
            ins.then_inc(r_turned, 1)
            pe.wait_ge(r_took, 10)
            for p in range(PT):
                pe.wait_ge(cp_ra, START.cp_ra + NB * NTL + p + 1)
                pe.wait_ge(cp_rb, START.cp_rb + NB * NTL + p + 1)
                sums(PA[p % 2], PB[p % 2], p, PT, 8, "chunk", PS[0:8 * PT, 2, :])
            pe.wait_ge(cp_rows, START.cp_rows + NB + 1)
            turn_blocks(CRp, 3, NCP)
            pe.wait_ge(cp_cols, START.cp_cols + NB + 1)
            phi(BLp, 5, NCP)
            pe.wait_ge(cp_took, START.cp_took + NB + 1)
            with pe.Fori(0, GRP) as r:
                def scores(n):
                    t = Turn(r, n, 8)
                    gp, ti, nk = pair(n)
                    for gg in range(2):
                        pe.wait_ge(pa_p, t.value(3, gg - 2, base=START.pa_p))
                        q = Qz[:, gp, gg, 128 * ti:128 * ti + 128]
                        for s, K in enumerate((KTs, KTw)):
                            mm(PS[:, 2 * gg + s, 0:nk], q, K[:, gp, 0:nk], True, False)
                            ins = mm(PS[:, 2 * gg + s, 128 * ti:nk], ident, C("causal"), False, True)
                        ins.then_inc(pa_s, 1)
                    pe.wait_ge(pa_p, t.value(3, 0, base=START.pa_p))
                    for gg in range(2):
                        out = PS[:, 7, 32 * gg:32 * gg + NCP]
                        mm(out, Qz[:, gp, gg, 128 * ti:128 * ti + 128], KCp[:, gp, 0:NCP], True, False)
                        ins = mm(out, ident, C("cmp_add")[:, 32 * ti:32 * ti + NCP], False, True)
                    ins.then_inc(pa_s, 1)

                def turns(n, b):
                    t = Turn(r, n, 8)
                    gp, ti, nk = pair(n)
                    P, what = PP[n % 2], BATCHES[b]
                    bank = bank_of(n, b)
                    if what is None:
                        pe.wait_ge(pa_p, t.value(3, 3, base=START.pa_p))
                        if ti == 0:
                            pe.wait_ge(pa_cm, r * 2 + (n // PT + 1))
                    else:
                        pe.wait_ge(pa_p, t.value(3, what[0] + 1, base=START.pa_p))
                    pe.wait_ge(*taken(r, n, b - 2))
                    if what is None:
                        for gg in range(2):
                            ins = turn(PS[0:NCP, bank, 128 * gg:128 * gg + 128], P[:, 2048 + 32 * gg:2048 + 32 * gg + NCP])
                    else:
                        o = 1024 * what[0] + 512 * what[1]
                        for j in range(ti + 1):
                            ins = turn(PS[:, bank, 128 * j:128 * j + 128], P[:, o + 128 * j:o + 128 * j + 128])
                    ins.then_inc(pa_t, 1)

                def outs(n, b):
                    t = Turn(r, n, 8)
                    gp, ti, nk = pair(n)
                    what = BATCHES[b]
                    if b == 0:
                        pe.wait_ge(pa_mix, t.value(1, 0, base=START.pa_mix))
                    pe.wait_ge(*taken(r, n, b))
                    if what is None:
                        for gg in range(2):
                            h = 128 * gp + 64 * gg
                            ins = mm(PS[:, 4, 64 * gg:64 * gg + 64], PTt[0:NCP, 2048 + 128 * gg:2176 + 128 * gg],
                                     VCp[0:NCP, h:h + 64])
                        ins.then_inc(pa_o, 1)
                    else:
                        gg, s = what
                        o, h, c = 1024 * gg + 512 * s, 128 * gp + 64 * gg, 128 * (s + 1) + 64 * gg
                        for j in range(ti + 1):
                            mm(PS[:, 4, c:c + 64], PTt[:, o + 128 * j:o + 128 * j + 128], P1[4 + s][:, j, h:h + 64],
                               j == 0, j == ti)

                def attend(n):
                    for b in range(len(BATCHES) + 2):
                        if b < len(BATCHES):
                            turns(n, b)
                        if b >= 2:
                            outs(n, b - 2)

                pe.wait_ge(pa_q, r * 2 + 2)
                for n in range(8):
                    scores(n)
                    if n:
                        attend(n - 1)
                attend(7)
            for t in range(PT):
                pe.wait_ge(yg, t + 1)
                pe.wait_ge(yg_c, t)
                for k in range(4):
                    ins = turn(PS[:, 6, 128 * k:128 * k + 128], MIXB[:, t, 128 * k:128 * k + 128])
                ins.then_inc(yg_t, 1)
                for k in range(4, 6):
                    ins = turn(PS[:, 7, 128 * (k - 4):128 * (k - 3)], MIXB[:, t, 128 * k:128 * k + 128])
                ins.then_inc(yg_t, 1)
            pe.wait_ge(yg_c, PT)

            def front(t, prev):
                n = t.n % 2
                pe.wait_ge(sa_qb, t.value(1, 1))
                pe.wait_ge(sa_ba, t.value(3, -3, base=START.sa_ba))
                pe.wait_ge(sa_bd, t.value(3, -3, base=START.sa_bd))
                for j in range(10):
                    if j >= 2:
                        pe.wait_ge(sa_fa if FRONT[j - 2] == "A" else sa_fd, front_value(t, j - 2))
                    if j < 8:
                        if j % 4 == 0:
                            pe.wait_ge(sa_k[j // 4], t.value(128, 128))
                        for g in range(2):
                            for q in range(2):
                                p = 2 * j + q
                                ins = turn(PS[:, 6 + j % 2, 256 * g + 128 * q:256 * g + 128 * q + 128],
                                           SK[p // 8][:, p % 8, 128 * g:128 * g + 128])
                    else:
                        if j == 8:
                            pe.wait_ge(sa_w[n], pair_value(t, 16))
                        for p in range(4):
                            ins = turn(PS[:, 6 + j % 2, 128 * p:128 * p + 128], SWI[n][:, p, 128 * (j - 8):128 * (j - 7)])
                    ins.then_inc(sa_ft, 1)
                    if j == 1:
                        pe.wait_ge(sa_new, t.value(1, 0))
                        for g in range(2):
                            ins = mm(PS[:, 5, 0:NC], SQB[n][:, g, :],
                                     KC[:, g, bass.ds(t.at(1), 1), 0:NC].rearrange("p a n -> p (a n)"), g == 0, g == 1)
                        ins.then_inc(sa_cs, 1)
                    if j == 7:
                        pe.wait_ge(sa_cn, t.value(1, 1))
                        mm(PS[:, 5, 384:384 + NC], C("same_gt"), SPC[n][:, 0:NC]).then_inc(sa_imp, 1)

            def middle(t):
                n = t.n % 2
                pe.wait_ge(sa_fa, front_value(t, 9, "A"))
                pe.wait_ge(sa_fd, front_value(t, 9, "D"))
                pe.wait_ge(sa_mask, t.value(1, 1))
                pe.wait_ge(sa_m, t.value(2, 0, base=START.sa_m))
                pe.wait_ge(sa_p, t.value(3, 0, base=START.sa_p))
                for g in range(2):
                    mm(PS[:, 4, :], SQB[n][:, g, :], SWKT[:, g, :], g == 0, g == 1)
                for s in range(2):
                    for g in range(2):
                        ins = mm(PS[:, 5, 128 + 64 * s:192 + 64 * s], SQB[n][:, g, :], Kn[:, s, g, :], g == 0, g == 1)
                ins.then_inc(sa_part, 1)
                for c in (2, 3, 0, 1):
                    if c == 0:
                        ins.then_inc(sa_part, 1)
                        pe.wait_ge(sa_done, t.value(1, 0, base=START.sa_done))
                    for g in range(2):
                        ins = mm(PS[:, c, :], SQB[n][:, g, :], SKT[:, g, 512 * c:512 * c + 512], g == 0, g == 1)
                ins.then_inc(sa_s, 1)

            def back(t, fronts):
                n = t.n % 2
                sel, win, cmp = PS[:, 0, 0:256], PS[:, 1, 256:512], PS[:, 1, 0:256]
                tiles = [(SPC[n][:, 0:NC], VC[0:NC, bass.ds(t.at(1), 1), :].rearrange("p a c -> p (a c)"), cmp, True, True)]
                tiles += [(SW[:, 128 * j:128 * j + 128], SWI[n][:, j, 256:512], win, j == 0, j == 3) for j in range(4)]
                tiles.insert(2, (SW[:, 512:576], Vn[0:NS, 1, :], win, False, False))
                tiles += [(SM[:, 128 * j:128 * j + 128], SV[n][:, j, :], sel, j == 0, j == NPG - 1) for j in range(NPG)]
                tiles.insert(7, (SM[:, 2048:2112], Vn[0:NS, 0, :], sel, False, False))

                def turns(j):
                    if j < 2:
                        pe.wait_ge(sa_fa, t.value(FRONT.count("A"), FRONT.count("A") * fronts))
                    pe.wait_ge(sa_ba if j % 2 == 0 else sa_bd, t.value(3, j // 2, base=START.sa_ba))
                    for q, (p, _, _, _, _) in enumerate(tiles[4 * j:4 * j + 4]):
                        ins = turn(PS[0:p.shape[1], 6 + j % 2, 128 * q:128 * q + 128], p)
                    ins.then_inc(sa_bt, 1)

                pe.wait_ge(sa_p, t.value(3, 2, base=START.sa_p))
                turns(0)
                pe.wait_ge(sa_p, t.value(3, 3, base=START.sa_p))
                pe.wait_ge(sa_v[n], pair_value(t, 256))
                for j in range(6):
                    if j < 5:
                        turns(j + 1)
                    pe.wait_ge(sa_ba if j % 2 == 0 else sa_bd, t.value(3, j // 2 + 1, base=START.sa_ba))
                    for q, (p, v, out, first, last) in enumerate(tiles[4 * j:4 * j + 4]):
                        ins = mm(out, SPT[j % 2][0:p.shape[1], q, :], v, first, last)
                    ins.then_inc(sa_used, 1)
                pe.wait_ge(sa_mix, t.value(1, 1))
                for gp in range(2):
                    ins = turn(PS[:, 1, 128 * gp:128 * gp + 128], SO[:, 128 * gp:128 * gp + 128])
                ins.then_inc(sa_y, 1)

            pe.wait_ge(r_spread, 6)
            pe.wait_ge(pa_mix, START.pa_mix + 24)
            sample_phase(pe, front, middle, back)
            for k in range(6):
                src = P1[5][0:NS, PT, 256 + 128 * k:384 + 128 * k] if k < 2 else P1[6][0:NS, PT, 128 * (k - 2):128 * (k - 1)]
                ins = turn(PS[:, 2, 64 * k:64 * k + 64], src)
            ins.then_inc(sz_t, 1)
            pe.wait_ge(sz_done, 1)
            pe.wait_ge(ht_zero, 1)
            out_proj(HT, B_OUT1, 1)

        @block.vector
        def _(dve):
            lk = Links(dve, dve_links)
            tt, tcopy, ts = nc.vector.tensor_tensor, nc.vector.tensor_copy, nc.vector.tensor_scalar
            bc = lambda ap, n: ap.unsqueeze(len(ap.shape)).to_broadcast(list(ap.shape) + [n])

            def norm_dve(first, count, number):
                a, b = 20 + first, 20 + first + count
                dve.wait_ge(squared, first + count)
                ts(rs(a, b), rs(first, first + count), 1.0 / D, EPS, ALU.mult, ALU.add).then_inc(mean_sq, 1)
                dve.wait_ge(root, number + 1)
                nc.vector.reciprocal(rs(a, b), rs(a, b)).then_inc(rstd, 1)

            def take_h(j, outs):
                for half in range(2):
                    n = 2 * j + half
                    dve.wait_ge(h_turned, n + 1)
                    for dst, g in outs:
                        ins = tt(dst[:, 4 * half:4 * half + 4, :],
                                 PS[:, n % 4, :].rearrange("p (k c) -> p k c", k=4), bc(g[:, 4 * half:4 * half + 4], 128),
                                 ALU.mult)
                    ins.then_inc(h_taken, 1)

            nc.vector.memset(X[NS:128, PT, :], 0.0).then_inc(x_zero, 1)
            dve.wait_ge(const_in, 48)
            norm_dve(0, 2, 0)
            for j in range(2):
                take_h(j, [(memT[l][:, :, 128 * j:128 * j + 128], S("g_mem")[:, 8 * l:8 * l + 8]) for l in range(2)])
            norm_dve(2, TT, 1)
            for j in range(2, 7):
                take_h(j, [(HT[:, :, 128 * (j - 2):128 * (j - 1)], S("g_x")[:, 0:8])])
            def page_prod0(t, first, last):
                for k in range(first, last):
                    dve.wait_ge(cp_in[k % 2], t.value(32 * TILE, 16 * TILE * (k // 2 + 1)))
                    dve.wait_ge(cp_ra, t.value(NTL, k, base=START.cp_ra))
                    tt(tile_view(CPM[0]), tile_view(PG[k % 2]), tile_pos("tile_pos0"), ALU.mult).then_inc(cp_a, 1)
                    dve.wait_ge(cp_a, t.value(NTL, k + 1, base=START.cp_a))
                    lk.link(tt(CPM[0][:, 0:1024], CPM[0][:, 0:1024], CPM[0][:, 1024:2048], ALU.add))
                    dve.wait_ge(cp_sum, t.value(NTL, k - 1, base=START.cp_sum))
                    tt(CPR[0][k % 2], CPM[0][:, 0:512], CPM[0][:, 512:1024], ALU.add).then_inc(cp_ra, 1)



            dve.wait_ge(pad_zero, 3)
            dve.wait_ge(product, PBASE[B_C0])
            for t in range(TT):
                dve.wait_ge(sig_exp, t + 1)
                lk.link(ts(GE0[:, t, :], GE0[:, t, :], 1.0, None, ALU.add))
                lk.link(nc.vector.reciprocal(GE0[:, t, :], GE0[:, t, :]))
                lk.link(tt(MQG0[:, t, 256:512], MQG0[:, t, 256:512], GE0[:, t, :], ALU.mult))
            with dve.Fori(0, CT // 2) as i:
                lk.enter(i, 2 * (10 + NTL))
                for n in range(2):
                    t = Turn(i, n, 2)
                    Up, Us = U[n][:, 0:514], U[n][:, 514:594].rearrange("p (b c) -> p b c", b=NB)
                    Yp, Ys = Y[:, 0:512], Y[:, 512:576].rearrange("p (b c) -> p b c", b=NB)
                    sb = Sb.rearrange("p (q b c) -> p q b c", q=4, b=NB)
                    wj = lambda j: small[:, bass.ds(t.at(3, SMALL["conv_w"][0] + j), 1)]
                    page_prod0(t, 0, 2)
                    dve.wait_ge(product, t.value(4, 2, base=PBASE[B_CONV]))
                    dve.wait_ge(c_copied, t.value(1, 1, base=START.c_copied))
                    dve.wait_ge(state_set, t.value(1, 1))
                    dve.wait_ge(state_kept, t.value(2, -2, base=START.state_kept))
                    tt(Up[:, 2:514], Cb[:, 0:512], PS[:, 1, :], ALU.mult).then_inc(u_made, 1)
                    dve.wait_ge(u_made, t.value(2, 1, base=START.u_made))
                    tcopy(CS[:, bass.ds(t.at(18), 2)], Up[:, 512:514]).then_inc(state_kept, 1)
                    lk.link(ts(Yp, Up[:, 0:512], wj(0), None, ALU.mult))
                    for j in (1, 2):
                        lk.link(nc.vector.scalar_tensor_tensor(Yp, Up[:, j:j + 512], wj(j), Yp, ALU.mult, ALU.add))
                    page_prod0(t, 2, NTL)
                    dve.wait_ge(product, t.value(4, 3, base=PBASE[B_CONV]))
                    tt(Yp, Yp, PS[:, 2, :], ALU.mult).then_inc(b_used, 1)

                    dve.wait_ge(s_copied, t.value(1, 1, base=START.s_copied))
                    tt(Us[:, :, 2:10], sb[:, 0], sb[:, 1], ALU.mult).then_inc(u_made, 1)
                    dve.wait_ge(u_made, t.value(2, 2, base=START.u_made))
                    tcopy(CS[:, bass.ds(t.at(18, 2), 16)].rearrange("p (b c) -> p b c", b=NB), Us[:, :, 8:10]
                          ).then_inc(state_kept, 1)
                    lk.link(ts(Ys, Us[:, :, 0:8], wj(0), None, ALU.mult))
                    for j in (1, 2):
                        lk.link(nc.vector.scalar_tensor_tensor(Ys, Us[:, :, j:j + 8], wj(j), Ys, ALU.mult, ALU.add))
                    lk.did(tt(Ys, Ys, sb[:, 2], ALU.mult))
                    dve.wait_ge(z_exp, t.value(1, 1))
                    lk.link(ts(E, E, 1.0, None, ALU.add))
                    lk.link(nc.vector.reciprocal(E, E))
                    lk.did(tt(E[:, 0:512], E[:, 0:512], PS[:, 3, :], ALU.mult))
                    tt(E[:, 512:576], E[:, 512:576], Sb[:, 192:256], ALU.mult).then_inc(z_used, 1)
                    dve.wait_ge(z_used, t.value(1, 1, base=START.z_used))
                    dve.wait_ge(b_used, t.value(1, 1, base=START.b_used))
                    lk.settle()
                    tt(YT0f[:, bass.ds(t.at(TOK, 2 * TOK), 576)], Y, E, ALU.mult).then_inc(conv_y, 1)
                lk.leave(CT // 2)

            def mem_prompt_dve(l):
                b_ = mem_bufs(l)
                P0 = MQG0 if l == 0 else P1[0]

                def scale_q(n):
                    if n:
                        dve.wait_ge(ma_qt, l * PT + n)
                    ts(b_["QS"], P0[:, n, 0:256], SCALE, None, ALU.mult).then_inc(ma_q, 1)

                def take_p(n):
                    T = l * PT + n
                    dve.wait_ge(ma_t, 2 * T + 1)
                    if T:
                        dve.wait_ge(ma_o, T)
                    tcopy(b_["PT"][:, 0:512], PS[:, 6, :]).then_inc(ma_td, 1)

                def maxes(n):
                    T, pr = l * PT + n, n % 2
                    dve.wait_ge(ma_s, T + 1)
                    for k in range(2):
                        nc.vector.tensor_reduce(stats[:, 60 + 8 * pr + k:63 + 8 * pr + k:2],
                                                PS[:, 2 * pr + k, :].rearrange("p (h m) -> p h m", h=2), AX, ALU.max,
                                                negate=True).then_inc(ma_m, 1)

                def gate(n):
                    T, pr = l * PT + n, n % 2
                    dve.wait_ge(ma_p, 4 * (T + 1))
                    lk.link(nc.vector.reciprocal(rs(92, 96), rs(76 + 8 * pr, 80 + 8 * pr)))
                    dve.wait_ge(ma_o, T + 1)
                    if n:
                        dve.wait_ge(ma_yt, T)
                    OY = b_["OY"].rearrange("p (h c) -> p h c", h=4)
                    lk.link(tt(OY, PS[:, 4, 256 * pr:256 * pr + 256].rearrange("p (h c) -> p h c", h=4),
                               bc(rs(92, 96), 64), ALU.mult))
                    tt(b_["OY"], b_["OY"], P0[:, n, 256:512], ALU.mult).then_inc(ma_y, 1)

                scale_q(0)
                mem_prompt_steps([(take_p, 1), (scale_q, -1), (maxes, 0), (gate, 1)])

            def mem_sample_dve(l, YT):
                b_ = mem_bufs(l)
                YTf = HTf if l else YT0f
                P0 = MQG0 if l == 0 else P1[0]
                dve.wait_ge(ma_qt, PT * (l + 1))
                ts(b_["QS"], P0[:, PT, 0:256], SCALE, None, ALU.mult).then_inc(ms_q, 1)
                dve.wait_ge(ms_qt, l + 1)
                dve.wait_ge(ms_qz, 5 * l + 1)
                for h in range(4):
                    o = 64 * (h % 2)
                    tcopy(b_["QZ"][o:o + 64, h // 2, :, 32 * h:32 * h + 8],
                          PS[o:o + 64, 5, 128 * (h // 2):128 * (h // 2) + 64].rearrange("p (b t) -> p b t", b=NB)
                          ).then_inc(ms_qz, 1)

                def value(t, plus):
                    return t.value(1, plus, base=NB * l)

                def take_y(t):
                    dve.wait_ge(ms_y, value(t, START.ms_y + 1))
                    for h in range(4):
                        o, g = 64 * (h % 2), h // 2
                        ins = tcopy(YTf[o:o + 64, bass.ds(t.at(NT, g * TOK + SEQ), NT)],
                                    PS[o:o + 64, 4, 128 * g + 32 * h:128 * g + 32 * h + NT])
                        if h < 3:
                            lk.did(ins)
                    ins.then_inc(ms_done, 1)

                def take_p(t):
                    dve.wait_ge(ms_t, value(t, 1))
                    tcopy(b_["SPT"][t.n % 2], PS[:, 7, 0:256]).then_inc(ms_c, 1)

                def maxes(t):
                    n = t.n % 2
                    dve.wait_ge(ms_s, value(t, START.ms_s + 1))
                    nc.vector.tensor_reduce(rs(100 + n, 101 + n), PS[:, n, 0:256], AX, ALU.max, negate=True
                                            ).then_inc(ms_m, 1)

                def scale_o(t):
                    n = t.n % 2
                    dve.wait_ge(ms_p, value(t, 1))
                    lk.link(nc.vector.reciprocal(rs(108 + n, 109 + n), rs(104 + n, 105 + n)))
                    dve.wait_ge(ms_o, value(t, START.ms_o + 1))
                    dve.wait_ge(ms_y, value(t, START.ms_y - 1))
                    ts(b_["SO"][n], PS[:, 2 + n, 0:256], rs(108 + n, 109 + n), None, ALU.mult).then_inc(ms_n, 1)

                mem_sample_steps(dve, [(take_y, 1), (take_p, 0), (maxes, -1), (scale_o, 0)], lk, 4)
                lk.settle()
                dve.wait_ge(ms_g, l + 1)
                dve.wait_ge(ms_done, START.ms_done + NB * (l + 1))
                tt(YT[:, 0:2, SEQ:SEQ + NS], YT[:, 0:2, SEQ:SEQ + NS],
                   PS[:, 5, 0:256].rearrange("p (g c) -> p g c", g=2)[:, :, 0:NS], ALU.mult).then_inc(ms_gm, 1)

            def add_out(first, l):
                for n in range(2):
                    pages = Turn(0, CT + n, 1)
                    for t in range(TT):
                        if l == 0 and t < PT:
                            page_prod0(pages, t, t + 1)

                        dve.wait_ge(product, PBASE[first + n] + t + 1)
                        xs = X[:, t, 512 * n:512 * n + 512]
                        tt(xs, xs, PS[:, t, :], ALU.add).then_inc(out_added, 1)
                        if (l, n) == (1, 1):
                            finish(t)

            def finish(t):
                q = rs(32 + t, 33 + t)
                dve.wait_ge(squared, 12 + t + 1)
                ts(q, rs(12 + t, 13 + t), 1.0 / D, EPS, ALU.mult, ALU.add).then_inc(mean_sq, 1)
                dve.wait_ge(root, 3 + t + 1)
                lk.link(nc.vector.reciprocal(q, q))
                if t == 0:
                    dve.wait_ge(gfin_in, 16)
                if t >= 2:
                    dve.wait_ge(y_out[t % 2], 16 * (t // 2))
                nc.vector.scalar_tensor_tensor(fin[t % 2], X[:, t, :], q, gfin, ALU.mult, ALU.mult).then_inc(y_ready, 1)

            mem_prompt_dve(0)
            mem_sample_dve(0, YT0)
            add_out(B_OUT0, 0)
            norm_dve(7, TT, 2)
            for j in range(TT):
                take_h(7 + j, [(HT[:, :, 128 * j:128 * j + 128], S("g_x")[:, 8:16])])
            for j, z in enumerate((P1[0][:, :, 256:512], P1[5][:, :, 256:512], P1[6][:, :, 0:256], P1[6][:, :, 256:512])):
                dve.wait_ge(sig_exp, TT + j + 1)
                lk.link(ts(GE[j % 2], GE[j % 2], 1.0, None, ALU.add))
                lk.link(nc.vector.reciprocal(GE[j % 2], GE[j % 2]))
                tt(z, z, GE[j % 2], ALU.mult).then_inc(sig_done, 1)
            dve.wait_ge(gates_taken, 1)
            lk.link(ts(Gate, Gate, 1.0, None, ALU.add))
            nc.vector.reciprocal(Gate, Gate).then_inc(sig_done, 1)

            mem_prompt_dve(1)
            mem_sample_dve(1, HT)
            dve.wait_ge(qz_zero, 2)
            dve.wait_ge(r_turned, 11)
            for g in range(KVH):
                o, gp = 64 * (g % 2), g // 2
                for r in range(GRP):
                    ins = ts(QZ[o:o + 64, gp, :, 32 * g + 8 * r:32 * g + 8 * r + 8],
                             PS[o:o + 64, 6, 64 * (2 * r + gp):64 * (2 * r + gp) + 64].rearrange("p (b t) -> p b t", b=NB),
                             SCALE, None, ALU.mult)
                ins.then_inc(r_spread, 1)
            dve.wait_ge(r_turned, 12)
            tcopy(Kn.rearrange("p s g n -> p (s g n)"), PS[:, 7, 0:256]).then_inc(r_spread, 2)
            for p in range(PT):
                if p >= 2:
                    dve.wait_ge(cp_sum, NB * NTL + START.cp_sum + p - 1)
                tt(heads(PA[p % 2][:, 0:256]), heads(P1[2][:, p, 256:512]), row_pos("pos0", 0), ALU.mult)
                tt(heads(PA[p % 2][:, 256:512]), heads(P1[3][:, p, 0:256]), row_pos("pos0", 1), ALU.mult
                   ).then_inc(cp_ra, 1)


            dve.wait_ge(cp_sum, PT + NB * NTL + START.cp_sum)
            dve.wait_ge(r_took, 10)
            stt = nc.vector.scalar_tensor_tensor
            dve.wait_ge(kv_stored, KV_STORED)
            lk.link(nc.vector.memset(Qz, 0.0))
            with dve.Fori(0, GRP) as r:
                lk.enter(r, 8 * 4)
                dve.wait_ge(pa_s, START.pa_s + r * 24)
                for gg in range(2):
                    o = 64 * gg
                    tcopy(Qz[o:o + 64, :, gg, :],
                          QTf[o:o + 64, bass.ds(r * 1024, 1024)].rearrange("p (g c) -> p g c", g=2)).then_inc(pa_q, 1)

                def maxes(n):
                    t = Turn(r, n, 8)
                    gp, ti, nk = pair(n)
                    m = 200 + 8 * (n % 2)
                    for gg in range(2):
                        dve.wait_ge(pa_s, t.value(3, gg + 1, base=START.pa_s))
                        nc.vector.tensor_reduce(rs(m + 2 + gg, m + 5 + gg)[:, 0:3:2], PS[:, 2 * gg:2 * gg + 2, 0:nk], AX, ALU.max,
                                                negate=True).then_inc(pa_m, 1)
                    dve.wait_ge(pa_s, t.value(3, 3, base=START.pa_s))
                    nc.vector.tensor_reduce(rs(m, m + 2), PS[:, 7, 0:64].rearrange("p (g n) -> p g n", g=2)[:, :, 0:NCP],
                                            AX, ALU.max, negate=True).then_inc(pa_m, 1)

                def cmp_mask(n):
                    m = 220 + 8 * (n % 2)
                    dve.wait_ge(pa_p, Turn(r, n, 8).value(3, 3, base=START.pa_p))
                    for gg in range(2):
                        c = PP[n % 2][:, 2048 + 32 * gg:2048 + 32 * gg + NCP]
                        ins = nc.vector.tensor_tensor_reduce(c, c, C("cmp_mul")[:, 0:NCP], 1.0, 0.0, ALU.mult,
                                                             ALU.add, rs(m + gg, m + gg + 1))
                    ins.then_inc(pa_cm, 1)

                def took(n):
                    gp, ti, nk = pair(n)
                    dve.wait_ge(pa_o, Turn(r, n, 8).value(1, 0, base=START.pa_o))
                    dve.wait_ge(pa_t, Turn(r, n, 8).value(5, 4, base=START.pa_t))
                    tcopy(PTt[:, 1536:1536 + nk], PS[:, bank_of(n, 3), 0:nk]).then_inc(pa_td, 1)
                    dve.wait_ge(pa_t, Turn(r, n, 8).value(5, 5, base=START.pa_t))
                    tcopy(PTt[0:NCP, 2048:2304], PS[0:NCP, bank_of(n, 4), 0:256]).then_inc(pa_td, 1)

                def mix(n):
                    t = Turn(r, n, 8)
                    gp, ti, nk = pair(n)
                    m = 220 + 8 * (n % 2)
                    if ti == 0:
                        dve.wait_ge(pa_cm, r * 2 + (n // PT + 1))
                    lk.link(ts(rs(240, 246), rs(m, m + 6), 1e-30, None, ALU.max))
                    lk.link(nc.vector.reciprocal(rs(240, 246), rs(240, 246)))
                    gate = Gate[:, ti, :].rearrange("p (s h) -> p s h", s=3)[:, :, bass.ds(r * KVH + 2 * gp, 2)]
                    lk.link(tt(rs(250, 256).rearrange("p (s g) -> p s g", s=3), rs(240, 246).rearrange("p (s g) -> p s g", s=3),
                               gate, ALU.mult))
                    dve.wait_ge(pa_o, t.value(1, 1, base=START.pa_o))
                    lk.link(tt(Om.rearrange("p (h d) -> p h d", d=HD), PS[:, 4, 0:384].rearrange("p (h d) -> p h d", d=HD),
                               bc(rs(250, 256), HD), ALU.mult))
                    nc.vector.tensor_reduce(MIXf[:, bass.ds(r * 256 + (MIX * ti + 128 * gp), 128)],
                                            Om.rearrange("p (s x) -> p x s", s=3), AX, ALU.add).then_inc(pa_mix, 1)

                for n in range(8):
                    maxes(n)
                    if n:
                        took(n - 1)
                    if n % PT == 0:
                        cmp_mask(n)
                    if n:
                        mix(n - 1)
                took(7)
                mix(7)
                lk.leave(GRP)
            dve.wait_ge(pa_mix, START.pa_mix + 24)
            for t in range(PT):
                lk.did(tt(MIXB[:, t, 0:256], MIXB[:, t, 0:256], P1[5][:, t, 256:512], ALU.mult))
                tt(MIXB[:, t, 256:768], MIXB[:, t, 256:768], P1[6][:, t, :], ALU.mult).then_inc(yg, 1)

            def front(t, prev):
                n = t.n % 2
                def took(j):
                    dve.wait_ge(sa_ft, t.value(10, j + 1, base=START.sa_ft))
                    tcopy(SKT[:, :, 256 * j:256 * j + 256], PS[:, 6 + j % 2, :].rearrange("p (g c) -> p g c", g=2)
                          ).then_inc(sa_fd, 1)

                def cmp_max():
                    dve.wait_ge(sa_cs, t.value(1, 1))
                    nc.vector.tensor_reduce(rs(140, 141), PS[:, 5, 0:NC], AX, ALU.max, negate=True).then_inc(sa_cm, 1)

                if prev is None:
                    cmp_max()
                else:
                    masks(prev, cmp_max)
                took(5)
                took(6)
                dve.wait_ge(sa_ce, t.value(1, 1))
                lk.link(ts(rs(155, 156), rs(141, 142), 1e-30, None, ALU.max))
                lk.link(nc.vector.reciprocal(rs(155, 156), rs(155, 156)))
                ts(SPC[n][:, 0:NC], SPC[n][:, 0:NC], rs(155, 156), None, ALU.mult).then_inc(sa_cn, 1)
                dve.wait_ge(sa_imp, t.value(1, 1))
                lk.link(tcopy(SIMP[:, 1:1 + NC], PS[:, 5, 384:384 + NC]))
                lk.link(tt(SCH, SIMP[:, 1:129], SIMP[:, 0:128], ALU.add))
                lk.link(nc.vector.tensor_reduce(SSC[:, 0:NSB - 1], SCH.rearrange("p (n c) -> p n c", c=4), AX, ALU.add))
                lk.link(tt(SS2[:, 0:NSB], SSC[:, 0:NSB], C("forced")[:, 0:NSB], ALU.add))
                for k in range(2):
                    step_dve()
                    lk.link(nc.vector.max(SM8, SS2[:, 0:NSB]))
                    step_dve()
                    lk.link(nc.vector.match_replace(SS2[:, 0:NSB], SM8, SS2[:, 0:NSB], -1.0))
                ts(SMB[:, 0:NSB], SS2[:, 0:NSB], 0.0, NEG, ALU.is_ge, ALU.mult).then_inc(sa_mask, 1)

            def masks(t, cmp_max):
                lk.settle()
                dve.wait_ge(sa_mask, t.value(1, 1))
                dve.wait_ge(sa_part, t.value(2, 1))
                dve.wait_ge(sa_bt, t.value(6, 0, base=START.sa_bt))
                ttr = nc.vector.tensor_tensor_reduce
                lk.did(tcopy(SNM, cst[:, bass.ds(t.at(-NT, CONST["new_add"][0] + NT * (NB - 1)), 64)]))
                lk.link(tt(PS[:, 4, 0:8], PS[:, 4, 0:8], C("win_add"), ALU.add))
                step_dve()
                lk.did(ttr(SM[:, 2048:2112], PS[:, 5, 128:192], SNM, 1.0, -3e38, ALU.add, ALU.max, rs(146, 147)))
                ttr(SW[:, 512:576], PS[:, 5, 192:256], SNM, 1.0, -3e38, ALU.add, ALU.max, rs(148, 149)).then_inc(sa_new, 1)
                lk.link(nc.vector.tensor_reduce(rs(147, 148), PS[:, 4, :], AX, ALU.max))
                dve.wait_ge(sa_new, t.value(1, 1))
                nc.vector.tensor_reduce(rs(151, 152), rs(147, 149), AX, ALU.max, negate=True).then_inc(sa_m, 1)
                for c in (2, 3, 0, 1):
                    if c == 2:
                        dve.wait_ge(sa_part, t.value(2, 2))
                        step_dve(396)
                    elif c == 0:
                        dve.wait_ge(sa_s, t.value(1, 1, base=START.sa_s))
                        step_dve(397)
                    lk.did(ttr(SM[:, 512 * c:512 * c + 512].rearrange("p (n k) -> p n k", k=SB),
                               PS[:, c, :].rearrange("p (n k) -> p n k", k=SB), bc(SMB[:, 8 * c:8 * c + 8], SB), 1.0, -3e38,
                               ALU.add, ALU.max, rs(142 + c, 143 + c)))
                lk.settle()
                nc.vector.tensor_reduce(rs(150, 151), rs(142, 147), AX, ALU.max, negate=True).then_inc(sa_m, 1)
                if cmp_max is not None:
                    cmp_max()

            def middle(t):
                if last_turn(t):
                    masks(t, None)

            def back(t, fronts):
                def took(j):
                    dve.wait_ge(sa_bt, t.value(6, j + 1, base=START.sa_bt))
                    dve.wait_ge(sa_used, t.value(6, j - 1, base=START.sa_used))
                    k = 4 if j < 5 else 3
                    tcopy(SPT[1][:, 0:k, :], PS[:, 7, 0:128 * k].rearrange("p (s c) -> p s c", s=k)).then_inc(sa_bd, 1)

                took(1)
                dve.wait_ge(sa_p, t.value(3, 3, base=START.sa_p))
                lk.link(tt(rs(153, 154), rs(153, 154), rs(154, 155), ALU.add))
                lk.link(ts(rs(156, 158), rs(152, 154), 1e-30, None, ALU.max))
                lk.link(nc.vector.reciprocal(rs(156, 158), rs(156, 158)))
                gr = Grow[:, bass.ds(t.at(1), 1), :].squeeze(1)
                lk.did(tcopy(rs(170, 173), gr))
                lk.link(tt(rs(158, 160), rs(156, 158), gr[:, 1:3], ALU.mult))
                took(3)
                dve.wait_ge(sa_used, t.value(6, 2, base=START.sa_used))
                dve.wait_ge(sa_y, t.value(1, 0, base=START.sa_y))
                lk.link(ts(SO, PS[:, 1, 0:256], rs(170, 171), None, ALU.mult))
                lk.link(stt(SO, PS[:, 1, 256:512], rs(159, 160), SO, ALU.mult, ALU.add))
                took(5)
                dve.wait_ge(sa_used, t.value(6, 6, base=START.sa_used))
                stt(SO, PS[:, 0, 0:256], rs(158, 159), SO, ALU.mult, ALU.add).then_inc(sa_mix, 1)
                dve.wait_ge(sa_y, t.value(1, 1, base=START.sa_y))
                for g in range(KVH):
                    o, gp = 64 * (g % 2), g // 2
                    ins = tcopy(HT[o:o + 64, 2 + gp:7 + gp:2, bass.ds(t.at(NT, SEQ), NT)],
                                PS[o:o + 64, 1, 128 * gp + 32 * g:128 * gp + 32 * g + 24].rearrange("p (r t) -> p r t", r=GRP))
                    if g < 3:
                        lk.did(ins)
                ins.then_inc(sa_done, 1)

            dve.wait_ge(kv_stored, KV_STORED)
            dve.wait_ge(gates_back, 16 * 36)
            dve.wait_ge(yg_c, PT)
            lk.did(nc.vector.memset(SIMP, 0.0))
            lk.link(nc.vector.memset(SSC, 0.0))
            sample_phase(dve, front, middle, back, lk)
            dve.wait_ge(sz_t, 1)
            dve.wait_ge(sa_done, START.sa_done + NB)
            tt(HT[:, 2:8, SEQ:SEQ + NS], HT[:, 2:8, SEQ:SEQ + NS], PS[:, 2, 0:384].rearrange("p (k c) -> p k c", k=6),
               ALU.mult).then_inc(sz_done, 1)
            add_out(B_OUT1, 1)


def w_count(n):
    return 16 * (n // 2 + 1)


def front_value(t, j, who=None):
    who = who or FRONT[j]
    return t.value(FRONT.count(who), FRONT[:j + 1].count(who))


def last_turn(t):
    return isinstance(t.i, int) and 2 * t.i + t.n == NB - 1


def pair_value(t, each):
    return t.i * each + (t.n // 2 + 1) * each


def constants():
    c = np.zeros((128, CONST_W), np.float32)
    p = np.arange(128)

    def put(name, v):
        a, w = CONST[name]
        c[:, a:a + w] = v

    put("ident", np.eye(128))
    put("causal", np.where(p[None, :] <= p[:, None], 0.0, NEG))
    q_pos = p[:, None, None] + 128 * np.arange(PT)[None, :, None]
    seen = (16 * np.arange(32)[None, None, :] + 31 <= q_pos).reshape(128, 128)
    put("cmp_add", np.where(seen, 0.0, NEG))
    put("cmp_mul", seen)
    real = p % 32 < 24
    put("same_gt", (p[:, None] // 32 == p[None, :] // 32) & (p[:, None] % 8 == p[None, :] % 8) & real[:, None] & real[None, :])
    new = np.full((128, 15, 8), NEG)
    new[:, NB - 1, :] = np.where(np.arange(8)[None, :] <= p[:, None] % 8, 0.0, NEG)
    put("new_add", new.reshape(128, 120))
    put("win_add", np.where(np.arange(8)[None, :] <= p[:, None] % 8, NEG, 0.0))
    put("chunk", p[:, None] // 16 + 8 * (PT - 1) == np.arange(58)[None, :])
    put("chunk4", p[:, None] // 4 + 8 * TILE * (NTL - 1) == np.arange(226)[None, :])
    pos = (p[:, None] + 128 * np.arange(TT)[None, :]).astype(np.float32)
    pos[:, PT] = PAST + p % NT
    inv = (np.float32(500000.0) ** (-np.arange(8, dtype=np.float32) * np.float32(2.0) / np.float32(16))).astype(np.float32)
    ang = (pos[:, :, None] * inv).astype(np.float32)
    put("cos", np.cos(ang).reshape(128, 40))
    put("sin", np.sin(ang).reshape(128, 40))
    forced = np.zeros(NSB + 1)
    forced[[0, NSB - 2, NSB - 1]] = 1e4
    put("forced", forced)
    return c


def lay_out(x):
    f = {k: np.asarray(v) for k, v in x.items()}
    out = {"xp": f["x_prompt"][0], "xs": f["x_sample"].reshape(NS, D), "mem": f["mem_prompt"][0],
           "cmem": f["cache_mem_kv"].reshape(2, NB, NMEM, 512), "ccmp": f["cache_cmp_kv"].reshape(POOL, PAGE, 512),
           "csel": f["cache_sel_kv"].reshape(POOL, PAGE, 512), "pages": f["page_table"].reshape(1, NB * NPG),
           "win": f["state_win_kv"].reshape(NB, WIN, 512), "const": constants()}

    def rgd(a, axis):
        sh = a.shape
        a = a.reshape(sh[:axis] + (KVH, GRP, sh[axis] // 12) + sh[axis + 1:])
        return np.swapaxes(a, axis, axis + 1).reshape(sh)

    wc, wn, wo = f["w_in_conv"][0], f["w_in_nsa"][0], f["w_out"]
    blocks = [f["w_mem_kv"][0], f["w_mem_kv"][1], wc[:, 0:512]]
    for i in range(CT):
        blocks.append(np.concatenate([wc[:, 512 + MIX * q + 128 * i:640 + MIX * q + 128 * i] for q in (1, 2, 0, 3)], 1))
    blocks += [wo[0][:, 0:512], wo[0][:, 512:1024]]
    q, kv, gl, z = wn[:, 512:1280], wn[:, 1280:2816], wn[:, 2816:2852], wn[:, 2852:3620]
    n = np.concatenate([wn[:, 0:512], rgd(q, 1), kv, rgd(z, 1)], 1)
    blocks += [n[:, 512 * c:512 * c + 512] for c in CHUNK_ORDER]
    w1 = np.concatenate([wo[1][0:256], rgd(wo[1][256:], 0)], 0)
    blocks += [w1[:, 0:512], w1[:, 512:1024]]
    out["wall"] = np.stack([b.reshape(KD, 128, 512).transpose(1, 0, 2).reshape(128, KD * 512) for b in blocks])
    g = gl.reshape(D, 3, KVH, GRP).swapaxes(2, 3).reshape(KD, 128, 36)
    out["wg"] = g.transpose(1, 0, 2).reshape(128, KD * 36)
    parts = {
        "g_mem": f["mem_norm_g"].reshape(2, KD, 128).transpose(2, 0, 1).reshape(128, 16),
        "g_x": f["norm_g"].reshape(2, KD, 128).transpose(2, 0, 1).reshape(128, 16),
        "conv_w": f["conv_w"][0].reshape(3, CT, 128).transpose(2, 1, 0).reshape(128, 18),
        "state": f["state_conv"][0].reshape(NB, 2, CT, 128).transpose(3, 2, 0, 1).reshape(128, CT * 16),
    }
    pos = f["cmp_pos_w"][0].reshape(2, 2, 16, HD)
    for m in range(2):
        w = pos[:, m].transpose(1, 0, 2).reshape(16, 2 * HD)
        parts[f"pos{m}"] = np.tile(w, (8, 1))
        parts[f"tile_pos{m}"] = np.tile(w.reshape(4, 4 * 2 * HD), (32, 1))
    for s, name in enumerate(("phi_k", "phi_v")):
        d = np.zeros((128, 128), np.float32)
        for k in range(2):
            d[64 * k:64 * k + 64, 64 * k:64 * k + 64] = f["cmp_phi"][0, s]
        parts[name] = d
    out["small"] = np.concatenate([parts[k] for k in SMALL], 1)
    out["gfin"] = np.broadcast_to(f["final_norm_g"][None, :], (128, D))
    return {k: np.ascontiguousarray(v) for k, v in out.items()}


OUTS = {"yp": (SEQ, D), "ys": (NS, D), "conv": (128, CT * 18), "cmp_p": (SEQ, 512), "sel_p": (SEQ, 512),
        "win_p": (SEQ, 512), "mem": (2, NMEM, 512), "cmp_s": (NS, 512), "sel_s": (NS, 512), "win_s": (NB, WIN, 512)}


def kernel(**inputs):
    import concourse.bacc as bacc
    from concourse.bass_utils import run_bass_kernel_spmd

    arrays = {"in_" + k: v for k, v in lay_out(inputs).items()}
    nc = bacc.Bacc("TRN2", target_bir_lowering=False, num_devices=1)
    I = {k[3:]: nc.dram_tensor(k, v.shape, I32 if v.dtype == np.int32 else F32, kind="ExternalInput").ap()
         for k, v in arrays.items()}
    O = {k: nc.dram_tensor("out_" + k, s, F32, kind="ExternalOutput").ap() for k, s in OUTS.items()}
    build(nc, I, O)
    r = run_bass_kernel_spmd(nc, [arrays], core_ids=[0]).results[0]
    r = {k: r["out_" + k] for k in OUTS}
    conv = r["conv"].reshape(128, CT, 18)
    kv = lambda a, *s: a.reshape(*s, 2, KVH, HD)
    conv_p = conv[:, :, 0:2].transpose(2, 1, 0).reshape(1, 1, 2, MIX)
    conv_s = conv[:, :, 2:18].reshape(128, CT, NB, 2).transpose(2, 3, 1, 0).reshape(1, NB, 2, MIX)
    return (r["yp"].reshape(1, SEQ, D), r["ys"].reshape(NB, NT, D), conv_p,
            kv(r["cmp_p"], 1, 1, SEQ), kv(r["sel_p"], 1, 1, SEQ), kv(r["win_p"], 1, 1, SEQ),
            r["mem"].reshape(2, 1, NMEM, 2, 4, HD), conv_s,
            kv(r["cmp_s"], 1, NB, NT), kv(r["sel_s"], 1, NB, NT), kv(r["win_s"], 1, NB, WIN))
```
